# Optimizing a Trainium2 kernel written in Bass

```python
import math
import jax, jax.numpy as jnp
from jax import lax
import numpy as np

D_MODEL = 1024
BATCH = 1
SEQ = 512
DEPTH = 2

N_MIXERS = 2
N_A = (DEPTH + 1) // 2
N_B = DEPTH // 2

A_HEADS = 16
A_KV_HEADS = 4
A_GROUP = A_HEADS // A_KV_HEADS
A_HEAD_DIM = 64
A_QKV = A_HEADS * A_HEAD_DIM + 2 * A_KV_HEADS * A_HEAD_DIM
WINDOW = 128
BLK = 128

B_HEADS = 16
Q_LORA = 384
KV_LORA = 256
NOPE_DIM = 64
ROPE_DIM = 32
V_DIM = 64
B_IN = Q_LORA + KV_LORA + ROPE_DIM
ROPE_THETA = 10000.0

D_FF = int(math.ceil(8 * D_MODEL / 3 / 256) * 256)

EPS = 1e-6
NEG = -1e30

kernel_name = "hybrid_swa_sink_alibi_mla_swiglu_encoder"

def _rmsnorm(x, g):
    x32 = x.astype(jnp.float32)
    y = x32 * lax.rsqrt(jnp.mean(x32 * x32, axis=-1, keepdims=True) + EPS)
    return (y * g.astype(jnp.float32)).astype(x.dtype)

def _alibi_slopes(n):
    return jnp.asarray(2.0 ** (-8.0 * np.arange(1, n + 1) / n), dtype=jnp.float32)

def _band(t, nb):
    pad = [(0, 0), (BLK, BLK)] + [(0, 0)] * (t.ndim - 2)
    tp = jnp.pad(t, pad).reshape((t.shape[0], nb + 2, BLK) + t.shape[2:])
    return jnp.concatenate([tp[:, :-2], tp[:, 1:-1], tp[:, 2:]], axis=2)

def _windowed_gqa(h, pos, w_qkv, sink, w_o):
    B, S, _ = h.shape
    nb = S // BLK
    qkv = h @ w_qkv
    q, k, v = jnp.split(qkv, [A_HEADS * A_HEAD_DIM, A_HEADS * A_HEAD_DIM + A_KV_HEADS * A_HEAD_DIM], axis=-1)
    q = q.reshape(B, nb, BLK, A_KV_HEADS, A_GROUP, A_HEAD_DIM) * (A_HEAD_DIM ** -0.5)
    kb = _band(k.reshape(B, S, A_KV_HEADS, A_HEAD_DIM), nb)
    vb = _band(v.reshape(B, S, A_KV_HEADS, A_HEAD_DIM), nb)
    qi = jnp.arange(nb)[:, None] * BLK + jnp.arange(BLK)[None, :]
    ki = (jnp.arange(nb)[:, None] - 1) * BLK + jnp.arange(3 * BLK)[None, :]
    mask = (jnp.abs(qi[:, :, None] - ki[:, None, :]) <= WINDOW) & (ki >= 0)[:, None, :] & (ki < S)[:, None, :]
    qpos = pos.reshape(B, nb, BLK)
    kpos = _band(pos, nb)
    dist = jnp.abs(qpos[:, :, :, None] - kpos[:, :, None, :]).astype(jnp.float32)
    slopes = _alibi_slopes(A_HEADS).reshape(A_KV_HEADS, A_GROUP)
    scores = jnp.einsum('bnqkgd,bnskd->bnkgqs', q, kb).astype(jnp.float32)
    scores = scores - slopes[None, None, :, :, None, None] * dist[:, :, None, None]
    scores = jnp.where(mask[None, :, None, None], scores, NEG)
    sink_col = jnp.broadcast_to(sink.astype(jnp.float32).reshape(1, 1, A_KV_HEADS, A_GROUP, 1, 1),
                                scores.shape[:-1] + (1,))
    p = jax.nn.softmax(jnp.concatenate([scores, sink_col], axis=-1), axis=-1)[..., :-1]
    out = jnp.einsum('bnkgqs,bnskd->bnqkgd', p.astype(vb.dtype), vb)
    return out.reshape(B, S, A_HEADS * A_HEAD_DIM) @ w_o

def _rope(t, pos):
    half = ROPE_DIM // 2
    inv_freq = ROPE_THETA ** (-jnp.arange(half, dtype=jnp.float32) * 2.0 / ROPE_DIM)
    ang = pos.astype(jnp.float32)[:, :, None] * inv_freq[None, None, :]
    cos = jnp.cos(ang)[:, :, None, :]
    sin = jnp.sin(ang)[:, :, None, :]
    t32 = t.astype(jnp.float32)
    t1, t2 = t32[..., :half], t32[..., half:]
    return jnp.concatenate([t1 * cos - t2 * sin, t1 * sin + t2 * cos], axis=-1).astype(t.dtype)

def _mla(h, pos, w_in, g_q, g_kv, w_uq, w_ukv, w_o):
    B, S, _ = h.shape
    nb = S // BLK
    lat = h @ w_in
    cq, ckv, k_rope = jnp.split(lat, [Q_LORA, Q_LORA + KV_LORA], axis=-1)
    cq = _rmsnorm(cq, g_q)
    ckv = _rmsnorm(ckv, g_kv)
    q = (cq @ w_uq).reshape(B, S, B_HEADS, NOPE_DIM + ROPE_DIM)
    kv = (ckv @ w_ukv).reshape(B, S, B_HEADS, NOPE_DIM + V_DIM)
    q_nope, q_rope = q[..., :NOPE_DIM], q[..., NOPE_DIM:]
    k_nope, v = kv[..., :NOPE_DIM], kv[..., NOPE_DIM:]
    q_rope = _rope(q_rope, pos)
    k_rope = _rope(k_rope[:, :, None, :], pos)
    k = jnp.concatenate([k_nope, jnp.broadcast_to(k_rope, (B, S, B_HEADS, ROPE_DIM))], axis=-1)
    q = jnp.concatenate([q_nope, q_rope], axis=-1) * ((NOPE_DIM + ROPE_DIM) ** -0.5)
    qb = q.reshape(B, nb, BLK, B_HEADS, NOPE_DIM + ROPE_DIM).transpose(1, 0, 2, 3, 4)

    def attend(qblk):
        s = jnp.einsum('bqhd,bkhd->bhqk', qblk, k).astype(jnp.float32)
        p = jax.nn.softmax(s, axis=-1)
        return jnp.einsum('bhqk,bkhd->bqhd', p.astype(v.dtype), v)

    o = lax.map(attend, qb)
    o = o.transpose(1, 0, 2, 3, 4).reshape(B, S, B_HEADS * V_DIM)
    return o @ w_o

def _swiglu(h, w_gu, w_down):
    g, u = jnp.split(h @ w_gu, 2, axis=-1)
    return (jax.nn.silu(g) * u) @ w_down

def setup_inputs(seed: int = 0) -> dict:
    key = jax.random.key(seed)
    ks = jax.random.split(key, 20)

    def w(k, shape, fan_in):
        return jax.random.normal(k, shape, jnp.float32) * (fan_in ** -0.5)

    def gain(k, shape):
        return 1.0 + 0.02 * jax.random.normal(k, shape, jnp.float32)

    x = jax.random.normal(ks[0], (BATCH, SEQ, D_MODEL), jnp.float32)
    offset = jax.random.randint(ks[1], (BATCH, 1), 0, 1024, dtype=jnp.int32)
    positions = offset + jnp.arange(SEQ, dtype=jnp.int32)[None, :]
    return {
        "x": x,
        "positions": positions,
        "norm_mix": gain(ks[2], (DEPTH, D_MODEL)),
        "norm_ffn": gain(ks[3], (DEPTH, D_MODEL)),
        "a_w_qkv": w(ks[4], (N_A, D_MODEL, A_QKV), D_MODEL),
        "a_sink": 0.5 * jax.random.normal(ks[5], (N_A, A_HEADS), jnp.float32),
        "a_w_o": w(ks[6], (N_A, A_HEADS * A_HEAD_DIM, D_MODEL), A_HEADS * A_HEAD_DIM),
        "b_w_in": w(ks[7], (N_B, D_MODEL, B_IN), D_MODEL),
        "b_g_q": gain(ks[8], (N_B, Q_LORA)),
        "b_g_kv": gain(ks[9], (N_B, KV_LORA)),
        "b_w_uq": w(ks[10], (N_B, Q_LORA, B_HEADS * (NOPE_DIM + ROPE_DIM)), Q_LORA),
        "b_w_ukv": w(ks[11], (N_B, KV_LORA, B_HEADS * (NOPE_DIM + V_DIM)), KV_LORA),
        "b_w_o": w(ks[12], (N_B, B_HEADS * V_DIM, D_MODEL), B_HEADS * V_DIM),
        "ffn_w_gu": w(ks[13], (DEPTH, D_MODEL, 2 * D_FF), D_MODEL),
        "ffn_w_down": w(ks[14], (DEPTH, D_FF, D_MODEL), D_FF),
        "final_norm": gain(ks[15], (D_MODEL,)),
    }

def reference(x, positions, norm_mix, norm_ffn, a_w_qkv, a_sink, a_w_o, b_w_in, b_g_q, b_g_kv,
              b_w_uq, b_w_ukv, b_w_o, ffn_w_gu, ffn_w_down, final_norm):
    h = x
    for i in range(DEPTH):
        j = i // N_MIXERS
        hn = _rmsnorm(h, norm_mix[i])
        if i % N_MIXERS == 0:
            mix = _windowed_gqa(hn, positions, a_w_qkv[j], a_sink[j], a_w_o[j])
        else:
            mix = _mla(hn, positions, b_w_in[j], b_g_q[j], b_g_kv[j], b_w_uq[j], b_w_ukv[j], b_w_o[j])
        h = h + mix.astype(h.dtype)
        h = h + _swiglu(_rmsnorm(h, norm_ffn[i]), ffn_w_gu[i], ffn_w_down[i]).astype(h.dtype)
    return _rmsnorm(h, final_norm)


_drawn_inputs = setup_inputs


def setup_inputs(seed=0):
    import zlib

    import numpy as np

    out = dict(_drawn_inputs(seed))
    spreads = {}
    factors = {'norm_mix': 5.948,
     'norm_ffn': 2.866,
     'a_sink': 5.193,
     'b_g_q': 8.0,
     'b_g_kv': 8.0,
     'final_norm': 2.86}
    for name, (base, spread) in spreads.items():
        noise = np.random.default_rng([zlib.crc32(name.encode()), seed]).standard_normal(out[name].shape)
        drawn = base * np.exp(spread * noise) if base else spread * noise
        out[name] = __import__('jax').numpy.asarray(drawn.astype(out[name].dtype))
    for name, factor in factors.items():
        out[name] = (out[name] * factor).astype(out[name].dtype)
    return out
```

```python
from contextlib import ExitStack

import numpy as np
import concourse.bass as bass
from concourse import mybir

F32 = mybir.dt.float32
F32R = mybir.dt.float32r
I32 = mybir.dt.int32
ALU = mybir.AluOpType
ACT = mybir.ActivationFunctionType
AX_X = mybir.AxisListType.X

P = 128
D = 1024
KD = D // P
T = 512
NT = T // P
HEADS = 16
GROUPS = 4
HG = HEADS // GROUPS
HD = 64
WINDOW = 128
QL, KVL, ROPE, NOPE = 384, 256, 32, 64
B_IN = QL + KVL + ROPE
QK = NOPE + ROPE
DFF = 2816
FB = DFF // P
HALF = FB // 2
EPS = 1e-6
MASKED = -1e36
SLOT = HALF * P
SA = 1 + 3 * P

C_K, C_V, C_Q, C_WOA = 0, 2, 4, 12
C_FFN0 = C_WOA + KD
C_HALF = 2 * HALF + KD
C_LAT = C_FFN0 + 2 * C_HALF
C_B = C_LAT + 4
C_WOB = C_B + 2 * GROUPS
C_FFN1 = C_WOB + KD
C_END = C_FFN1 + 2 * C_HALF
W_COLS = KD * P
W_DOWN = HALF * P
W_LAT = 2 * B_IN
W_UQ = QL // P * HG * QK
W_UKV = KVL // P * HG * 2 * HD

U_K, U_Q, U_WOA = 0, 2, 10
U_FFN0 = U_WOA + KD
U_B = U_FFN0 + 2 * C_HALF
U_BG = 8
U_WOB = U_B + U_BG * GROUPS
U_FFN1 = U_WOB + KD

T_A = KD
A_KB = [(0, 2), (0, 3), (1, 3), (2, 2)]
A_T0 = [0, 2, 5, 8]
A_TG = 10
T_BPRE = T_A + A_TG * GROUPS
T_B = T_BPRE + 6 + HG
B_TG = 4 * HG + HG
T_FIN = T_B + B_TG * GROUPS - HG

O_NORM0, O_A = 0, 1
O_NORM1 = O_A + 4 * GROUPS
O_B = O_NORM1 + 1
O_NORM3 = O_B + 2 * GROUPS
O_NORM4 = O_NORM3 + 1
S_A = 16
S_B = S_A + 16 * GROUPS

INV_FREQ = np.float32(10000.0) ** (-np.arange(16, dtype=np.float32) * np.float32(2.0) / np.float32(32))
ROUND = 12582912.0


TAB_STEPS = 21


def two_pi_parts():
    rest, parts = 2.0 * np.pi, []
    for _ in range(4):
        m, e = np.frexp(rest)
        part = float(np.ldexp(np.floor(m * 2048.0), int(e) - 11))
        parts.append(part)
        rest -= part
    return parts


def build(nc, x, positions, norm_mix, norm_ffn, a_w_qkv, a_sink, a_w_o, b_w_in, b_g_q, b_g_kv,
          b_w_uq, b_w_ukv, b_w_o, ffn_w_gu, ffn_w_down, final_norm, out):
    ctx = ExitStack()
    with ctx:
        place = {"at": (nc.sbuf_base + 63) // 64 * 64}
        top = nc.sbuf_usable_end

        def tile_at(name, shape, dtype, offset):
            size = 4 * int(np.prod(shape[1:]))
            assert offset + size <= top, (name, offset + size, top)
            return nc.alloc_sbuf_tensor_at(name, shape, dtype, offset=offset), offset + (size + 31) // 32 * 32

        def tile(name, shape, dtype=F32):
            t, place["at"] = tile_at(name, shape, dtype, place["at"])
            return t

        def region(start, specs):
            tiles, at = [], start
            for name, shape, dtype in specs:
                t, at = tile_at(name, shape, dtype, at)
                tiles.append(t)
            return tiles

        h = tile("h", [P, KD, T])
        x_hi = tile("x_hi", [P, KD, T], F32R)
        x_lo = tile("x_lo", [P, KD, T], F32R)
        ot_start = place["at"]
        ot_hi = tile("ot_hi", [P, KD, T], F32R)
        ot_lo = tile("ot_lo", [P, KD, T], F32R)
        scratch_size = 88 * 1024
        scratch = place["at"]
        place["at"] += scratch_size
        w_raw = [tile(f"w_raw{s}", [P, SLOT]) for s in range(2)]
        w_hi = [tile(f"w_hi{s}", [P, SLOT], F32R) for s in range(2)]
        w_lo = [tile(f"w_lo{s}", [P, SLOT], F32R) for s in range(2)]
        ident = tile("ident", [P, P])
        ones = tile("ones", [P, P], F32R)
        rs_t = tile("rs_t", [P, T])
        rs_n = tile("rs_n", [P, 8])
        gains = tile("gains", [P, 4, KD, 1])
        g_q = tile("g_q", [P, QL // P])
        g_kv = tile("g_kv", [P, KVL // P])
        eps = tile("eps", [P, 1])
        par_all = tile("par_all", [P, GROUPS, 2 * HG])
        par = tile("par", [P, 2 * HG])
        sink_in = tile("sink_in", [P, HEADS])
        stat = tile("stat", [P, 3, 8])
        lat_stat = tile("lat_stat", [P, 3, 8])
        cos_n = tile("cos_n", [P, NT, ROPE])
        sin_n = tile("sin_n", [P, NT, ROPE])
        x_start = ot_start - 2 * 4 * KD * T

        x_n, sq0, ss0, ss0_hi, ss0_lo = region(ot_start, [
            ("x_n", [P, NT, D], F32), ("sq0", [P, 2, T], F32), ("ss0", [P, T], F32),
            ("ss0_hi", [P, T], F32R), ("ss0_lo", [P, T], F32R)])
        (q_tmp, aq_hi, aq_lo, k_dup, kp_hi, kp_lo, v_all, av_hi, av_lo, near, bias, s_a, apt_hi, apt_lo) = \
            region(scratch, [
                ("q_tmp", [P, T], F32), ("aq_hi", [P, 2, T], F32R), ("aq_lo", [P, 2, T], F32R),
                ("k_dup", [P, GROUPS, T], F32), ("kp_hi", [P, 2, T], F32R), ("kp_lo", [P, 2, T], F32R),
                ("v_all", [P, NT, GROUPS * HD], F32),
                ("av_hi", [P, NT, 3 * HD], F32R), ("av_lo", [P, NT, 3 * HD], F32R),
                ("near", [P, NT, 3 * P], F32), ("bias", [P, 2, 3 * P], F32),
                ("s_a", [P, 2, HG, SA], F32),
                ("apt_hi", [P, 2, 3, T], F32R), ("apt_lo", [P, 2, 3, T], F32R)])
        pos_k, pos_q, dist_i, pos_f, inv_f, ang, turns, turns_hi, half_sin = region(scratch + 58 * 1024, [
            ("pos_k", [P, T], I32), ("pos_q", [P, NT], I32), ("dist_i", [P, NT, 3 * P], I32),
            ("pos_f", [P, NT], F32), ("inv_f", [P, 16], F32), ("ang", [P, NT, 16], F32),
            ("turns", [P, NT, 16], F32), ("turns_hi", [P, NT, 16], F32), ("half_sin", [P, NT, 16], F32)])
        f_hi, f_lo, gate_t, gate_s, hid = region(ot_start, [
            ("f_hi", [P, HALF, T], F32R), ("f_lo", [P, HALF, T], F32R),
            ("gate_t", [P, T], F32), ("gate_s", [P, T], F32), ("hid", [P, T], F32)])
        sq1, ss1, ss1_hi, ss1_lo, h_fin, g_fin = region(scratch + 24 * 1024, [
            ("sq1", [P, 2, T], F32), ("ss1", [P, T], F32), ("ss1_hi", [P, T], F32R), ("ss1_lo", [P, T], F32R),
            ("h_fin", [P, 2, T], F32), ("g_fin", [P, KD, P], F32)])
        (out_n,) = region(x_start, [("out_n", [P, NT, D], F32)])
        bq_hi, bq_lo, bk_hi, bk_lo = region(x_start, [
            ("bq_hi", [P, HG, T], F32R), ("bq_lo", [P, HG, T], F32R),
            ("bk_hi", [P, HG, T], F32R), ("bk_lo", [P, HG, T], F32R)])
        cq_hi, cq_lo, ckv_hi, ckv_lo, q_n, bv_hi, bv_lo, s_b, bpt_hi, bpt_lo, rope_a = region(scratch, [
            ("cq_hi", [P, QL // P, T], F32R), ("cq_lo", [P, QL // P, T], F32R),
            ("ckv_hi", [P, KVL // P, T], F32R), ("ckv_lo", [P, KVL // P, T], F32R),
            ("q_n", [P, NT, HG * QK], F32),
            ("bv_hi", [P, NT, 2, 3 * HD], F32R), ("bv_lo", [P, NT, 2, 3 * HD], F32R),
            ("s_b", [P, 2, HG, T], F32),
            ("bpt_hi", [P, 2, NT, T], F32R), ("bpt_lo", [P, 2, NT, T], F32R),
            ("rope_a", [P, T], F32)])
        rope_b = rs_t
        lat, lat_sq = region(scratch + 54 * 1024, [("lat", [P, NT, B_IN], F32), ("lat_sq", [P, QL], F32)])

        banks = [ctx.enter_context(nc.psum_tensor(f"bank{i}", [P, T], F32)) for i in range(8)]

        def sem(name):
            return ctx.enter_context(nc.semaphore(name))

        x_in = [sem(f"x_in{i}") for i in range(NT)]
        small_in = sem("small_in")
        gfin_in = sem("gfin_in")
        w_in = [sem(f"w_in{i}") for i in range(2)]
        w_hi_ready = sem("w_hi_ready")
        w_ready = sem("w_ready")
        w_used = sem("w_used")
        pool_consts = sem("pool_consts")
        vec_consts = sem("vec_consts")
        near_p = sem("near_p")
        near_v = sem("near_v")
        tab_v = sem("tab_v")
        tab_a = sem("tab_a")
        proj_done = sem("proj_done")
        proj_free = sem("proj_free")
        pt_done = sem("pt_done")
        pt_hi_ready = sem("pt_hi_ready")
        pt_free = sem("pt_free")
        s_done = sem("s_done")
        s_free = sem("s_free")
        o_done = sem("o_done")
        o_hi_ready = sem("o_hi_ready")
        o_free = sem("o_free")
        x_hi_ready = sem("x_hi_ready")
        x_ready = sem("x_ready")
        sq_ready = sem("sq_ready")
        ss_ready = sem("ss_ready")
        sshi_ready = sem("sshi_ready")
        sslo_ready = sem("sslo_ready")
        st_done = sem("st_done")
        rs_t_ready = sem("rs_t_ready")
        rms_n = sem("rms_n")
        rs_n_ready = sem("rs_n_ready")
        k_dup_ready = sem("k_dup_ready")
        q_hi_ready = sem("q_hi_ready")
        q_ready = sem("q_ready")
        kp_hi_ready = sem("kp_hi_ready")
        kp_ready = sem("kp_ready")
        v_hi_ready = sem("v_hi_ready")
        v_ready = sem("v_ready")
        par_ready = sem("par_ready")
        sinkcol_ready = sem("sinkcol_ready")
        bias_ready = sem("bias_ready")
        max_ready = sem("max_ready")
        exp_ready = sem("exp_ready")
        rsum_ready = sem("rsum_ready")
        p_ready = sem("p_ready")
        lat_ready = sem("lat_ready")
        lsq_ready = sem("lsq_ready")
        lrms_ready = sem("lrms_ready")
        lrs_ready = sem("lrs_ready")
        latn_ready = sem("latn_ready")
        rope_v = sem("rope_v")
        krope_hi = sem("krope_hi")
        krope_ready = sem("krope_ready")
        silu_ready = sem("silu_ready")
        silu_rs_ready = sem("silu_rs_ready")
        f_hi_ready = sem("f_hi_ready")
        f_ready = sem("f_ready")
        out_ready = [sem("out_ready_v"), sem("out_ready_a")]
        out_sent = sem("out_sent")

        def wait(eng, s, value):
            eng.wait_ge(s, value)
            if not isinstance(value, int):
                eng.nop(nofuse=True)

        def f(ap):
            return ap.bitcast(F32)

        def raw_part(s, cols, kv):
            w = w_raw[s][:, 0:cols]
            return w if not kv else w.rearrange("p (b c d) -> p b c d", c=2, d=HD)

        def split_part(w, s, cols, kv):
            w = w[s][:, 0:cols]
            return w if not kv else w.rearrange("p (c b d) -> p b c d", c=2, d=HD)

        class Norm:

            def __init__(self, number, gain, block_sem, block_base, tiles, sum_t, sum_n, o_index):
                self.number, self.gain, self.base = number, gain, KD * number
                self.block_sem, self.block_base = block_sem, block_base
                self.sq, self.ss, self.ss_hi, self.ss_lo = tiles
                self.sum_t, self.sum_n, self.o_index = sum_t, sum_n, o_index

        later = (sq1, ss1, ss1_hi, ss1_lo)
        U_DOWN0 = U_FFN0 + C_HALF + 2 * HALF
        U_DOWN1 = U_FFN1 + C_HALF + 2 * HALF
        norms = [
            Norm(0, 0, pt_free, 0, (sq0, ss0, ss0_hi, ss0_lo), banks[5], banks[4][:, 0:8], O_NORM0),
            Norm(1, 2, proj_free, U_WOA, later, banks[5], None, O_NORM1),
            Norm(2, 1, proj_free, U_DOWN0, later, None, banks[7][:, B_IN - QL:B_IN - QL + 8], None),
            Norm(3, 3, proj_free, U_WOB, later, banks[5], None, O_NORM3),
            Norm(4, None, proj_free, U_DOWN1, later, None, banks[5][:, 0:8], O_NORM4)]

        qkv_v = a_w_qkv[0].rearrange("(k p) (j n) -> p k j n", p=P, n=P)
        v_v = a_w_qkv[0].rearrange("(k p) n -> p k n", p=P)
        wo_v = [w[0].rearrange("(k p) (m n) -> p k m n", p=P, n=P) for w in (a_w_o, b_w_o)]
        gu_v = [ffn_w_gu[i].rearrange("(k p) (j n) -> p k j n", p=P, n=P) for i in range(2)]
        down_v = [ffn_w_down[i].rearrange("(k p) (m n) -> p k m n", p=P, n=P) for i in range(2)]
        in_v = b_w_in[0].rearrange("(k p) n -> p k n", p=P)
        uq_v = b_w_uq[0].rearrange("(k p) (g n) -> p k g n", p=P, n=HG * QK)
        ukv_v = b_w_ukv[0].rearrange("(k p) (g n) -> p k g n", p=P, n=HG * 2 * HD)

        block = ctx.enter_context(nc.Block())

        @block.sync
        def _(sp):
            def load(c2, s, src, cols):
                if not (isinstance(c2, int) and c2 == 0):
                    wait(sp, w_ready, 2 * c2 + s - 1)
                dst = w_raw[s][:, 0:src.shape[1] * cols].rearrange("p (k n) -> p k n", n=cols)
                sp.dma_start(dst, src).then_inc(w_in[s], 16)

            xv = x[0].rearrange("(t p) d -> p t d", p=P)
            for t in range(NT):
                sp.dma_start(x_n[:, t, :], xv[:, t, :]).then_inc(x_in[t], 16)
            with nc.allow_non_contiguous_dma(reason="gains by partition"):
                for i, g in enumerate((norm_mix[0], norm_mix[1], norm_ffn[0], norm_ffn[1])):
                    sp.dma_start(gains[:, i, :, 0], g.rearrange("(k p) -> p k", p=P)).then_inc(small_in, 16)
                load(0, 0, qkv_v[:, :, 8, :], P)
                load(0, 1, qkv_v[:, :, 9, :], P)
                sp.dma_start(g_q[:], b_g_q[0].rearrange("(k p) -> p k", p=P)).then_inc(small_in, 16)
                sp.dma_start(g_kv[:], b_g_kv[0].rearrange("(k p) -> p k", p=P)).then_inc(small_in, 16)
                sp.dma_start(pos_q[:], positions[0].rearrange("(t p) -> p t", p=P)).then_inc(small_in, 16)
            sp.dma_start(sink_in[:], a_sink[0].partition_broadcast(P)).then_inc(small_in, 16)
            sp.dma_start(pos_k[:], positions[0].partition_broadcast(P)).then_inc(small_in, 16)

            for s in range(2):
                load(C_V // 2, s, v_v[:, 4 * s:4 * s + 4, (HEADS + GROUPS) * HD:], GROUPS * HD)
            with sp.Fori(0, GROUPS) as g:
                for s in range(2):
                    load(C_Q // 2 + g, s, qkv_v[:, :, 2 * g + s, :], P)

            def load_wo(layer, c0):
                with sp.Fori(0, KD // 2) as i:
                    for s in range(2):
                        load(c0 // 2 + i, s, wo_v[layer][:, :, 2 * i + s, :], P)

            def load_ffn(layer, c0):
                for half in range(2):
                    c2 = c0 // 2 + half * C_HALF // 2
                    with sp.Fori(0, HALF) as j:
                        load(c2 + j, 0, gu_v[layer][:, :, half * HALF + j, :], P)
                        load(c2 + j, 1, gu_v[layer][:, :, FB + half * HALF + j, :], P)
                    with sp.Fori(0, KD // 2) as i:
                        for s in range(2):
                            load(c2 + HALF + i, s,
                                 down_v[layer][:, half * HALF:(half + 1) * HALF, 2 * i + s, :], P)

            load_wo(0, C_WOA)
            load_ffn(0, C_FFN0)
            for i in range(4):
                load(C_LAT // 2 + i // 2, i % 2, in_v[:, 2 * i:2 * i + 2, :], B_IN)
            with sp.Fori(0, GROUPS) as g:
                load(C_B // 2 + g, 0, uq_v[:, :, g, :], HG * QK)
                load(C_B // 2 + g, 1, ukv_v[:, :, g, :], HG * 2 * HD)
            load_wo(1, C_WOB)
            sp.wait_ge(w_used, C_WOB + 1)
            sp.dma_start(g_fin[:], final_norm.rearrange("(k n) -> k n", n=P).partition_broadcast(P)) \
                .then_inc(gfin_in, 16)
            load_ffn(1, C_FFN1)
            ov = out[0].rearrange("(t p) d -> p t d", p=P)
            for t in range(NT):
                sp.wait_ge(out_ready[t % 2], t // 2 + 1)
                sp.dma_start(ov[:, t, :], out_n[:, t, :]).then_inc(out_sent, 16)
            sp.wait_ge(out_sent, 16 * NT)

        @block.gpsimd
        def _(pool):
            def w_split_hi(c2, s, cols, kv=False):
                wait(pool, w_in[s], 16 * c2 + 16)
                if not (isinstance(c2, int) and c2 == 0):
                    wait(pool, w_used, 2 * c2 + s - 1)
                pool.tensor_scalar(split_part(w_hi, s, cols, kv), raw_part(s, cols, kv), 1.0, 1.0, ALU.mult, ALU.mult) \
                    .then_inc(w_hi_ready, 1)

            def sum_squares(n, m, b, first=False):
                wait(pool, sq_ready, n.base + m + 1)
                if first:
                    if n.number:
                        pool.wait_ge(sslo_ready, n.number)
                    pool.tensor_scalar(n.ss[:], n.sq[:, b, :], 1.0, 1.0, ALU.mult, ALU.mult).then_inc(ss_ready, 1)
                else:
                    wait(pool, ss_ready, n.base + m)
                    pool.tensor_tensor(n.ss[:], n.ss[:], n.sq[:, b, :], ALU.add).then_inc(ss_ready, 1)

            pool.memset(ident[:], 0.0).then_inc(pool_consts, 1)
            pool.wait_ge(pool_consts, 1)
            pool.affine_select(out=ident[:], in_=ident[:], compare_op=ALU.not_equal, fill=1.0, base=0,
                               pattern=[[-1, P]], channel_multiplier=1).then_inc(pool_consts, 1)
            for i in range(HEADS):
                slope = float(np.float32(2.0 ** (-8.0 * (i + 1) / HEADS)))
                pool.memset(par_all[:, i // HG, i % HG:i % HG + 1], slope).then_inc(pool_consts, 1)
            for i in range(ROPE // 2):
                pool.memset(inv_f[:, i:i + 1], float(INV_FREQ[i])).then_inc(pool_consts, 1)
            w_split_hi(0, 0, W_COLS)
            w_split_hi(0, 1, W_COLS)
            sum_squares(norms[0], 0, 0, first=True)
            sum_squares(norms[0], 1, 1)
            with pool.Fori(1, KD // 2) as i:
                for s in range(2):
                    sum_squares(norms[0], 2 * i + s, s)
            pool.wait_ge(small_in, 9 * 16)
            for qb in range(NT):
                k0, nk = A_KB[qb]
                pool.tensor_tensor(dist_i[:, qb, 0:nk * P], pos_k[:, k0 * P:(k0 + nk) * P],
                                   pos_q[:, qb:qb + 1].to_broadcast([P, nk * P]), ALU.subtract).then_inc(near_p, 1)
            w_split_hi(C_V // 2, 0, 4 * GROUPS * HD)
            for qb in range(NT):
                k0, nk = A_KB[qb]
                gap = (k0 - qb) * P
                view = near[:, qb, 0:nk * P]
                pool.wait_ge(near_v, 2 * qb + 2)
                pool.affine_select(out=view, in_=view, compare_op=ALU.is_ge, fill=MASKED, base=WINDOW - gap,
                                   pattern=[[-1, nk * P]], channel_multiplier=1).then_inc(near_p, 1)
                pool.wait_ge(near_p, NT + 2 * qb + 1)
                pool.affine_select(out=view, in_=view, compare_op=ALU.is_ge, fill=MASKED, base=WINDOW + gap,
                                   pattern=[[1, nk * P]], channel_multiplier=-1).then_inc(near_p, 1)
            w_split_hi(C_V // 2, 1, 4 * GROUPS * HD)
            for s in range(2):
                w_split_hi(C_Q // 2, s, W_COLS)

            pool.wait_ge(near_p, 3 * NT)
            pool.wait_ge(pool_consts, 2 + HEADS)
            pool.wait_ge(vec_consts, 7)

            def a_group(g):
                wait(pool, s_free, S_A + 16 * g)
                pool.tensor_copy(par[:], par_all[:, g, :]).then_inc(par_ready, 1)
                wait(pool, par_ready, g + 1)
                wait(pool, pt_done, T_A + A_TG * g)
                for b in range(2):
                    pool.tensor_copy(s_a[:, b, :, 0:1], par[:, HG:2 * HG].unsqueeze(2)).then_inc(sinkcol_ready, 1)

                def make_bias(u):
                    nk = A_KB[u // HG][1]
                    if u >= 2:
                        wait(pool, s_free, S_A + 16 * g + u - 1)
                    pool.tensor_scalar(bias[:, u % 2, 0:nk * P], near[:, u // HG, 0:nk * P],
                                       par[:, u % HG:u % HG + 1], 1.0, ALU.mult, ALU.mult).then_inc(bias_ready, 1)

                make_bias(0)
                make_bias(1)
                for u in range(16):
                    n, hd = u // HG, u % HG
                    nk = A_KB[n][1]
                    if u + 2 < 16:
                        make_bias(u + 2)
                    wait(pool, rsum_ready, 16 * g + u + 1)
                    view = s_a[:, n % 2, hd, 1:1 + nk * P]
                    pool.tensor_scalar(view, view, stat[:, 2, u % 8:u % 8 + 1], 1.0, ALU.mult, ALU.mult) \
                        .then_inc(p_ready, 1)
                    if u == 3:
                        w_split_hi(C_Q // 2 + 1 + g, 0, W_COLS)
                    if u == 7:
                        w_split_hi(C_Q // 2 + 1 + g, 1, W_COLS)

            with pool.Fori(0, GROUPS) as g:
                a_group(g)

            def wo_phase(n, c0):
                for s in range(2):
                    w_split_hi(c0 // 2 + 1, s, W_COLS)
                    sum_squares(n, s, s, first=s == 0)
                with pool.Fori(1, KD // 2) as i:
                    for s in range(2):
                        w_split_hi(c0 // 2 + 1 + i, s, W_COLS)
                        sum_squares(n, 2 * i + s, s)

            def ffn_half(layer, half, n, next_cols):
                c2 = ((C_FFN0, C_FFN1)[layer] + half * C_HALF) // 2
                j0 = (2 * layer + half) * HALF

                def hidden(j, cols):
                    w_split_hi(c2 + j + 1, 0, cols)
                    wait(pool, silu_ready, j0 + j + 1)
                    pool.tensor_tensor(gate_s[:], gate_s[:], rs_t[:], ALU.mult).then_inc(silu_rs_ready, 1)
                    w_split_hi(c2 + j + 1, 1, cols)

                with pool.Fori(0, HALF - 1) as j:
                    hidden(j, W_COLS)
                hidden(HALF - 1, W_DOWN)

                def pair(i, cols, first=False):
                    for s in range(2):
                        if cols:
                            w_split_hi(c2 + HALF + 1 + i, s, cols)
                        if n is not None:
                            sum_squares(n, 2 * i + s, s, first=first and s == 0)

                pair(0, W_DOWN, first=True)
                with pool.Fori(1, KD // 2 - 1) as i:
                    pair(i, W_DOWN)
                pair(KD // 2 - 1, next_cols)

            wo_phase(norms[1], C_WOA)
            ffn_half(0, 0, None, W_COLS)
            ffn_half(0, 1, norms[2], W_LAT)

            w_split_hi(C_LAT // 2 + 1, 0, W_LAT)
            w_split_hi(C_LAT // 2 + 1, 1, W_LAT)
            w_split_hi(C_B // 2, 0, W_UQ)
            w_split_hi(C_B // 2, 1, W_UKV, kv=True)
            pool.wait_ge(lrs_ready, 1)
            for t in range(NT):
                view = lat[:, t, QL:QL + KVL]
                pool.tensor_scalar(view, view, lat_stat[:, 2, NT + t:NT + t + 1], 1.0, ALU.mult, ALU.mult) \
                    .then_inc(latn_ready, 1)

            def b_group(g, cols0, cols1):
                for u in range(16):
                    wait(pool, rsum_ready, 16 * (GROUPS + g) + u + 1)
                    view = s_b[:, u // 4 % 2, u % 4, :]
                    pool.tensor_scalar(view, view, stat[:, 2, u % 8:u % 8 + 1], 1.0, ALU.mult, ALU.mult) \
                        .then_inc(p_ready, 1)
                    if u == 3:
                        w_split_hi(C_B // 2 + 1 + g, 0, cols0)
                    if u == 7:
                        w_split_hi(C_B // 2 + 1 + g, 1, cols1, kv=cols0 == W_UQ)

            with pool.Fori(0, GROUPS - 1) as g:
                b_group(g, W_UQ, W_UKV)
            b_group(GROUPS - 1, W_COLS, W_COLS)

            wo_phase(norms[3], C_WOB)
            ffn_half(1, 0, None, W_COLS)
            ffn_half(1, 1, norms[4], 0)

        @block.scalar
        def _(act):
            def split_x(n, m, b, src=None):
                src = h[:, m, :] if src is None else src
                wait(act, n.block_sem, n.block_base + m + 1)
                if n.gain is not None:
                    act.activation(x_hi[:, m, :], src, ACT.Copy, scale=gains[:, n.gain, m, :]) \
                        .then_inc(x_hi_ready, 1)
                if n.number or not isinstance(m, int):
                    wait(act, ss_ready, n.base + m - 1)
                act.activation(n.sq[:, b, :], src, ACT.Square).then_inc(sq_ready, 1)

            def rms(n):
                act.wait_ge(ss_ready, n.base + KD)
                act.activation(n.ss_hi[:], n.ss[:], ACT.Copy).then_inc(sshi_ready, 1)
                act.wait_ge(st_done, n.number + 1)
                if n.sum_n is not None:
                    act.activation(rs_n[:], n.sum_n, ACT.Sqrt, scale=1.0 / D, bias=eps[:, 0:1]).then_inc(rms_n, 1)
                if n.sum_t is not None:
                    act.activation(rs_t[:], n.sum_t[:], ACT.Sqrt, scale=1.0 / D, bias=eps[:, 0:1]) \
                        .then_inc(o_free, 1)

            act.wait_ge(small_in, 9 * 16)
            for s in range(2):
                split_x(norms[0], s, s)
            with act.Fori(1, KD // 2) as i:
                for s in range(2):
                    split_x(norms[0], 2 * i + s, s)
            act.wait_ge(vec_consts, 1)
            rms(norms[0])
            act.wait_ge(w_used, C_V + 2)
            act.wait_ge(rs_n_ready, 1)
            for t in range(NT):
                act.activation(v_all[:, t, :], banks[t][:, 0:GROUPS * HD], ACT.Copy, scale=rs_n[:, 2 * t:2 * t + 1]) \
                    .then_inc(s_free, 16 // NT)

            def a_k_hi(g, first=False):
                if not first:
                    wait(act, s_done, 16 * g)
                for b in range(2):
                    act.activation(kp_hi[b * HD:(b + 1) * HD, b, :], k_dup[b * HD:(b + 1) * HD, g, :], ACT.Copy) \
                        .then_inc(kp_hi_ready, 1)

            v_by_group = v_all[:].rearrange("p t (g d) -> p t g d", g=GROUPS)

            def a_v_hi(g, first=False):
                if not first:
                    wait(act, o_done, 4 * g)
                act.activation(av_hi[:, :, HD:2 * HD], v_by_group[:, :, g, :], ACT.Copy).then_inc(v_hi_ready, 1)

            def a_q_hi(g, i, first=False):
                if not first:
                    wait(act, s_done, 16 * g)
                wait(act, proj_free, U_Q + 2 * g + i + 1)
                act.activation(aq_hi[:, i, :], q_tmp[:], ACT.Copy).then_inc(q_hi_ready, 1)

            act.wait_ge(k_dup_ready, 6)
            act.wait_ge(proj_free, U_Q)
            a_k_hi(0, first=True)
            a_q_hi(0, 0, first=True)
            a_q_hi(0, 1, first=True)
            act.wait_ge(s_free, S_A)
            a_v_hi(0, first=True)
            act.wait_ge(tab_v, TAB_STEPS)
            act.activation(half_sin[:], ang[:], ACT.Sin, scale=0.5).then_inc(tab_a, 1)
            act.activation(sin_n[:, :, 16:32], ang[:], ACT.Sin).then_inc(tab_a, 1)

            def a_group(g, last):
                def expo(u):
                    n, hd = u // HG, u % HG
                    if u == 0:
                        wait(act, sinkcol_ready, 2 * g + 2)
                    wait(act, s_free, S_A + 16 * g + u + 1)
                    view = s_a[:, n % 2, hd, 0:1 + A_KB[n][1] * P]
                    act.activation(view, view, ACT.Exp, scale=-1.0, bias=stat[:, 0, u % 8:u % 8 + 1],
                                   accum_out=stat[:, 1, u % 8:u % 8 + 1]).then_inc(exp_ready, 1)

                def pt_hi(n, i):
                    unit = T_A + A_T0[n] + i
                    wait(act, pt_done, unit + A_TG * g + 1)
                    act.activation(apt_hi[:, n % 2, i, :], banks[3 + unit % 2][:], ACT.Copy).then_inc(pt_hi_ready, 1)

                def o_hi(n):
                    wait(act, o_done, 4 * g + n + 1)
                    act.activation(ot_hi_q[:, g, :, n, :], banks[5][:, 0:2 * P].rearrange("p (a q) -> p a q", a=2),
                                   ACT.Copy).then_inc(o_hi_ready, 1)

                for u in range(4):
                    expo(u)
                for n in range(NT):
                    nk = A_KB[n][1]
                    if n < 3:
                        expo(4 * n + 4)
                        expo(4 * n + 5)
                        pt_hi(n, 0)
                        expo(4 * n + 6)
                        pt_hi(n, 1)
                        expo(4 * n + 7)
                        if nk > 2:
                            pt_hi(n, 2)
                    else:
                        pt_hi(n, 0)
                        pt_hi(n, 1)
                        if not last:
                            a_q_hi(g + 1, 0)
                            a_k_hi(g + 1)
                    if n:
                        o_hi(n - 1)
                if not last:
                    a_q_hi(g + 1, 1)
                o_hi(3)
                if not last:
                    a_v_hi(g + 1)

            ot_hi_q = ot_hi[:].rearrange("p (g a) (n q) -> p g a n q", a=2, n=NT)
            with act.Fori(0, GROUPS - 1) as g:
                a_group(g, False)
            a_group(GROUPS - 1, True)

            def wo_phase(n):
                with act.Fori(0, KD // 2) as i:
                    for s in range(2):
                        split_x(n, 2 * i + s, s)
                rms(n)

            def ffn_half(layer, half, n):
                u0 = (U_FFN0, U_FFN1)[layer] + half * C_HALF
                j0 = (2 * layer + half) * HALF
                with act.Fori(0, HALF) as j:
                    wait(act, proj_free, u0 + 2 * j + 1)
                    act.activation(gate_s[:], gate_t[:], ACT.Silu).then_inc(silu_ready, 1)
                    wait(act, proj_free, u0 + 2 * j + 2)
                    act.activation(f_hi[:, j, :], hid[:], ACT.Copy).then_inc(f_hi_ready, 1)
                if n is not None:
                    with act.Fori(0, KD // 2) as i:
                        for s in range(2):
                            split_x(n, 2 * i + s, s, h_fin[:, s, :] if n.gain is None else None)
                    rms(n)

            wo_phase(norms[1])
            ffn_half(0, 0, None)
            ffn_half(0, 1, norms[2])

            act.wait_ge(rs_n_ready, 2)
            for t in range(NT):
                act.activation(lat[:, t, 0:QL], banks[2 * t][:, 0:QL], ACT.Copy, scale=rs_n[:, 2 * t:2 * t + 1]) \
                    .then_inc(lat_ready, 1)
            act.wait_ge(lat_ready, 2 * NT)
            for i in range(2 * NT):
                if i:
                    act.wait_ge(lsq_ready, i)
                at, width = ((0, QL), (QL, KVL))[i // NT]
                act.activation(lat_sq[:, 0:width], lat[:, i % NT, at:at + width], ACT.Square,
                               accum_out=lat_stat[:, 0, i:i + 1]).then_inc(lsq_ready, 1)
            act.wait_ge(lsq_ready, 2 * NT)
            for i, width in enumerate((QL, KVL)):
                act.activation(lat_stat[:, 1, i * NT:(i + 1) * NT], lat_stat[:, 0, i * NT:(i + 1) * NT], ACT.Sqrt,
                               scale=1.0 / width, bias=eps[:, 0:1]).then_inc(lrms_ready, 1)

            def b_pt_hi(unit, base, dst, src_rows=P, scale=1.0):
                wait(act, pt_done, unit + base + 1)
                act.activation(dst, banks[3 + unit % 2][0:src_rows, :], ACT.Copy, scale=scale).then_inc(pt_hi_ready, 1)

            for b in range(QL // P):
                b_pt_hi(T_BPRE + b, 0, cq_hi[:, b, :], scale=g_q[:, b:b + 1])
            for b in range(KVL // P):
                b_pt_hi(T_BPRE + 3 + b, 0, ckv_hi[:, b, :], scale=g_kv[:, b:b + 1])
            act.wait_ge(pt_free, T_BPRE + 6)
            for hd in range(HG):
                act.activation(bk_hi[NOPE:QK, hd, :], rope_a[NOPE:QK, :], ACT.Copy) \
                    .then_inc(krope_hi if hd < HG - 1 else pt_hi_ready, 1)

            def b_q_out(g):
                if not isinstance(g, int):
                    wait(act, pt_done, T_B + B_TG * (g - 1))
                elif g:
                    act.wait_ge(pt_done, T_B + B_TG * (g - 1))
                for t in range(NT):
                    wait(act, proj_done, U_BG * g + t + 1)
                    act.activation(q_n[:, t, :], banks[6 + t % 2][:, 0:HG * QK], ACT.Copy, scale=QK ** -0.5) \
                        .then_inc(proj_free, 1)

            def b_k_hi(g):
                for i in range(2):
                    wait(act, proj_done, U_BG * g + 4 + i + 1)
                    for b in range(2):
                        act.activation(bk_hi[0:NOPE, 2 * i + b, :], banks[6 + i][b * HD:(b + 1) * HD, :], ACT.Copy) \
                            .then_inc(kp_hi_ready, 1)

            def b_q_hi(g, base):
                for hd in range(HG):
                    wait(act, pt_done, base + hd + 1)
                    act.activation(bq_hi[0:QK, hd, :], banks[3 + hd % 2][0:QK, :], ACT.Copy).then_inc(pt_hi_ready, 1)

            bv_hi_v = bv_hi[:].rearrange("p t a (s d) -> p (t a) s d", d=HD)

            def b_v_hi(g, first=False):
                if first:
                    wait(act, vec_consts, 9)
                else:
                    wait(act, o_done, 4 * GROUPS + 2 * g)
                for i in range(2):
                    wait(act, proj_done, U_BG * g + 6 + i + 1)
                    act.activation(bv_hi_v[:, 4 * i:4 * i + 4, ::2, :],
                                   banks[6 + i][:].rearrange("p (t s d) -> p t s d", t=4, s=2), ACT.Copy) \
                        .then_inc(v_hi_ready, 1)

            b_q_out(0)
            b_k_hi(0)
            b_v_hi(0, first=True)
            b_q_hi(0, T_BPRE + 6)

            def b_group(g, last):
                def expo(u):
                    n = u // 4
                    wait(act, max_ready, 16 * g + u + 1)
                    if u >= 8:
                        wait(act, pt_done, T_B + B_TG * g + 4 * (n - 1))
                    elif isinstance(g, int) and g == 0:
                        pass
                    else:
                        wait(act, pt_done, T_B + B_TG * g)
                    act.activation(s_b[:, n % 2, u % 4, :], banks[u % 3][:], ACT.Exp, bias=stat[:, 0, u % 8:u % 8 + 1],
                                   accum_out=stat[:, 1, u % 8:u % 8 + 1]).then_inc(exp_ready, 1)

                def pt_hi(n, i):
                    wait(act, pt_done, T_B + B_TG * g + 4 * n + i + 1)
                    act.activation(bpt_hi[:, n % 2, i, :], banks[3 + i % 2][:], ACT.Copy).then_inc(pt_hi_ready, 1)

                def o_hi(pair):
                    wait(act, o_done, 4 * GROUPS + 2 * g + pair + 1)
                    act.activation(ot_hi[:, 2 * g + pair, :], banks[5][:], ACT.Copy).then_inc(o_hi_ready, 1)

                for u in range(4):
                    expo(u)
                for n in range(HG):
                    if n < 3:
                        expo(4 * n + 4)
                        expo(4 * n + 5)
                        pt_hi(n, 0)
                        expo(4 * n + 6)
                        pt_hi(n, 1)
                        expo(4 * n + 7)
                        pt_hi(n, 2)
                        pt_hi(n, 3)
                        if n == 2:
                            o_hi(0)
                    else:
                        if not last:
                            b_q_out(g + 1)
                        for i in range(4):
                            pt_hi(n, i)
                        if not last:
                            b_k_hi(g + 1)
                            b_q_hi(g + 1, T_B + B_TG * g + 16)
                        o_hi(1)
                        if not last:
                            b_v_hi(g + 1)

            with act.Fori(0, GROUPS - 1) as g:
                b_group(g, False)
            b_group(GROUPS - 1, True)

            wo_phase(norms[3])
            ffn_half(1, 0, None)
            ffn_half(1, 1, norms[4])
            act.wait_ge(rs_n_ready, 3)
            act.wait_ge(pt_free, T_FIN + KD)
            for t in (1, 3):
                act.activation(out_n[:, t, :], out_n[:, t, :], ACT.Copy, scale=rs_n[:, 2 * t:2 * t + 1]) \
                    .then_inc(out_ready[1], 1)

        @block.tensor
        def _(pe):
            def product(o, lh, ll, rh, rl, start, stop):
                pe.matmul(o, ll, rh, start=start, stop=False)
                pe.matmul(o, lh, rl, start=False, stop=False)
                return pe.matmul(o, lh, rh, start=False, stop=stop)

            def w_block(s, cols, k):
                return w_hi[s][:, k * cols:(k + 1) * cols], w_lo[s][:, k * cols:(k + 1) * cols]

            def project(c2, s, unit, unit_base, src_hi, src_lo, blocks=KD, ready=None):
                pe.wait_ge(w_ready, 2 * c2 + s + 1)
                if not (isinstance(unit_base, int) and unit + unit_base < 2):
                    pe.wait_ge(proj_free, unit_base + unit - 1)
                for k in range(blocks):
                    if ready is not None:
                        pe.wait_ge(*ready(k))
                    wh, wl = w_block(s, P, k)
                    last = product(banks[6 + unit % 2][:], wh, wl, src_hi[:, k, :], src_lo[:, k, :],
                                   k == 0, k == blocks - 1)
                last.then_inc(w_used, 1)

            def sum_partitions(n):
                pe.wait_ge(sslo_ready, n.number + 1)
                if n.o_index:
                    pe.wait_ge(o_free, n.o_index)
                if n.sum_t is not None:
                    pe.matmul(n.sum_t[:], ones[:], n.ss_lo[:], start=True, stop=False)
                    last = pe.matmul(n.sum_t[:], ones[:], n.ss_hi[:], start=False, stop=True)
                if n.sum_n is not None:
                    for t in range(NT):
                        o = n.sum_n[:, 2 * t:2 * t + 2]
                        pe.matmul(o, n.ss_lo[:, t * P:(t + 1) * P], ones[:, 0:2], start=True, stop=False)
                        last = pe.matmul(o, n.ss_hi[:, t * P:(t + 1) * P], ones[:, 0:2], start=False, stop=True)
                last.then_inc(st_done, 1)

            pe.wait_ge(pool_consts, 2)
            for m in range(KD):
                if m >= 2:
                    pe.wait_ge(pt_free, m - 1)
                for t in range(NT):
                    if m == 0:
                        pe.wait_ge(x_in[t], 16)
                    last = pe.transpose(banks[3 + m % 2][:, t * P:(t + 1) * P], x_n[:, t, m * P:(m + 1) * P], ident[:])
                last.then_inc(pt_done, 1)

            pe.wait_ge(vec_consts, 7)
            project(0, 0, 0, 0, x_hi, x_lo, ready=lambda k: (x_ready, k + 1))
            pe.wait_ge(pt_free, KD)
            sum_partitions(norms[0])
            project(0, 1, 1, 0, x_hi, x_lo)
            pe.wait_ge(rms_n, 1)
            for s in range(2):
                pe.wait_ge(w_ready, C_V + s + 1)
                for t in range(NT):
                    for k in range(4):
                        wh, wl = w_block(s, GROUPS * HD, k)
                        xk = (4 * s + k, slice(t * P, (t + 1) * P))
                        last = product(banks[t][:, 0:GROUPS * HD], x_hi[:, xk[0], xk[1]], x_lo[:, xk[0], xk[1]],
                                       wh, wl, s == 0 and k == 0, s == 1 and k == 3)
                last.then_inc(w_used, 1)

            def a_q(g, i):
                project(C_Q // 2 + g, i, i, U_Q + 2 * g, x_hi, x_lo)

            a_q(0, 0)
            a_q(0, 1)

            def a_group(g, last):
                def scores(u):
                    n, hd = u // HG, u % HG
                    k0, nk = A_KB[n]
                    before = 16 * g + (u - 2 if u >= 3 else (0, -2, -1)[u])
                    pe.wait_ge(s_free, S_A + before)
                    q = (slice(None), hd // 2, slice(n * P, (n + 1) * P))
                    k = (slice(None), hd % 2, slice(k0 * P, (k0 + nk) * P))
                    product(banks[u % 3][:, 0:nk * P], aq_hi[q], aq_lo[q], kp_hi[k], kp_lo[k], True, True) \
                        .then_inc(s_done, 1)

                def transposes(n, i):
                    unit = T_A + A_T0[n] + i
                    pe.wait_ge(pt_free, A_TG * g + unit - 1)
                    for j, hd in enumerate((0, 2, 1, 3)):
                        if i == 0:
                            pe.wait_ge(p_ready, 16 * g + 4 * n + (hd + 1 if j != 2 else 3))
                        last_ = pe.transpose(banks[3 + unit % 2][:, j * P:(j + 1) * P],
                                             s_a[:, n % 2, hd, 1 + i * P:1 + (i + 1) * P], ident[:])
                    last_.then_inc(pt_done, 1)

                def values(n):
                    k0, nk = A_KB[n]
                    pe.wait_ge(pt_free, T_A + A_TG * g + A_T0[n] + nk)
                    pe.wait_ge(o_free, O_A + 4 * g + n)
                    if n == 0:
                        pe.wait_ge(v_ready, g + 1)
                    for i in range(nk):
                        for odd in range(2):
                            v = (slice(None), k0 + i, slice(0, P) if odd else slice(HD, HD + P))
                            p = (slice(None), n % 2, i, slice(2 * P * odd, 2 * P * (odd + 1)))
                            last_ = product(banks[5][:, 0:2 * P], av_hi[v], av_lo[v], apt_hi[p], apt_lo[p],
                                            i == 0 and odd == 0, i == nk - 1 and odd == 1)
                    last_.then_inc(o_done, 1)

                pe.wait_ge(q_ready, 2 * g + 2)
                pe.wait_ge(kp_ready, 2 * g + 2)
                for u in range(4):
                    scores(u)
                for n in range(NT):
                    nk = A_KB[n][1]
                    if n < 3:
                        scores(4 * n + 4)
                        scores(4 * n + 5)
                        transposes(n, 0)
                        scores(4 * n + 6)
                        transposes(n, 1)
                        scores(4 * n + 7)
                        if nk > 2:
                            transposes(n, 2)
                    else:
                        if not last:
                            a_q(g + 1, 0)
                        transposes(n, 0)
                        transposes(n, 1)
                    if n:
                        values(n - 1)
                if not last:
                    a_q(g + 1, 1)
                values(3)

            with pe.Fori(0, GROUPS - 1) as g:
                a_group(g, False)
            a_group(GROUPS - 1, True)

            def wo_phase(c0, u0, o_count):
                pe.wait_ge(o_free, o_count)
                with pe.Fori(0, KD // 2) as i:
                    for s in range(2):
                        project(c0 // 2 + i, s, s, u0 + 2 * i, ot_hi, ot_lo)

            def ffn_half(layer, half, n, fin=None):
                c2 = ((C_FFN0, C_FFN1)[layer] + half * C_HALF) // 2
                u0 = (U_FFN0, U_FFN1)[layer] + half * C_HALF
                j0 = (2 * layer + half) * HALF
                if n is not None:
                    project(c2, 0, 0, u0, x_hi, x_lo, ready=lambda k: (x_ready, n.base + k + 1))
                    sum_partitions(n)
                else:
                    project(c2, 0, 0, u0, x_hi, x_lo)
                project(c2, 1, 1, u0, x_hi, x_lo)
                with pe.Fori(1, HALF) as j:
                    for s in range(2):
                        project(c2 + j, s, s, u0 + 2 * j, x_hi, x_lo)

                def down(i, s, first=False):
                    project(c2 + HALF + i, s, s, u0 + 2 * HALF + 2 * i, f_hi, f_lo, blocks=HALF,
                            ready=(lambda k: (f_ready, j0 + k + 1)) if first else None)

                def turn(m0, s):
                    pe.wait_ge(proj_free, U_DOWN1 + m0 + s + 1)
                    pe.wait_ge(pt_free, T_FIN + m0 + s - 1)
                    for t in range(NT):
                        last = pe.transpose(banks[3 + s][:, t * P:(t + 1) * P], h_fin[:, s, t * P:(t + 1) * P], ident[:])
                    last.then_inc(pt_done, 1)

                down(0, 0, first=True)
                down(0, 1)
                if fin:
                    turn(0, 0)
                with pe.Fori(1, KD // 2) as i:
                    down(i, 0)
                    if fin:
                        turn(2 * i - 2, 1)
                    down(i, 1)
                    if fin:
                        turn(2 * i, 0)
                if fin:
                    turn(KD - 2, 1)
                    sum_partitions(norms[4])

            wo_phase(C_WOA, U_WOA, O_A + 4 * GROUPS)
            ffn_half(0, 0, norms[1])
            ffn_half(0, 1, None)

            pe.wait_ge(proj_free, U_B)
            for c in range(4):
                pe.wait_ge(w_ready, C_LAT + c + 1)
                for t in range(NT):
                    for kk in range(2):
                        k = 2 * c + kk
                        if t == 0:
                            pe.wait_ge(x_ready, norms[2].base + k + 1)
                        wh, wl = w_block(c % 2, B_IN, kk)
                        xh, xl = x_hi[:, k, t * P:(t + 1) * P], x_lo[:, k, t * P:(t + 1) * P]
                        for half, (a, b) in enumerate(((0, QL), (QL, B_IN))):
                            last = product(banks[2 * t + half][:, 0:b - a], xh, xl, wh[:, a:b], wl[:, a:b],
                                           k == 0, k == KD - 1)
                last.then_inc(w_used, 1)
            sum_partitions(norms[2])
            pe.wait_ge(latn_ready, 2 * NT)
            for b in range(QL // P + KVL // P):
                if b >= 2:
                    pe.wait_ge(pt_free, T_BPRE + b - 1)
                for t in range(NT):
                    last = pe.transpose(banks[3 + b % 2][:, t * P:(t + 1) * P], lat[:, t, b * P:(b + 1) * P], ident[:])
                last.then_inc(pt_done, 1)
            pe.wait_ge(rope_v, 4)
            pe.wait_ge(pt_free, T_BPRE + 4)
            for t in range(NT):
                last = pe.transpose(banks[4][0:ROPE, t * P:(t + 1) * P], lat[:, t, QL + KVL:B_IN], ident[:])
            last.then_inc(pt_done, 1)

            def b_q(g):
                pe.wait_ge(w_ready, C_B + 2 * g + 1)
                for t in range(NT):
                    pe.wait_ge(proj_free, U_B + U_BG * g + t - 1)
                    for k in range(QL // P):
                        wh, wl = w_block(0, HG * QK, k)
                        ch, cl = cq_hi[:, k, t * P:(t + 1) * P], cq_lo[:, k, t * P:(t + 1) * P]
                        last = product(banks[6 + t % 2][:, 0:HG * QK], ch, cl, wh, wl, k == 0, k == QL // P - 1)
                    last.then_inc(proj_done, 1)

            def b_k(g):
                pe.wait_ge(w_ready, C_B + 2 * g + 2)
                for i in range(2):
                    pe.wait_ge(proj_free, U_B + U_BG * g + 4 + i - 1)
                    for k in range(KVL // P):
                        wh, wl = (w[1][:, k * HG * HD + i * P:k * HG * HD + (i + 1) * P] for w in (w_hi, w_lo))
                        o = banks[6 + i][:]
                        first = pe.matmul(o, wl, ckv_hi[:, k, :], start=k == 0, stop=False)
                        if i == 0 and k == 0:
                            first.then_inc(w_used, 1)
                        pe.matmul(o, wh, ckv_lo[:, k, :], start=False, stop=False)
                        last = pe.matmul(o, wh, ckv_hi[:, k, :], start=False, stop=k == KVL // P - 1)
                    last.then_inc(proj_done, 1)

            def b_v(g):
                for i in range(2):
                    pe.wait_ge(proj_free, U_B + U_BG * g + 6 + i - 1)
                    for t in (2 * i, 2 * i + 1):
                        o = banks[6 + i][:, t % 2 * HG * HD:(t % 2 + 1) * HG * HD]
                        for k in range(KVL // P):
                            wh, wl = (w[1][:, W_UKV // 2 + k * HG * HD:W_UKV // 2 + (k + 1) * HG * HD]
                                      for w in (w_hi, w_lo))
                            ch, cl = ckv_hi[:, k, t * P:(t + 1) * P], ckv_lo[:, k, t * P:(t + 1) * P]
                            last = product(o, ch, cl, wh, wl, k == 0, k == KVL // P - 1)
                    last.then_inc(proj_done, 1)

            def b_turn_q(g, base, w_free):
                pe.wait_ge(rope_v, 4 * g + 8)
                for hd in range(HG):
                    pe.wait_ge(pt_free, base + hd - 1)
                    for t in range(NT):
                        last = pe.transpose(banks[3 + hd % 2][0:QK, t * P:(t + 1) * P],
                                            q_n[:, t, hd * QK:(hd + 1) * QK], ident[:])
                        if w_free and hd == 0 and t == 0:
                            last.then_inc(w_used, 1)
                    last.then_inc(pt_done, 1)

            pe.wait_ge(pt_free, T_BPRE + 5)
            b_q(0)
            b_k(0)
            b_v(0)
            b_turn_q(0, T_BPRE + 6, True)
            pe.wait_ge(krope_ready, HG)

            def b_group(g, last):
                def scores(u):
                    n, qb = u // 4, u % 4
                    before = 16 * g + (u - 2 if u >= 3 else (0, -2, -1)[u])
                    pe.wait_ge(exp_ready, S_B - S_A + before)
                    q = (slice(0, QK), n, slice(qb * P, (qb + 1) * P))
                    k = (slice(0, QK), n, slice(None))
                    product(banks[u % 3][:], bq_hi[q], bq_lo[q], bk_hi[k], bk_lo[k], True, True).then_inc(s_done, 1)

                def transposes(n, i):
                    pe.wait_ge(pt_free, T_B + B_TG * g + 4 * n + i - 1)
                    for qb in range(NT):
                        if i == 0:
                            pe.wait_ge(p_ready, 16 * (GROUPS + g) + 4 * n + qb + 1)
                        last_ = pe.transpose(banks[3 + i % 2][:, qb * P:(qb + 1) * P],
                                             s_b[:, n % 2, qb, i * P:(i + 1) * P], ident[:])
                    last_.then_inc(pt_done, 1)

                def values(n, w_free=False):
                    pe.wait_ge(pt_free, T_B + B_TG * g + 4 * n + 4)
                    if n % 2 == 0:
                        pe.wait_ge(o_free, O_B + 2 * g + n // 2)
                    for i in range(NT):
                        v = (slice(None), i, n // 2, slice(HD, HD + P) if n % 2 else slice(0, P))
                        p = (slice(None), n % 2, i, slice(None))
                        o = banks[5][:]
                        first = pe.matmul(o, bv_lo[v], bpt_hi[p], start=n % 2 == 0 and i == 0, stop=False)
                        if w_free and i == 0:
                            first.then_inc(w_used, 1)
                        pe.matmul(o, bv_hi[v], bpt_lo[p], start=False, stop=False)
                        last_ = pe.matmul(o, bv_hi[v], bpt_hi[p], start=False, stop=n % 2 == 1 and i == NT - 1)
                    if n % 2:
                        last_.then_inc(o_done, 1)

                pe.wait_ge(proj_free, U_B + U_BG * g + U_BG)
                pe.wait_ge(pt_free, T_B + B_TG * g)
                for u in range(4):
                    scores(u)
                for n in range(HG):
                    if n < 3:
                        scores(4 * n + 4)
                        scores(4 * n + 5)
                        transposes(n, 0)
                        scores(4 * n + 6)
                        transposes(n, 1)
                        scores(4 * n + 7)
                        transposes(n, 2)
                        transposes(n, 3)
                        if n:
                            values(n - 1)
                    else:
                        if not last:
                            b_q(g + 1)
                        for i in range(4):
                            transposes(n, i)
                        values(2)
                        if not last:
                            b_k(g + 1)
                            b_turn_q(g + 1, T_B + B_TG * g + 16, False)
                            b_v(g + 1)
                        values(3, w_free=not last)

            with pe.Fori(0, GROUPS - 1) as g:
                b_group(g, False)
            b_group(GROUPS - 1, True)

            wo_phase(C_WOB, U_WOB, O_B + 2 * GROUPS)
            ffn_half(1, 0, norms[3])
            ffn_half(1, 1, None, fin=True)

        @block.vector
        def _(dve):
            def w_split_lo(c2, s, cols, kv=False):
                wait(dve, w_hi_ready, 2 * c2 + s + 1)
                dve.tensor_tensor(split_part(w_lo, s, cols, kv), raw_part(s, cols, kv), f(split_part(w_hi, s, cols, kv)),
                                  ALU.subtract) \
                    .then_inc(w_ready, 1)

            def split_x_lo(n, m):
                wait(dve, x_hi_ready, n.base + m + 1)
                dve.scalar_tensor_tensor(x_lo[:, m, :], h[:, m, :], gains[:, n.gain, m, :], f(x_hi[:, m, :]),
                                         ALU.mult, ALU.subtract).then_inc(x_ready, 1)

            def split_sum(n):
                dve.wait_ge(sshi_ready, n.number + 1)
                dve.tensor_tensor(n.ss_lo[:], n.ss[:], f(n.ss_hi[:]), ALU.subtract).then_inc(sslo_ready, 1)

            def invert_t(n, count):
                dve.wait_ge(o_free, n.o_index + 1)
                dve.reciprocal(rs_t[:], rs_t[:]).then_inc(rs_t_ready, 1)
                dve.wait_ge(rs_t_ready, count)

            def invert_n(count):
                dve.wait_ge(rms_n, count)
                dve.reciprocal(rs_n[:], rs_n[:]).then_inc(rs_n_ready, 1)

            dve.memset(eps[:], EPS).then_inc(vec_consts, 1)
            dve.memset(f(ones[:]), 1.0).then_inc(vec_consts, 1)
            for t in (kp_hi, kp_lo, av_hi, av_lo):
                dve.memset(f(t[:]), 0.0).then_inc(vec_consts, 1)
            w_split_lo(0, 0, W_COLS)
            w_split_lo(0, 1, W_COLS)
            dve.wait_ge(small_in, 9 * 16)
            with dve.Fori(0, KD // 2) as i:
                for s in range(2):
                    m = 2 * i + s
                    wait(dve, pt_done, m + 1)
                    dve.tensor_copy(h[:, m, :], banks[3 + s][:]).then_inc(pt_free, 1)
                    split_x_lo(norms[0], m)
            split_sum(norms[0])
            dve.tensor_scalar(par_all[:, :, HG:], sink_in[:].rearrange("p (g h) -> p g h", g=GROUPS), -1.0, None,
                              ALU.mult).then_inc(vec_consts, 1)
            for qb in range(NT):
                nk = A_KB[qb][1]
                dve.wait_ge(near_p, qb + 1)
                view = near[:, qb, 0:nk * P]
                dve.tensor_copy(view, dist_i[:, qb, 0:nk * P]).then_inc(near_v, 1)
                dve.wait_ge(near_v, 2 * qb + 1)
                dve.scalar_tensor_tensor(view, view, -1.0, view, ALU.mult, ALU.min).then_inc(near_v, 1)

            tab = [0]

            def step(ins):
                tab[0] += 1
                ins.then_inc(tab_v, 1)
                dve.wait_ge(tab_v, tab[0])

            dve.wait_ge(pool_consts, 2 + HEADS + ROPE // 2)
            step(dve.tensor_copy(pos_f[:], pos_q[:]))
            for t in range(NT):
                step(dve.tensor_scalar(ang[:, t, :], inv_f[:], pos_f[:, t:t + 1], None, ALU.mult))
            step(dve.tensor_scalar(turns[:], ang[:], float(1.0 / (2.0 * np.pi)), None, ALU.mult))
            step(dve.tensor_scalar(turns[:], turns[:], ROUND, None, ALU.add))
            step(dve.tensor_scalar(turns[:], turns[:], ROUND, None, ALU.subtract))
            step(dve.tensor_scalar(turns_hi[:], turns[:], 1.0 / 2048.0, None, ALU.mult))
            step(dve.tensor_scalar(turns_hi[:], turns_hi[:], ROUND, None, ALU.add))
            step(dve.tensor_scalar(turns_hi[:], turns_hi[:], ROUND, 2048.0, ALU.subtract, ALU.mult))
            step(dve.tensor_tensor(turns[:], turns[:], turns_hi[:], ALU.subtract))
            for part in two_pi_parts():
                step(dve.scalar_tensor_tensor(ang[:], turns_hi[:], -part, ang[:], ALU.mult, ALU.add))
                step(dve.scalar_tensor_tensor(ang[:], turns[:], -part, ang[:], ALU.mult, ALU.add))
            step(dve.tensor_scalar(ang[:], ang[:], 3.1415925, -3.1415925, ALU.min, ALU.max))
            assert tab[0] == TAB_STEPS

            w_split_lo(C_V // 2, 0, 4 * GROUPS * HD)
            invert_n(1)
            invert_t(norms[0], 1)
            for m in range(2):
                dve.wait_ge(w_used, m + 1)
                for a in range(2):
                    rows = slice(a * HD, (a + 1) * HD)
                    for b in range(2):
                        ins = dve.tensor_tensor(k_dup[b * HD:(b + 1) * HD, 2 * m + a, :], banks[6 + m][rows, :],
                                                rs_t[rows, :], ALU.mult)
                        if a == 1 and b == 1:
                            ins.then_inc(proj_free, 1)
                        else:
                            ins.then_inc(k_dup_ready, 1)
                if m == 0:
                    w_split_lo(C_V // 2, 1, 4 * GROUPS * HD)
            for s in range(2):
                w_split_lo(C_Q // 2, s, W_COLS)

            def a_k_lo(g):
                for b in range(2):
                    rows = slice(b * HD, (b + 1) * HD)
                    wait(dve, kp_hi_ready, 2 * g + b + 1)
                    dve.tensor_tensor(kp_lo[rows, b, :], k_dup[rows, g, :], f(kp_hi[rows, b, :]), ALU.subtract) \
                        .then_inc(kp_ready, 1)

            v_by_group = v_all[:].rearrange("p t (g d) -> p t g d", g=GROUPS)

            def a_v_lo(g):
                wait(dve, v_hi_ready, g + 1)
                dve.tensor_tensor(av_lo[:, :, HD:2 * HD], v_by_group[:, :, g, :], f(av_hi[:, :, HD:2 * HD]),
                                  ALU.subtract).then_inc(v_ready, 1)

            def a_q_out(g, i, first=False):
                wait(dve, w_used, C_Q + 2 * g + i + 1)
                if not (first and i == 0):
                    wait(dve, q_ready, 2 * g + i)
                dve.scalar_tensor_tensor(q_tmp[:], banks[6 + i][:], HD ** -0.5, rs_t[:], ALU.mult, ALU.mult) \
                    .then_inc(proj_free, 1)

            def a_q_lo(g, i):
                wait(dve, q_hi_ready, 2 * g + i + 1)
                dve.tensor_tensor(aq_lo[:, i, :], q_tmp[:], f(aq_hi[:, i, :]), ALU.subtract).then_inc(q_ready, 1)

            a_k_lo(0)
            for i in range(2):
                a_q_out(0, i, first=True)
                a_q_lo(0, i)
            a_v_lo(0)
            dve.wait_ge(tab_a, 1)
            step(dve.tensor_tensor(turns[:], half_sin[:], half_sin[:], ALU.mult))
            step(dve.tensor_scalar(cos_n[:, :, 0:16], turns[:], -2.0, 1.0, ALU.mult, ALU.add))
            step(dve.tensor_scalar(cos_n[:, :, 16:32], turns[:], -2.0, 1.0, ALU.mult, ALU.add))
            dve.wait_ge(tab_a, 2)
            step(dve.tensor_scalar(sin_n[:, :, 0:16], sin_n[:, :, 16:32], -1.0, None, ALU.mult))

            ot_lo_q = ot_lo[:].rearrange("p (g a) (n q) -> p g a n q", a=2, n=NT)
            ot_hi_q = ot_hi[:].rearrange("p (g a) (n q) -> p g a n q", a=2, n=NT)

            def invert_sum(count, u):
                wait(dve, exp_ready, count)
                dve.reciprocal(stat[:, 2, u % 8:u % 8 + 1], stat[:, 1, u % 8:u % 8 + 1]).then_inc(rsum_ready, 1)

            def a_group(g, last):
                def read_scores(u):
                    n, hd = u // HG, u % HG
                    w = A_KB[n][1] * P
                    wait(dve, bias_ready, 16 * g + u + 1)
                    wait(dve, s_done, 16 * g + u + 1)
                    if n >= 2:
                        wait(dve, pt_done, T_A + A_TG * g + A_T0[n - 1])
                    dve.tensor_tensor_reduce(s_a[:, n % 2, hd, 1:1 + w], bias[:, u % 2, 0:w], banks[u % 3][:, 0:w],
                                             -1.0, par[:, HG + hd:HG + hd + 1], ALU.add, ALU.min,
                                             stat[:, 0, u % 8:u % 8 + 1]).then_inc(s_free, 1)

                def pt_lo(n, i):
                    unit = T_A + A_T0[n] + i
                    wait(dve, pt_hi_ready, unit - T_A + A_TG * g + 1)
                    dve.tensor_tensor(apt_lo[:, n % 2, i, :], banks[3 + unit % 2][:], f(apt_hi[:, n % 2, i, :]),
                                      ALU.subtract).then_inc(pt_free, 1)

                def o_lo(n):
                    wait(dve, o_hi_ready, 4 * g + n + 1)
                    dve.tensor_tensor(ot_lo_q[:, g, :, n, :], banks[5][:, 0:2 * P].rearrange("p (a q) -> p a q", a=2),
                                      f(ot_hi_q[:, g, :, n, :]), ALU.subtract).then_inc(o_free, 1)

                def inv(u):
                    invert_sum(16 * g + u + 1, u)

                read_scores(0)
                read_scores(1)
                inv(0)
                read_scores(2)
                inv(1)
                read_scores(3)
                inv(2)
                inv(3)
                for n in range(NT):
                    nk = A_KB[n][1]
                    u = 4 * n + 4
                    if n < 3:
                        read_scores(u)
                        read_scores(u + 1)
                        pt_lo(n, 0)
                        inv(u)
                        read_scores(u + 2)
                        pt_lo(n, 1)
                        inv(u + 1)
                        read_scores(u + 3)
                        if nk > 2:
                            pt_lo(n, 2)
                        inv(u + 2)
                        inv(u + 3)
                        if n < 2:
                            w_split_lo(C_Q // 2 + 1 + g, n, W_COLS)
                    else:
                        if not last:
                            a_q_out(g + 1, 0)
                        pt_lo(n, 0)
                        pt_lo(n, 1)
                        if not last:
                            a_q_lo(g + 1, 0)
                            a_k_lo(g + 1)
                    if n:
                        o_lo(n - 1)
                if not last:
                    a_q_out(g + 1, 1)
                    a_q_lo(g + 1, 1)
                o_lo(3)
                if not last:
                    a_v_lo(g + 1)

            with dve.Fori(0, GROUPS - 1) as g:
                a_group(g, False)
            a_group(GROUPS - 1, True)

            def add_to_h(c, bank_s, m, used, dst=None):
                wait(dve, w_used, used)
                dst = h[:, m, :] if dst is None else dst
                dve.tensor_tensor(dst, h[:, m, :], banks[6 + bank_s][:], ALU.add).then_inc(proj_free, 1)

            def wo_phase(n, c0):
                with dve.Fori(0, KD // 2) as i:
                    for s in range(2):
                        w_split_lo(c0 // 2 + 1 + i, s, W_COLS)
                        add_to_h(c0, s, 2 * i + s, c0 + 2 * i + s + 1)
                        split_x_lo(n, 2 * i + s)
                split_sum(n)

            def ffn_half(layer, half, n, rs_count, next_cols):
                c2 = ((C_FFN0, C_FFN1)[layer] + half * C_HALF) // 2
                j0 = (2 * layer + half) * HALF

                def hidden(j, cols, ahead=True):
                    w_split_lo(c2 + j + 1, 0, cols)
                    if rs_count is not None and isinstance(j, int) and j == 0:
                        invert_t(norms[2 * layer + 1], rs_count)
                    wait(dve, w_used, 2 * c2 + 2 * j + 1)
                    if not (isinstance(j, int) and j0 + j == 0):
                        wait(dve, silu_ready, j0 + j)
                    dve.tensor_tensor(gate_t[:], banks[6][:], rs_t[:], ALU.mult).then_inc(proj_free, 1)
                    w_split_lo(c2 + j + 1, 1, cols)
                    wait(dve, w_used, 2 * c2 + 2 * j + 2)
                    wait(dve, silu_rs_ready, j0 + j + 1)
                    if not (isinstance(j, int) and j0 + j == 0):
                        wait(dve, f_ready, j0 + j)
                    dve.tensor_tensor(hid[:], banks[7][:], gate_s[:], ALU.mult).then_inc(proj_free, 1)
                    wait(dve, f_hi_ready, j0 + j + 1)
                    dve.tensor_tensor(f_lo[:, j, :], hid[:], f(f_hi[:, j, :]), ALU.subtract).then_inc(f_ready, 1)

                hidden(0, W_COLS)
                with dve.Fori(1, HALF - 1) as j:
                    hidden(j, W_COLS)
                hidden(HALF - 1, W_DOWN)

                def turned(m, s):
                    wait(dve, pt_done, T_FIN + m + 1)
                    dve.tensor_tensor(out_n_v[:, :, m, :], banks[3 + s][:].rearrange("p (t n) -> p t n", t=NT),
                                      g_fin[:, m, :].unsqueeze(1).to_broadcast([P, NT, P]), ALU.mult) \
                        .then_inc(pt_free, 1)

                final = n is not None and n.gain is None

                def pair(i, cols):
                    for s in range(2):
                        m = 2 * i + s
                        if cols:
                            w_split_lo(c2 + HALF + 1 + i, s, cols)
                        if final and not (isinstance(i, int) and i == 0):
                            wait(dve, pt_done, T_FIN + m - 1)
                            wait(dve, sq_ready, n.base + m - 1)
                        add_to_h(c2, s, m, 2 * c2 + 2 * HALF + m + 1, h_fin[:, s, :] if final else None)
                        if final:
                            if not (isinstance(i, int) and i == 0 and s == 0):
                                turned(m - 1, 1 - s)
                        elif n is not None:
                            split_x_lo(n, m)

                pair(0, W_DOWN)
                with dve.Fori(1, KD // 2 - 1) as i:
                    pair(i, W_DOWN)
                pair(KD // 2 - 1, next_cols)
                if n is not None:
                    split_sum(n)
                if final:
                    turned(KD - 1, 1)

            out_n_v = out_n[:].rearrange("p t (m n) -> p t m n", n=P)

            wo_phase(norms[1], C_WOA)
            ffn_half(0, 0, None, 2, W_COLS)
            ffn_half(0, 1, norms[2], None, W_LAT)

            w_split_lo(C_LAT // 2 + 1, 0, W_LAT)
            w_split_lo(C_LAT // 2 + 1, 1, W_LAT)
            invert_n(2)
            dve.wait_ge(rs_n_ready, 2)
            for t in range(NT):
                dve.tensor_scalar(lat[:, t, QL:B_IN], banks[2 * t + 1][:, 0:B_IN - QL], rs_n[:, 2 * t:2 * t + 1], None,
                                  ALU.mult).then_inc(lat_ready, 1)
            w_split_lo(C_B // 2, 0, W_UQ)
            w_split_lo(C_B // 2, 1, W_UKV, kv=True)

            def rotate(view, cos_v, sin_v, a, b, base):
                dve.tensor_tensor(a, view, cos_v, ALU.mult).then_inc(rope_v, 1)
                dve.tensor_tensor(b[..., 0:16], view[..., 16:32], sin_v[..., 0:16], ALU.mult).then_inc(rope_v, 1)
                dve.tensor_tensor(b[..., 16:32], view[..., 0:16], sin_v[..., 16:32], ALU.mult).then_inc(rope_v, 1)
                wait(dve, rope_v, base + 3)
                dve.tensor_tensor(view, a, b, ALU.add).then_inc(rope_v, 1)

            dve.wait_ge(lat_ready, 2 * NT)
            dve.wait_ge(tab_v, TAB_STEPS + 4)
            rotate(lat[:, :, QL + KVL:B_IN], cos_n[:], sin_n[:],
                   rope_a[:, 0:NT * ROPE].rearrange("p (t d) -> p t d", t=NT),
                   rope_b[:, 0:NT * ROPE].rearrange("p (t d) -> p t d", t=NT), 0)
            dve.wait_ge(lrms_ready, 2)
            dve.reciprocal(lat_stat[:, 2, :], lat_stat[:, 1, :]).then_inc(lrs_ready, 1)
            dve.wait_ge(lrs_ready, 1)
            for t in range(NT):
                dve.tensor_scalar(lat[:, t, 0:QL], lat[:, t, 0:QL], lat_stat[:, 2, t:t + 1], None, ALU.mult) \
                    .then_inc(latn_ready, 1)

            dve.wait_ge(rms_n, 2)
            for t in (bv_hi, bv_lo):
                dve.memset(f(t[:]), 0.0).then_inc(vec_consts, 1)

            def b_pt_lo(unit, base, dst, hi, rows=P, gain=None):
                wait(dve, pt_hi_ready, unit - T_A + base + 1)
                src = banks[3 + unit % 2][0:rows, :]
                if gain is None:
                    dve.tensor_tensor(dst, src, f(hi), ALU.subtract).then_inc(pt_free, 1)
                else:
                    dve.scalar_tensor_tensor(dst, src, gain, f(hi), ALU.mult, ALU.subtract).then_inc(pt_free, 1)

            for b in range(QL // P):
                b_pt_lo(T_BPRE + b, 0, cq_lo[:, b, :], cq_hi[:, b, :], gain=g_q[:, b:b + 1])
            for b in range(KVL // P):
                b_pt_lo(T_BPRE + 3 + b, 0, ckv_lo[:, b, :], ckv_hi[:, b, :], gain=g_kv[:, b:b + 1])
            dve.wait_ge(pt_done, T_BPRE + 6)
            dve.wait_ge(rope_v, 4)
            dve.tensor_copy(rope_a[NOPE:QK, :], banks[4][0:ROPE, :]).then_inc(pt_free, 1)
            for hd in range(HG):
                if hd < HG - 1:
                    dve.wait_ge(krope_hi, hd + 1)
                else:
                    dve.wait_ge(pt_hi_ready, T_BPRE + 6 - T_A)
                ins = dve.tensor_tensor(bk_lo[NOPE:QK, hd, :], rope_a[NOPE:QK, :], f(bk_hi[NOPE:QK, hd, :]), ALU.subtract)
                ins.then_inc(krope_ready, 1)

            def b_rotate_q(g):
                wait(dve, proj_free, U_B + U_BG * g + 4)
                view = q_n[:].rearrange("p t (h d) -> p t h d", h=HG)[:, :, :, NOPE:QK]
                shape = [P, NT, HG, ROPE]
                rotate(view, cos_n[:].unsqueeze(2).to_broadcast(shape), sin_n[:].unsqueeze(2).to_broadcast(shape),
                       rope_a[:].rearrange("p (t h d) -> p t h d", t=NT, h=HG),
                       rope_b[:].rearrange("p (t h d) -> p t h d", t=NT, h=HG), 4 * g + 4)

            def b_k_lo(g):
                for i in range(2):
                    for b in range(2):
                        wait(dve, kp_hi_ready, 2 * GROUPS + 4 * g + 2 * i + b + 1)
                        ins = dve.tensor_tensor(bk_lo[0:NOPE, 2 * i + b, :], banks[6 + i][b * HD:(b + 1) * HD, :],
                                                f(bk_hi[0:NOPE, 2 * i + b, :]), ALU.subtract)
                        if b:
                            ins.then_inc(proj_free, 1)

            def b_q_lo(g, base):
                for hd in range(HG):
                    wait(dve, pt_hi_ready, base - T_A + hd + 1)
                    dve.tensor_tensor(bq_lo[0:QK, hd, :], banks[3 + hd % 2][0:QK, :], f(bq_hi[0:QK, hd, :]),
                                      ALU.subtract).then_inc(pt_free, 1)

            bv_hi_v = bv_hi[:].rearrange("p t a (s d) -> p (t a) s d", d=HD)
            bv_lo_v = bv_lo[:].rearrange("p t a (s d) -> p (t a) s d", d=HD)

            def b_v_lo(g):
                for i in range(2):
                    wait(dve, v_hi_ready, GROUPS + 2 * g + i + 1)
                    dve.tensor_tensor(bv_lo_v[:, 4 * i:4 * i + 4, ::2, :],
                                      banks[6 + i][:].rearrange("p (t s d) -> p t s d", t=4, s=2),
                                      f(bv_hi_v[:, 4 * i:4 * i + 4, ::2, :]), ALU.subtract).then_inc(proj_free, 1)

            dve.wait_ge(krope_ready, HG)
            b_rotate_q(0)
            b_k_lo(0)
            b_v_lo(0)
            b_q_lo(0, T_BPRE + 6)

            def b_group(g, last, cols0, cols1):
                def maximum(u):
                    wait(dve, s_done, 16 * (GROUPS + g) + u + 1)
                    dve.tensor_reduce(stat[:, 0, u % 8:u % 8 + 1], banks[u % 3][:], AX_X, ALU.max, negate=True) \
                        .then_inc(max_ready, 1)

                def pt_lo(n, i):
                    wait(dve, pt_hi_ready, T_B - T_A + B_TG * g + 4 * n + i + 1)
                    dve.tensor_tensor(bpt_lo[:, n % 2, i, :], banks[3 + i % 2][:], f(bpt_hi[:, n % 2, i, :]),
                                      ALU.subtract).then_inc(pt_free, 1)

                def o_lo(pair):
                    wait(dve, o_hi_ready, 4 * GROUPS + 2 * g + pair + 1)
                    dve.tensor_tensor(ot_lo[:, 2 * g + pair, :], banks[5][:], f(ot_hi[:, 2 * g + pair, :]),
                                      ALU.subtract).then_inc(o_free, 1)

                def inv(u):
                    invert_sum(16 * (GROUPS + g) + u + 1, u)

                maximum(0)
                maximum(1)
                inv(0)
                maximum(2)
                inv(1)
                maximum(3)
                inv(2)
                inv(3)
                for n in range(HG):
                    u = 4 * n + 4
                    if n < 3:
                        maximum(u)
                        maximum(u + 1)
                        pt_lo(n, 0)
                        inv(u)
                        maximum(u + 2)
                        pt_lo(n, 1)
                        inv(u + 1)
                        maximum(u + 3)
                        pt_lo(n, 2)
                        inv(u + 2)
                        pt_lo(n, 3)
                        inv(u + 3)
                        if n < 2:
                            w_split_lo(C_B // 2 + 1 + g, n, (cols0, cols1)[n], kv=n == 1 and cols0 == W_UQ)
                        else:
                            o_lo(0)
                    else:
                        for i in range(4):
                            pt_lo(n, i)
                        if not last:
                            b_rotate_q(g + 1)
                            b_k_lo(g + 1)
                            b_q_lo(g + 1, T_B + B_TG * g + 16)
                        o_lo(1)
                        if not last:
                            b_v_lo(g + 1)

            with dve.Fori(0, GROUPS - 1) as g:
                b_group(g, False, W_UQ, W_UKV)
            b_group(GROUPS - 1, True, W_COLS, W_COLS)

            wo_phase(norms[3], C_WOB)
            ffn_half(1, 0, None, 3, W_COLS)
            ffn_half(1, 1, norms[4], None, 0)
            invert_n(3)
            dve.wait_ge(rs_n_ready, 3)
            dve.wait_ge(pt_free, T_FIN + KD)
            for t in (0, 2):
                dve.tensor_scalar(out_n[:, t, :], out_n[:, t, :], rs_n[:, 2 * t:2 * t + 1], None, ALU.mult) \
                    .then_inc(out_ready[0], 1)


_INS = ["x", "positions", "norm_mix", "norm_ffn", "a_w_qkv", "a_sink", "a_w_o", "b_w_in", "b_g_q", "b_g_kv",
        "b_w_uq", "b_w_ukv", "b_w_o", "ffn_w_gu", "ffn_w_down", "final_norm"]


def kernel(**inputs):
    import concourse.bacc as bacc
    from concourse.bass_utils import run_bass_kernel_spmd as run

    nc = bacc.Bacc("TRN2", target_bir_lowering=False, num_devices=1)
    arrays, args = {}, []
    for name in _INS:
        a = np.ascontiguousarray(inputs[name])
        arrays[f"in_{name}"] = a
        args.append(nc.dram_tensor(f"in_{name}", a.shape, mybir.dt.from_np(a.dtype), kind="ExternalInput").ap())
    args.append(nc.dram_tensor("out_0", (1, T, D), F32, kind="ExternalOutput").ap())
    build(nc, *args)
    r = run(nc, [arrays], core_ids=[0])
    return r.results[0]["out_0"]
```

```python
from contextlib import ExitStack

import numpy as np
import concourse.bass as bass
from concourse import mybir

F32 = mybir.dt.float32
F32R = mybir.dt.float32r
I32 = mybir.dt.int32
ALU = mybir.AluOpType
ACT = mybir.ActivationFunctionType
AX_X = mybir.AxisListType.X

P = 128
D = 1024
KD = D // P
T = 512
NT = T // P
HEADS = 16
GROUPS = 4
HG = HEADS // GROUPS
HD = 64
WINDOW = 128
QL, KVL, ROPE, NOPE = 384, 256, 32, 64
B_IN = QL + KVL + ROPE
QK = NOPE + ROPE
DFF = 2816
FB = DFF // P
HALF = FB // 2
EPS = 1e-6
MASKED = -1e36
SLOT = HALF * P
SA = 1 + 3 * P

C_K, C_V, C_Q, C_WOA = 0, 2, 4, 12
C_FFN0 = C_WOA + KD
C_HALF = 2 * HALF + KD
C_LAT = C_FFN0 + 2 * C_HALF
C_B = C_LAT + 4
C_WOB = C_B + 2 * GROUPS
C_FFN1 = C_WOB + KD
C_END = C_FFN1 + 2 * C_HALF
W_COLS = KD * P
W_DOWN = HALF * P
W_LAT = 2 * B_IN
W_UQ = QL // P * HG * QK
W_UKV = KVL // P * HG * 2 * HD

U_K, U_Q, U_WOA = 0, 2, 10
U_FFN0 = U_WOA + KD
U_B = U_FFN0 + 2 * C_HALF
U_BG = 8
U_WOB = U_B + U_BG * GROUPS
U_FFN1 = U_WOB + KD

T_A = KD
A_KB = [(0, 2), (0, 3), (1, 3), (2, 2)]
A_T0 = [0, 2, 5, 8]
A_TG = 10
T_BPRE = T_A + A_TG * GROUPS
T_B = T_BPRE + 6 + HG
B_TG = 4 * HG + HG
T_FIN = T_B + B_TG * GROUPS - HG

O_NORM0, O_A = 0, 1
O_NORM1 = O_A + 4 * GROUPS
O_B = O_NORM1 + 1
O_NORM3 = O_B + 2 * GROUPS
S_A = 16
S_B = S_A + 16 * GROUPS

INV_FREQ = np.float32(10000.0) ** (-np.arange(16, dtype=np.float32) * np.float32(2.0) / np.float32(32))
ROUND = 12582912.0


TAB_STEPS = 21


def two_pi_parts():
    rest, parts = 2.0 * np.pi, []
    for _ in range(4):
        m, e = np.frexp(rest)
        part = float(np.ldexp(np.floor(m * 2048.0), int(e) - 11))
        parts.append(part)
        rest -= part
    return parts


def build(nc, x, positions, norm_mix, norm_ffn, a_w_qkv, a_sink, a_w_o, b_w_in, b_g_q, b_g_kv,
          b_w_uq, b_w_ukv, b_w_o, ffn_w_gu, ffn_w_down, final_norm, out):
    ctx = ExitStack()
    with ctx:
        place = {"at": (nc.sbuf_base + 63) // 64 * 64}
        top = nc.sbuf_usable_end

        def tile_at(name, shape, dtype, offset):
            size = 4 * int(np.prod(shape[1:]))
            assert offset + size <= top, (name, offset + size, top)
            return nc.alloc_sbuf_tensor_at(name, shape, dtype, offset=offset), offset + (size + 31) // 32 * 32

        def tile(name, shape, dtype=F32):
            t, place["at"] = tile_at(name, shape, dtype, place["at"])
            return t

        def region(start, specs):
            tiles, at = [], start
            for name, shape, dtype in specs:
                t, at = tile_at(name, shape, dtype, at)
                tiles.append(t)
            return tiles

        h = tile("h", [P, KD, T])
        x_hi = tile("x_hi", [P, KD, T], F32R)
        x_lo = tile("x_lo", [P, KD, T], F32R)
        ot_start = place["at"]
        ot_hi = tile("ot_hi", [P, KD, T], F32R)
        ot_lo = tile("ot_lo", [P, KD, T], F32R)
        scratch_size = 88 * 1024
        scratch = place["at"]
        place["at"] += scratch_size
        w_raw = [tile(f"w_raw{s}", [P, SLOT]) for s in range(2)]
        w_hi = [tile(f"w_hi{s}", [P, SLOT], F32R) for s in range(2)]
        w_lo = [tile(f"w_lo{s}", [P, SLOT], F32R) for s in range(2)]
        ident = tile("ident", [P, P])
        ones = tile("ones", [P, 2])
        rs_t = tile("rs_t", [P, T])
        rs_n = tile("rs_n", [P, 8])
        ms_n = tile("ms_n", [P, 3, 8])
        gains = tile("gains", [P, 4, KD, 1])
        g_q = tile("g_q", [P, QL // P])
        g_kv = tile("g_kv", [P, KVL // P])
        eps = tile("eps", [P, 1])
        par_all = tile("par_all", [P, GROUPS, 2 * HG])
        par = tile("par", [P, 2 * HG])
        sink_in = tile("sink_in", [P, HEADS])
        stat = tile("stat", [P, 3, 8])
        lat_stat = tile("lat_stat", [P, 3, 8])
        cos_n = tile("cos_n", [P, NT, ROPE])
        sin_n = tile("sin_n", [P, NT, ROPE])
        x_start = ot_start - 2 * 4 * KD * T

        x_n, sq0, ss0 = region(ot_start, [
            ("x_n", [P, NT, D], F32), ("sq0", [P, 2, T], F32), ("ss0", [P, T], F32)])
        (q_tmp, aq_hi, aq_lo, k_dup, kp_hi, kp_lo, v_all, av_hi, av_lo, near, bias, s_a, apt_hi, apt_lo) = \
            region(scratch, [
                ("q_tmp", [P, T], F32), ("aq_hi", [P, 2, T], F32R), ("aq_lo", [P, 2, T], F32R),
                ("k_dup", [P, GROUPS, T], F32), ("kp_hi", [P, 2, T], F32R), ("kp_lo", [P, 2, T], F32R),
                ("v_all", [P, NT, GROUPS * HD], F32),
                ("av_hi", [P, NT, 3 * HD], F32R), ("av_lo", [P, NT, 3 * HD], F32R),
                ("near", [P, NT, 3 * P], F32), ("bias", [P, 2, 3 * P], F32),
                ("s_a", [P, 2, HG, SA], F32),
                ("apt_hi", [P, 2, 3, T], F32R), ("apt_lo", [P, 2, 3, T], F32R)])
        pos_k, pos_q, dist_i = region(scratch + 58 * 1024, [
            ("pos_k", [P, T], I32), ("pos_q", [P, NT], I32), ("dist_i", [P, NT, 3 * P], I32)])
        pos_r, pos_f, inv_f, ang, turns, turns_hi, half_sin = region(scratch + 44 * 1024, [
            ("pos_r", [P, NT], I32), ("pos_f", [P, NT], F32), ("inv_f", [P, 16], F32), ("ang", [P, NT, 16], F32),
            ("turns", [P, NT, 16], F32), ("turns_hi", [P, NT, 16], F32), ("half_sin", [P, NT, 16], F32)])
        f_hi, f_lo, gate_t, gate_s, hid = region(ot_start, [
            ("f_hi", [P, HALF, T], F32R), ("f_lo", [P, HALF, T], F32R),
            ("gate_t", [P, T], F32), ("gate_s", [P, T], F32), ("hid", [P, T], F32)])
        sq1, ss1, h_fin, g_fin = region(scratch + 24 * 1024, [
            ("sq1", [P, 2, T], F32), ("ss1", [P, T], F32),
            ("h_fin", [P, 2, T], F32), ("g_fin", [P, KD, P], F32)])
        (out_n,) = region(x_start, [("out_n", [P, NT, D], F32)])
        bq_hi, bq_lo, bk_hi, bk_lo = region(x_start, [
            ("bq_hi", [P, HG, T], F32R), ("bq_lo", [P, HG, T], F32R),
            ("bk_hi", [P, HG, T], F32R), ("bk_lo", [P, HG, T], F32R)])
        cq_hi, cq_lo, ckv_hi, ckv_lo, q_n, bv_hi, bv_lo, s_b, bpt_hi, bpt_lo, rope_a = region(scratch, [
            ("cq_hi", [P, QL // P, T], F32R), ("cq_lo", [P, QL // P, T], F32R),
            ("ckv_hi", [P, KVL // P, T], F32R), ("ckv_lo", [P, KVL // P, T], F32R),
            ("q_n", [P, NT, HG * QK], F32),
            ("bv_hi", [P, NT, 2, 3 * HD], F32R), ("bv_lo", [P, NT, 2, 3 * HD], F32R),
            ("s_b", [P, 2, HG, T], F32),
            ("bpt_hi", [P, 2, NT, T], F32R), ("bpt_lo", [P, 2, NT, T], F32R),
            ("rope_a", [P, T], F32)])
        rope_b = rs_t
        lat, lat_sq = region(scratch + 54 * 1024, [("lat", [P, NT, B_IN], F32), ("lat_sq", [P, QL], F32)])

        banks = [ctx.enter_context(nc.psum_tensor(f"bank{i}", [P, T], F32)) for i in range(8)]

        def sem(name):
            return ctx.enter_context(nc.semaphore(name))

        x_in = [sem(f"x_in{i}") for i in range(NT)]
        gain_in = sem("gain_in")
        small_in = sem("small_in")
        pos_in = sem("pos_in")
        gfin_in = sem("gfin_in")
        w_in = [sem(f"w_in{i}") for i in range(2)]
        w_hi_ready = sem("w_hi_ready")
        w_ready = sem("w_ready")
        w_used = sem("w_used")
        pool_consts = sem("pool_consts")
        vec_consts = sem("vec_consts")
        near_p = sem("near_p")
        near_v = sem("near_v")
        tab_v = sem("tab_v")
        tab_a = sem("tab_a")
        proj_done = sem("proj_done")
        proj_free = sem("proj_free")
        pt_done = sem("pt_done")
        pt_hi_ready = sem("pt_hi_ready")
        pt_free = sem("pt_free")
        s_done = sem("s_done")
        s_free = sem("s_free")
        o_done = sem("o_done")
        o_hi_ready = sem("o_hi_ready")
        o_free = sem("o_free")
        x_hi_ready = sem("x_hi_ready")
        x_ready = sem("x_ready")
        sq_ready = sem("sq_ready")
        ss_ready = sem("ss_ready")
        st_done = sem("st_done")
        ms_ready = sem("ms_ready")
        rms_n = sem("rms_n")
        rs_step = sem("rs_step")
        rs_n_ready = sem("rs_n_ready")
        rs_spread = sem("rs_spread")
        k_dup_ready = sem("k_dup_ready")
        q_hi_ready = sem("q_hi_ready")
        q_ready = sem("q_ready")
        kp_hi_ready = sem("kp_hi_ready")
        kp_ready = sem("kp_ready")
        v_hi_ready = sem("v_hi_ready")
        v_ready = sem("v_ready")
        par_ready = sem("par_ready")
        sinkcol_ready = sem("sinkcol_ready")
        bias_ready = sem("bias_ready")
        bias_odd_ready = sem("bias_odd_ready")
        max_ready = sem("max_ready")
        exp_ready = sem("exp_ready")
        rsum_ready = sem("rsum_ready")
        p_ready = sem("p_ready")
        lat_ready = sem("lat_ready")
        lsq_ready = sem("lsq_ready")
        lrms_ready = sem("lrms_ready")
        lrs_ready = sem("lrs_ready")
        latn_ready = sem("latn_ready")
        rope_v = sem("rope_v")
        krope_hi = sem("krope_hi")
        krope_ready = sem("krope_ready")
        silu_ready = sem("silu_ready")
        silu_rs_ready = sem("silu_rs_ready")
        f_hi_ready = sem("f_hi_ready")
        f_ready = sem("f_ready")
        out_ready = [sem("out_ready_v"), sem("out_ready_a")]
        out_sent = sem("out_sent")

        def wait(eng, s, value):
            eng.wait_ge(s, value)
            if not isinstance(value, int):
                eng.nop(nofuse=True)

        def wait_on(eng, s, value):
            eng.wait_ge(s, value)

        def f(ap):
            return ap.bitcast(F32)

        def raw_part(s, cols, kv):
            w = w_raw[s][:, 0:cols]
            return w if not kv else w.rearrange("p (b c d) -> p b c d", c=2, d=HD)

        def split_part(w, s, cols, kv):
            w = w[s][:, 0:cols]
            return w if not kv else w.rearrange("p (c b d) -> p b c d", c=2, d=HD)

        class Norm:

            def __init__(self, number, gain, block_sem, block_base, tiles, sums, o_index):
                self.number, self.gain, self.base = number, gain, KD * number
                self.block_sem, self.block_base = block_sem, block_base
                self.sq, self.ss = tiles
                self.sums, self.o_index = sums, o_index

        later = (sq1, ss1)
        U_DOWN0 = U_FFN0 + C_HALF + 2 * HALF
        U_DOWN1 = U_FFN1 + C_HALF + 2 * HALF
        norms = [
            Norm(0, 0, pt_free, 0, (sq0, ss0), banks[4][:, 0:8], O_NORM0),
            Norm(1, 2, proj_free, U_WOA, later, banks[4][:, 0:8], O_NORM1),
            Norm(2, 1, proj_free, U_DOWN0, later, banks[7][:, B_IN - QL:B_IN - QL + 8], None),
            Norm(3, 3, proj_free, U_WOB, later, banks[4][:, 0:8], O_NORM3),
            Norm(4, None, proj_free, U_DOWN1, later, banks[5][:, 0:8], None)]

        qkv_v = a_w_qkv[0].rearrange("(k p) (j n) -> p k j n", p=P, n=P)
        v_v = a_w_qkv[0].rearrange("(k p) n -> p k n", p=P)
        wo_v = [w[0].rearrange("(k p) (m n) -> p k m n", p=P, n=P) for w in (a_w_o, b_w_o)]
        gu_v = [ffn_w_gu[i].rearrange("(k p) (j n) -> p k j n", p=P, n=P) for i in range(2)]
        down_v = [ffn_w_down[i].rearrange("(k p) (m n) -> p k m n", p=P, n=P) for i in range(2)]
        in_v = b_w_in[0].rearrange("(k p) n -> p k n", p=P)
        uq_v = b_w_uq[0].rearrange("(k p) (g n) -> p k g n", p=P, n=HG * QK)
        ukv_v = b_w_ukv[0].rearrange("(k p) (g n) -> p k g n", p=P, n=HG * 2 * HD)

        block = ctx.enter_context(nc.Block())

        @block.sync
        def _(sp):
            def load(c2, s, src, cols):
                if not (isinstance(c2, int) and c2 == 0):
                    wait(sp, w_ready, 2 * c2 + s - 1)
                dst = w_raw[s][:, 0:src.shape[1] * cols].rearrange("p (k n) -> p k n", n=cols)
                sp.dma_start(dst, src).then_inc(w_in[s], 16)

            xv = x[0].rearrange("(t p) d -> p t d", p=P)
            for t in range(NT):
                sp.dma_start(x_n[:, t, :], xv[:, t, :]).then_inc(x_in[t], 16)
            def load_gain(i, g, landed):
                with nc.allow_non_contiguous_dma(reason="gains by partition"):
                    sp.dma_start(gains[:, i, :, 0], g.rearrange("(k p) -> p k", p=P)).then_inc(landed, 16)

            load_gain(0, norm_mix[0], gain_in)
            load(0, 0, qkv_v[:, :, 8, :], P)
            load(0, 1, qkv_v[:, :, 9, :], P)
            for i, g in enumerate((norm_mix[1], norm_ffn[0], norm_ffn[1])):
                load_gain(i + 1, g, small_in)
            with nc.allow_non_contiguous_dma(reason="gains by partition"):
                sp.dma_start(g_q[:], b_g_q[0].rearrange("(k p) -> p k", p=P)).then_inc(small_in, 16)
                sp.dma_start(g_kv[:], b_g_kv[0].rearrange("(k p) -> p k", p=P)).then_inc(small_in, 16)
                sp.dma_start(pos_q[:], positions[0].rearrange("(t p) -> p t", p=P)).then_inc(small_in, 16)
            sp.dma_start(sink_in[:], a_sink[0].partition_broadcast(P)).then_inc(small_in, 16)
            sp.dma_start(pos_k[:], positions[0].partition_broadcast(P)).then_inc(small_in, 16)

            for s in range(2):
                load(C_V // 2, s, v_v[:, 4 * s:4 * s + 4, (HEADS + GROUPS) * HD:], GROUPS * HD)
            with sp.Fori(0, GROUPS) as g:
                for s in range(2):
                    load(C_Q // 2 + g, s, qkv_v[:, :, 2 * g + s, :], P)

            def load_wo(layer, c0):
                with sp.Fori(0, KD // 2) as i:
                    for s in range(2):
                        load(c0 // 2 + i, s, wo_v[layer][:, :, 2 * i + s, :], P)

            def load_ffn(layer, c0):
                for half in range(2):
                    c2 = c0 // 2 + half * C_HALF // 2
                    with sp.Fori(0, HALF) as j:
                        load(c2 + j, 0, gu_v[layer][:, :, half * HALF + j, :], P)
                        load(c2 + j, 1, gu_v[layer][:, :, FB + half * HALF + j, :], P)
                    with sp.Fori(0, KD // 2) as i:
                        for s in range(2):
                            load(c2 + HALF + i, s,
                                 down_v[layer][:, half * HALF:(half + 1) * HALF, 2 * i + s, :], P)

            load_wo(0, C_WOA)
            sp.wait_ge(w_used, C_WOA + 1)
            with nc.allow_non_contiguous_dma(reason="positions by partition"):
                sp.dma_start(pos_r[:], positions[0].rearrange("(t p) -> p t", p=P)).then_inc(pos_in, 16)
            load_ffn(0, C_FFN0)
            for i in range(4):
                load(C_LAT // 2 + i // 2, i % 2, in_v[:, 2 * i:2 * i + 2, :], B_IN)
            with sp.Fori(0, GROUPS) as g:
                load(C_B // 2 + g, 0, uq_v[:, :, g, :], HG * QK)
                load(C_B // 2 + g, 1, ukv_v[:, :, g, :], HG * 2 * HD)
            load_wo(1, C_WOB)
            sp.wait_ge(w_used, C_WOB + 1)
            sp.dma_start(g_fin[:], final_norm.rearrange("(k n) -> k n", n=P).partition_broadcast(P)) \
                .then_inc(gfin_in, 16)
            load_ffn(1, C_FFN1)
            ov = out[0].rearrange("(t p) d -> p t d", p=P)
            for t in range(NT):
                sp.wait_ge(out_ready[t % 2], t // 2 + 1)
                sp.dma_start(ov[:, t, :], out_n[:, t, :]).then_inc(out_sent, 16)
            sp.wait_ge(out_sent, 16 * NT)

        @block.gpsimd
        def _(pool):
            def w_split_hi(c2, s, cols, kv=False):
                wait(pool, w_in[s], 16 * c2 + 16)
                if not (isinstance(c2, int) and c2 == 0):
                    wait(pool, w_used, 2 * c2 + s - 1)
                pool.tensor_scalar(split_part(w_hi, s, cols, kv), raw_part(s, cols, kv), 1.0, 1.0, ALU.mult, ALU.mult) \
                    .then_inc(w_hi_ready, 1)

            def sum_squares(n, m, b, first=False):
                wait(pool, sq_ready, n.base + m + 1)
                if first:
                    if n.number:
                        pool.wait_ge(st_done, n.number)
                    pool.tensor_scalar(n.ss[:], n.sq[:, b, :], 1.0, 1.0, ALU.mult, ALU.mult).then_inc(ss_ready, 1)
                else:
                    wait(pool, ss_ready, n.base + m)
                    pool.tensor_tensor(n.ss[:], n.ss[:], n.sq[:, b, :], ALU.add).then_inc(ss_ready, 1)

            pool.memset(ident[:], 0.0).then_inc(pool_consts, 1)
            pool.wait_ge(pool_consts, 1)
            pool.affine_select(out=ident[:], in_=ident[:], compare_op=ALU.not_equal, fill=1.0, base=0,
                               pattern=[[-1, P]], channel_multiplier=1).then_inc(pool_consts, 1)
            for i in range(HEADS):
                slope = float(np.float32(2.0 ** (-8.0 * (i + 1) / HEADS)))
                pool.memset(par_all[:, i // HG, i % HG:i % HG + 1], slope).then_inc(pool_consts, 1)
            w_split_hi(0, 0, W_COLS)
            sum_squares(norms[0], 0, 0, first=True)
            w_split_hi(0, 1, W_COLS)
            sum_squares(norms[0], 1, 1)
            with pool.Fori(1, KD // 2) as i:
                for s in range(2):
                    sum_squares(norms[0], 2 * i + s, s)
            pool.wait_ge(small_in, 8 * 16)
            for qb in range(NT):
                k0, nk = A_KB[qb]
                pool.tensor_tensor(dist_i[:, qb, 0:nk * P], pos_k[:, k0 * P:(k0 + nk) * P],
                                   pos_q[:, qb:qb + 1].to_broadcast([P, nk * P]), ALU.subtract).then_inc(near_p, 1)
            for s in range(2):
                w_split_hi(C_V // 2, s, 4 * GROUPS * HD)
            for qb in range(NT):
                k0, nk = A_KB[qb]
                gap = (k0 - qb) * P
                view = near[:, qb, 0:nk * P]
                pool.wait_ge(near_v, 2 * qb + 2)
                pool.affine_select(out=view, in_=view, compare_op=ALU.is_ge, fill=MASKED, base=WINDOW - gap,
                                   pattern=[[-1, nk * P]], channel_multiplier=1).then_inc(near_p, 1)
                pool.wait_ge(near_p, NT + 2 * qb + 1)
                pool.affine_select(out=view, in_=view, compare_op=ALU.is_ge, fill=MASKED, base=WINDOW + gap,
                                   pattern=[[1, nk * P]], channel_multiplier=-1).then_inc(near_p, 1)
            for s in range(2):
                w_split_hi(C_Q // 2, s, W_COLS)

            pool.wait_ge(near_p, 3 * NT)
            pool.wait_ge(pool_consts, 2 + HEADS)
            pool.wait_ge(vec_consts, 7)

            def a_group(g):
                wait(pool, s_free, S_A + 16 * g)
                pool.tensor_copy(par[:], par_all[:, g, :]).then_inc(par_ready, 1)
                wait(pool, par_ready, g + 1)
                wait(pool, pt_done, T_A + A_TG * g)
                for b in range(2):
                    pool.tensor_copy(s_a[:, b, :, 0:1], par[:, HG:2 * HG].unsqueeze(2)).then_inc(sinkcol_ready, 1)

                def make_bias(u):
                    nk = A_KB[u // HG][1]
                    if u >= 2:
                        wait(pool, s_free, S_A + 16 * g + u - 1)
                    pool.tensor_scalar(bias[:, u % 2, 0:nk * P], near[:, u // HG, 0:nk * P],
                                       par[:, u % HG:u % HG + 1], 1.0, ALU.mult, ALU.mult).then_inc(bias_ready, 1)

                make_bias(0)
                for u in range(16):
                    n, hd = u // HG, u % HG
                    nk = A_KB[n][1]
                    if u + 2 < 16 and u % 2 == 0:
                        make_bias(u + 2)
                    wait(pool, rsum_ready, 16 * g + u + 1)
                    view = s_a[:, n % 2, hd, 1:1 + nk * P]
                    pool.tensor_scalar(view, view, stat[:, 2, u % 8:u % 8 + 1], 1.0, ALU.mult, ALU.mult) \
                        .then_inc(p_ready, 1)
                    if u == 3:
                        w_split_hi(C_Q // 2 + 1 + g, 0, W_COLS)
                    if u == 7:
                        w_split_hi(C_Q // 2 + 1 + g, 1, W_COLS)

            with pool.Fori(0, GROUPS) as g:
                a_group(g)

            def wo_phase(n, c0):
                for s in range(2):
                    w_split_hi(c0 // 2 + 1, s, W_COLS)
                    sum_squares(n, s, s, first=s == 0)
                with pool.Fori(1, KD // 2) as i:
                    for s in range(2):
                        w_split_hi(c0 // 2 + 1 + i, s, W_COLS)
                        sum_squares(n, 2 * i + s, s)

            def ffn_half(layer, half, n, next_cols):
                c2 = ((C_FFN0, C_FFN1)[layer] + half * C_HALF) // 2
                j0 = (2 * layer + half) * HALF

                def hidden(j, cols, first=False):
                    w_split_hi(c2 + j + 1, 0, cols)
                    if first:
                        w_split_hi(c2 + j + 1, 1, cols)
                    wait(pool, silu_ready, j0 + j + 1)
                    pool.tensor_tensor(gate_s[:], gate_s[:], rs_t[:], ALU.mult).then_inc(silu_rs_ready, 1)
                    if not first:
                        w_split_hi(c2 + j + 1, 1, cols)

                hidden(0, W_COLS, first=half == 0)
                with pool.Fori(1, HALF - 1) as j:
                    hidden(j, W_COLS)
                hidden(HALF - 1, W_DOWN)

                def pair(i, cols, first=False):
                    for s in range(2):
                        if cols:
                            w_split_hi(c2 + HALF + 1 + i, s, cols)
                        if n is not None:
                            sum_squares(n, 2 * i + s, s, first=first and s == 0)

                pair(0, W_DOWN, first=True)
                with pool.Fori(1, KD // 2 - 1) as i:
                    pair(i, W_DOWN)
                pair(KD // 2 - 1, next_cols)

            wo_phase(norms[1], C_WOA)
            ffn_half(0, 0, None, W_COLS)
            pool.wait_ge(pos_in, 16)
            for i in range(ROPE // 2):
                pool.memset(inv_f[:, i:i + 1], float(INV_FREQ[i])).then_inc(pool_consts, 1)
            ffn_half(0, 1, norms[2], W_LAT)

            w_split_hi(C_LAT // 2 + 1, 0, W_LAT)
            w_split_hi(C_LAT // 2 + 1, 1, W_LAT)
            w_split_hi(C_B // 2, 0, W_UQ)
            w_split_hi(C_B // 2, 1, W_UKV, kv=True)
            pool.wait_ge(lrs_ready, 1)
            for t in range(NT):
                view = lat[:, t, QL:QL + KVL]
                pool.tensor_scalar(view, view, lat_stat[:, 2, NT + t:NT + t + 1], 1.0, ALU.mult, ALU.mult) \
                    .then_inc(latn_ready, 1)

            def b_group(g, cols0, cols1):
                for u in range(16):
                    wait(pool, rsum_ready, 16 * (GROUPS + g) + u + 1)
                    view = s_b[:, u // 4 % 2, u % 4, :]
                    pool.tensor_scalar(view, view, stat[:, 2, u % 8:u % 8 + 1], 1.0, ALU.mult, ALU.mult) \
                        .then_inc(p_ready, 1)
                    if u == 3:
                        w_split_hi(C_B // 2 + 1 + g, 0, cols0)
                    if u == 7:
                        w_split_hi(C_B // 2 + 1 + g, 1, cols1, kv=cols0 == W_UQ)

            with pool.Fori(0, GROUPS - 1) as g:
                b_group(g, W_UQ, W_UKV)
            b_group(GROUPS - 1, W_COLS, W_COLS)

            wo_phase(norms[3], C_WOB)
            ffn_half(1, 0, None, W_COLS)
            ffn_half(1, 1, norms[4], 0)

        @block.scalar
        def _(act):
            def split_x(n, m, b, src=None):
                src = h[:, m, :] if src is None else src
                wait(act, n.block_sem, n.block_base + m + 1)
                if n.gain is not None:
                    act.activation(x_hi[:, m, :], src, ACT.Copy, scale=gains[:, n.gain, m, :]) \
                        .then_inc(x_hi_ready, 1)
                if n.number or not isinstance(m, int):
                    wait(act, ss_ready, n.base + m - 1)
                act.activation(n.sq[:, b, :], src, ACT.Square).then_inc(sq_ready, 1)

            def rms(n):
                act.wait_ge(ms_ready, n.number + 1)
                act.activation(ms_n[:, 1, :], ms_n[:, 0, :], ACT.Sqrt).then_inc(rms_n, 1)

            act.wait_ge(gain_in, 16)
            for s in range(2):
                split_x(norms[0], s, s)
            with act.Fori(1, KD // 2) as i:
                for s in range(2):
                    split_x(norms[0], 2 * i + s, s)
            rms(norms[0])
            act.wait_ge(w_used, C_V + 2)
            act.wait_ge(rs_n_ready, 1)
            for t in range(NT):
                act.activation(v_all[:, t, :], banks[t][:, 0:GROUPS * HD], ACT.Copy, scale=rs_n[:, 2 * t:2 * t + 1]) \
                    .then_inc(s_free, 16 // NT)

            def a_k_hi(g, first=False):
                if not first:
                    wait(act, s_done, 16 * g)
                for b in range(2):
                    act.activation(kp_hi[b * HD:(b + 1) * HD, b, :], k_dup[b * HD:(b + 1) * HD, g, :], ACT.Copy) \
                        .then_inc(kp_hi_ready, 1)

            v_by_group = v_all[:].rearrange("p t (g d) -> p t g d", g=GROUPS)

            def a_v_hi(g, first=False):
                if not first:
                    wait(act, o_done, 4 * g)
                act.activation(av_hi[:, :, HD:2 * HD], v_by_group[:, :, g, :], ACT.Copy).then_inc(v_hi_ready, 1)

            def a_q_hi(g, i, first=False):
                if not first:
                    wait(act, s_done, 16 * g)
                wait(act, proj_free, U_Q + 2 * g + i + 1)
                act.activation(aq_hi[:, i, :], q_tmp[:], ACT.Copy).then_inc(q_hi_ready, 1)

            act.wait_ge(k_dup_ready, 6)
            act.wait_ge(proj_free, U_Q)
            a_k_hi(0, first=True)
            a_q_hi(0, 0, first=True)
            a_q_hi(0, 1, first=True)
            act.wait_ge(s_free, S_A)
            a_v_hi(0, first=True)
            def a_group(g, last):
                def expo(u):
                    n, hd = u // HG, u % HG
                    if u == 0:
                        wait(act, sinkcol_ready, 2 * g + 2)
                    (wait if u else wait_on)(act, s_free, S_A + 16 * g + u + 1)
                    view = s_a[:, n % 2, hd, 0:1 + A_KB[n][1] * P]
                    act.activation(view, view, ACT.Exp, scale=-1.0, bias=stat[:, 0, u % 8:u % 8 + 1],
                                   accum_out=stat[:, 1, u % 8:u % 8 + 1]).then_inc(exp_ready, 1)

                def odd_bias(u):
                    nk = A_KB[u // HG][1]
                    if u == 1:
                        wait(act, par_ready, g + 1)
                    else:
                        wait(act, s_free, S_A + 16 * g + u - 1)
                    act.activation(bias[:, 1, 0:nk * P], near[:, u // HG, 0:nk * P], ACT.Copy,
                                   scale=par[:, u % HG:u % HG + 1]).then_inc(bias_odd_ready, 1)

                def pt_hi(n, i):
                    unit = T_A + A_T0[n] + i
                    wait(act, pt_done, unit + A_TG * g + 1)
                    act.activation(apt_hi[:, n % 2, i, :], banks[3 + unit % 2][:], ACT.Copy).then_inc(pt_hi_ready, 1)

                def o_hi(n):
                    wait(act, o_done, 4 * g + n + 1)
                    act.activation(ot_hi_q[:, g, :, n, :], banks[5][:, 0:2 * P].rearrange("p (a q) -> p a q", a=2),
                                   ACT.Copy).then_inc(o_hi_ready, 1)

                odd_bias(1)
                expo(0)
                expo(1)
                odd_bias(3)
                expo(2)
                expo(3)
                odd_bias(5)
                for n in range(NT):
                    if n < 3:
                        expo(4 * n + 4)
                        expo(4 * n + 5)
                        odd_bias(4 * n + 7)
                        expo(4 * n + 6)
                        pt_hi(n, 0)
                        expo(4 * n + 7)
                        if n < 2:
                            odd_bias(4 * n + 9)
                        pt_hi(n, 1)
                        if n:
                            o_hi(n - 1)
                        if A_KB[n][1] > 2:
                            pt_hi(n, 2)
                    else:
                        if not last:
                            a_q_hi(g + 1, 0)
                            a_k_hi(g + 1)
                        pt_hi(n, 0)
                        o_hi(n - 1)
                        pt_hi(n, 1)
                if not last:
                    a_q_hi(g + 1, 1)
                o_hi(3)
                if not last:
                    a_v_hi(g + 1)

            ot_hi_q = ot_hi[:].rearrange("p (g a) (n q) -> p g a n q", a=2, n=NT)
            with act.Fori(0, GROUPS - 1) as g:
                a_group(g, False)
            a_group(GROUPS - 1, True)

            def wo_phase(n):
                with act.Fori(0, KD // 2) as i:
                    for s in range(2):
                        split_x(n, 2 * i + s, s)
                rms(n)

            def ffn_half(layer, half, n):
                u0 = (U_FFN0, U_FFN1)[layer] + half * C_HALF
                j0 = (2 * layer + half) * HALF
                with act.Fori(0, HALF) as j:
                    wait(act, proj_free, u0 + 2 * j + 1)
                    act.activation(gate_s[:], gate_t[:], ACT.Silu).then_inc(silu_ready, 1)
                    wait(act, proj_free, u0 + 2 * j + 2)
                    act.activation(f_hi[:, j, :], hid[:], ACT.Copy).then_inc(f_hi_ready, 1)
                if n is not None:
                    with act.Fori(0, KD // 2) as i:
                        for s in range(2):
                            split_x(n, 2 * i + s, s, h_fin[:, s, :] if n.gain is None else None)
                    rms(n)

            wo_phase(norms[1])
            ffn_half(0, 0, None)
            act.wait_ge(tab_v, TAB_STEPS)
            act.activation(half_sin[:], ang[:], ACT.Sin, scale=0.5).then_inc(tab_a, 1)
            act.activation(sin_n[:, :, 16:32], ang[:], ACT.Sin).then_inc(tab_a, 1)
            ffn_half(0, 1, norms[2])

            act.wait_ge(rs_n_ready, 3)
            for t in range(NT):
                act.activation(lat[:, t, 0:QL], banks[2 * t][:, 0:QL], ACT.Copy, scale=rs_n[:, 2 * t:2 * t + 1]) \
                    .then_inc(lat_ready, 1)
            act.wait_ge(lat_ready, 2 * NT)
            for i in range(2 * NT):
                if i:
                    act.wait_ge(lsq_ready, i)
                at, width = ((0, QL), (QL, KVL))[i // NT]
                act.activation(lat_sq[:, 0:width], lat[:, i % NT, at:at + width], ACT.Square,
                               accum_out=lat_stat[:, 0, i:i + 1]).then_inc(lsq_ready, 1)
            act.wait_ge(lsq_ready, 2 * NT)
            for i, width in enumerate((QL, KVL)):
                act.activation(lat_stat[:, 1, i * NT:(i + 1) * NT], lat_stat[:, 0, i * NT:(i + 1) * NT], ACT.Sqrt,
                               scale=1.0 / width, bias=eps[:, 0:1]).then_inc(lrms_ready, 1)

            def b_pt_hi(unit, base, dst, src_rows=P, scale=1.0):
                wait(act, pt_done, unit + base + 1)
                act.activation(dst, banks[3 + unit % 2][0:src_rows, :], ACT.Copy, scale=scale).then_inc(pt_hi_ready, 1)

            for b in range(QL // P):
                b_pt_hi(T_BPRE + b, 0, cq_hi[:, b, :], scale=g_q[:, b:b + 1])
            for b in range(KVL // P):
                b_pt_hi(T_BPRE + 3 + b, 0, ckv_hi[:, b, :], scale=g_kv[:, b:b + 1])
            act.wait_ge(pt_free, T_BPRE + 6)
            for hd in range(HG):
                act.activation(bk_hi[NOPE:QK, hd, :], rope_a[NOPE:QK, :], ACT.Copy) \
                    .then_inc(krope_hi if hd < HG - 1 else pt_hi_ready, 1)

            def b_q_out(g):
                if not isinstance(g, int):
                    wait(act, pt_done, T_B + B_TG * (g - 1))
                elif g:
                    act.wait_ge(pt_done, T_B + B_TG * (g - 1))
                for t in range(NT):
                    wait(act, proj_done, U_BG * g + t + 1)
                    act.activation(q_n[:, t, :], banks[6 + t % 2][:, 0:HG * QK], ACT.Copy, scale=QK ** -0.5) \
                        .then_inc(proj_free, 1)

            def b_k_hi(g, i):
                wait(act, proj_done, U_BG * g + 4 + i + 1)
                for b in range(2):
                    act.activation(bk_hi[0:NOPE, 2 * i + b, :], banks[6 + i][b * HD:(b + 1) * HD, :], ACT.Copy) \
                        .then_inc(kp_hi_ready, 1)

            def b_q_hi(g, base):
                for hd in range(HG):
                    wait(act, pt_done, base + hd + 1)
                    act.activation(bq_hi[0:QK, hd, :], banks[3 + hd % 2][0:QK, :], ACT.Copy).then_inc(pt_hi_ready, 1)

            bv_hi_v = bv_hi[:].rearrange("p t a (s d) -> p (t a) s d", d=HD)

            def b_v_hi(g, i):
                wait(act, o_done, 4 * GROUPS + 2 * g)
                wait(act, proj_done, U_BG * g + 6 + i + 1)
                act.activation(bv_hi_v[:, 4 * i:4 * i + 4, ::2, :],
                               banks[6 + i][:].rearrange("p (t s d) -> p t s d", t=4, s=2), ACT.Copy) \
                    .then_inc(v_hi_ready, 1)

            b_q_out(0)
            b_k_hi(0, 0)
            b_k_hi(0, 1)
            b_q_hi(0, T_BPRE + 6)
            act.wait_ge(vec_consts, 9)

            def b_group(g, last):
                def expo(u):
                    n = u // 4
                    if u >= 8:
                        wait(act, pt_done, T_B + B_TG * g + 4 * (n - 1))
                    elif isinstance(g, int) and g == 0:
                        pass
                    else:
                        wait(act, pt_done, T_B + B_TG * g)
                    (wait if u else wait_on)(act, max_ready, 16 * g + u + 1)
                    act.activation(s_b[:, n % 2, u % 4, :], banks[u % 3][:], ACT.Exp, bias=stat[:, 0, u % 8:u % 8 + 1],
                                   accum_out=stat[:, 1, u % 8:u % 8 + 1]).then_inc(exp_ready, 1)

                def pt_hi(n, i):
                    wait(act, pt_done, T_B + B_TG * g + 4 * n + i + 1)
                    act.activation(bpt_hi[:, n % 2, i, :], banks[3 + i % 2][:], ACT.Copy).then_inc(pt_hi_ready, 1)

                def o_hi(pair):
                    wait(act, o_done, 4 * GROUPS + 2 * g + pair + 1)
                    act.activation(ot_hi[:, 2 * g + pair, :], banks[5][:], ACT.Copy).then_inc(o_hi_ready, 1)

                expo(0)
                expo(1)
                expo(2)
                expo(3)
                for n in range(HG):
                    if n < 3:
                        expo(4 * n + 4)
                        expo(4 * n + 5)
                        expo(4 * n + 6)
                        pt_hi(n, 0)
                        expo(4 * n + 7)
                        for i in range(1, 4):
                            pt_hi(n, i)
                            if n == 0 and i < 3:
                                b_v_hi(g, i - 1)
                        if n == 2:
                            o_hi(0)
                            if not last:
                                b_q_out(g + 1)
                    else:
                        for i in range(4):
                            pt_hi(n, i)
                            if i % 2 == 0 and not last:
                                b_k_hi(g + 1, i // 2)
                        if not last:
                            b_q_hi(g + 1, T_B + B_TG * g + 16)
                        o_hi(1)

            with act.Fori(0, GROUPS - 1) as g:
                b_group(g, False)
            b_group(GROUPS - 1, True)

            wo_phase(norms[3])
            ffn_half(1, 0, None)
            ffn_half(1, 1, norms[4])
            act.wait_ge(rs_n_ready, 5)
            act.wait_ge(pt_free, T_FIN + KD)
            for t in (1, 3):
                act.activation(out_n[:, t, :], out_n[:, t, :], ACT.Copy, scale=rs_n[:, 2 * t:2 * t + 1]) \
                    .then_inc(out_ready[1], 1)

        @block.tensor
        def _(pe):
            def product(o, lh, ll, rh, rl, start, stop):
                pe.matmul(o, ll, rh, start=start, stop=False)
                pe.matmul(o, lh, rl, start=False, stop=False)
                return pe.matmul(o, lh, rh, start=False, stop=stop)

            def w_block(s, cols, k):
                return w_hi[s][:, k * cols:(k + 1) * cols], w_lo[s][:, k * cols:(k + 1) * cols]

            def project(c2, s, unit, unit_base, src_hi, src_lo, blocks=KD, ready=None):
                pe.wait_ge(w_ready, 2 * c2 + s + 1)
                if not (isinstance(unit_base, int) and unit + unit_base < 2):
                    pe.wait_ge(proj_free, unit_base + unit - 1)
                for k in range(blocks):
                    if ready is not None:
                        pe.wait_ge(*ready(k))
                    wh, wl = w_block(s, P, k)
                    last = product(banks[6 + unit % 2][:], wh, wl, src_hi[:, k, :], src_lo[:, k, :],
                                   k == 0, k == blocks - 1)
                last.then_inc(w_used, 1)

            def sum_partitions(n):
                pe.wait_ge(ss_ready, n.base + KD)
                for t in range(NT):
                    last = pe.matmul(n.sums[:, 2 * t:2 * t + 2], n.ss[:, t * P:(t + 1) * P], ones[:],
                                     start=True, stop=True)
                last.then_inc(st_done, 1)

            def spread(n):
                pe.wait_ge(rs_n_ready, n.number + 1)
                if n.o_index:
                    pe.wait_ge(o_free, n.o_index)
                for t in range(NT):
                    last = pe.transpose(banks[5][:, t * P:(t + 1) * P],
                                        rs_n[:, 2 * t:2 * t + 1].to_broadcast([P, P]), ident[:])
                last.then_inc(rs_spread, 1)

            pe.wait_ge(pool_consts, 2)

            def k_block(k):
                for s in range(2):
                    if k == 0:
                        pe.wait_ge(w_ready, s + 1)
                    pe.wait_ge(x_ready, k + 1)
                    wh, wl = w_block(s, P, k)
                    last = product(banks[6 + s][:], wh, wl, x_hi[:, k, :], x_lo[:, k, :], k == 0, k == KD - 1)
                    if k == KD - 1:
                        last.then_inc(w_used, 1)

            for m in range(KD):
                if m >= 2:
                    pe.wait_ge(pt_free, m - 1)
                for t in range(NT):
                    if m == 0:
                        pe.wait_ge(x_in[t], 16)
                    last = pe.transpose(banks[3 + m % 2][:, t * P:(t + 1) * P], x_n[:, t, m * P:(m + 1) * P], ident[:])
                last.then_inc(pt_done, 1)
                if m >= 2:
                    k_block(m - 2)
            k_block(KD - 2)
            k_block(KD - 1)
            pe.wait_ge(vec_consts, 6)

            pe.wait_ge(pt_free, KD)
            for s in range(2):
                pe.wait_ge(w_ready, C_V + s + 1)
                for t in range(NT):
                    if s == 0 and t == 2:
                        sum_partitions(norms[0])
                    if s == 1 and t == 1:
                        spread(norms[0])
                    for k in range(4):
                        wh, wl = w_block(s, GROUPS * HD, k)
                        xk = (4 * s + k, slice(t * P, (t + 1) * P))
                        last = product(banks[t][:, 0:GROUPS * HD], x_hi[:, xk[0], xk[1]], x_lo[:, xk[0], xk[1]],
                                       wh, wl, s == 0 and k == 0, s == 1 and k == 3)
                last.then_inc(w_used, 1)

            def a_q(g, i):
                project(C_Q // 2 + g, i, i, U_Q + 2 * g, x_hi, x_lo)

            a_q(0, 0)
            a_q(0, 1)

            def a_group(g, last):
                def scores(u):
                    n, hd = u // HG, u % HG
                    k0, nk = A_KB[n]
                    before = 16 * g + (u - 2 if u >= 3 else (0, -2, -1)[u])
                    pe.wait_ge(s_free, S_A + before)
                    q = (slice(None), hd // 2, slice(n * P, (n + 1) * P))
                    k = (slice(None), hd % 2, slice(k0 * P, (k0 + nk) * P))
                    product(banks[u % 3][:, 0:nk * P], aq_hi[q], aq_lo[q], kp_hi[k], kp_lo[k], True, True) \
                        .then_inc(s_done, 1)

                def transposes(n, i):
                    unit = T_A + A_T0[n] + i
                    pe.wait_ge(pt_free, A_TG * g + unit - 1)
                    for j, hd in enumerate((0, 2, 1, 3)):
                        if i == 0:
                            pe.wait_ge(p_ready, 16 * g + 4 * n + (hd + 1 if j != 2 else 3))
                        last_ = pe.transpose(banks[3 + unit % 2][:, j * P:(j + 1) * P],
                                             s_a[:, n % 2, hd, 1 + i * P:1 + (i + 1) * P], ident[:])
                    last_.then_inc(pt_done, 1)

                def values(n):
                    k0, nk = A_KB[n]
                    pe.wait_ge(pt_free, T_A + A_TG * g + A_T0[n] + nk)
                    pe.wait_ge(o_free, O_A + 4 * g + n)
                    if n == 0:
                        pe.wait_ge(v_ready, g + 1)
                    for i in range(nk):
                        for odd in range(2):
                            v = (slice(None), k0 + i, slice(0, P) if odd else slice(HD, HD + P))
                            p = (slice(None), n % 2, i, slice(2 * P * odd, 2 * P * (odd + 1)))
                            last_ = product(banks[5][:, 0:2 * P], av_hi[v], av_lo[v], apt_hi[p], apt_lo[p],
                                            i == 0 and odd == 0, i == nk - 1 and odd == 1)
                    last_.then_inc(o_done, 1)

                pe.wait_ge(kp_ready, 2 * g + 2)
                pe.wait_ge(q_ready, 2 * g + 1)
                scores(0)
                scores(1)
                pe.wait_ge(q_ready, 2 * g + 2)
                scores(2)
                scores(3)
                for n in range(NT):
                    if n < 3:
                        scores(4 * n + 4)
                        scores(4 * n + 5)
                        scores(4 * n + 6)
                        scores(4 * n + 7)
                        transposes(n, 0)
                        transposes(n, 1)
                        if n:
                            values(n - 1)
                        if A_KB[n][1] > 2:
                            transposes(n, 2)
                        if n == 1 and not last:
                            a_q(g + 1, 0)
                    else:
                        transposes(n, 0)
                        values(n - 1)
                        transposes(n, 1)
                if not last:
                    a_q(g + 1, 1)
                values(3)

            with pe.Fori(0, GROUPS - 1) as g:
                a_group(g, False)
            a_group(GROUPS - 1, True)

            def wo_phase(c0, u0, o_count):
                pe.wait_ge(o_free, o_count)
                with pe.Fori(0, KD // 2) as i:
                    for s in range(2):
                        project(c0 // 2 + i, s, s, u0 + 2 * i, ot_hi, ot_lo)

            def ffn_half(layer, half, n, fin=None):
                c2 = ((C_FFN0, C_FFN1)[layer] + half * C_HALF) // 2
                u0 = (U_FFN0, U_FFN1)[layer] + half * C_HALF
                j0 = (2 * layer + half) * HALF
                if n is not None:
                    def part(c, bank, blocks):
                        if blocks[0] == 0:
                            pe.wait_ge(w_ready, 2 * c2 + c + 1)
                            pe.wait_ge(proj_free, u0 if bank >= 6 else u0 - 1)
                        for k in blocks:
                            pe.wait_ge(x_ready, n.base + k + 1)
                            wh, wl = w_block(c % 2, P, k)
                            last = product(banks[bank][:], wh, wl, x_hi[:, k, :], x_lo[:, k, :],
                                           k == 0, k == KD - 1)
                        return last

                    part(0, 0, range(KD - 1))
                    part(1, 1, range(KD - 3))
                    part(0, 0, [KD - 1]).then_inc(w_used, 1)
                    sum_partitions(n)
                    part(1, 1, [KD - 3, KD - 2, KD - 1]).then_inc(w_used, 1)
                    part(2, 6, range(KD // 2))
                    spread(n)
                    part(2, 6, range(KD // 2, KD)).then_inc(w_used, 1)
                    part(3, 7, range(KD)).then_inc(w_used, 1)
                else:
                    for j in range(2):
                        for s in range(2):
                            project(c2 + j, s, s, u0 + 2 * j, x_hi, x_lo)
                with pe.Fori(2, HALF) as j:
                    for s in range(2):
                        project(c2 + j, s, s, u0 + 2 * j, x_hi, x_lo)

                def down(i, s, first=False):
                    project(c2 + HALF + i, s, s, u0 + 2 * HALF + 2 * i, f_hi, f_lo, blocks=HALF,
                            ready=(lambda k: (f_ready, j0 + k + 1)) if first else None)

                def turn(m0, s):
                    pe.wait_ge(proj_free, U_DOWN1 + m0 + s + 1)
                    pe.wait_ge(pt_free, T_FIN + m0 + s - 1)
                    for t in range(NT):
                        last = pe.transpose(banks[3 + s][:, t * P:(t + 1) * P], h_fin[:, s, t * P:(t + 1) * P], ident[:])
                    last.then_inc(pt_done, 1)

                down(0, 0, first=True)
                down(0, 1)
                if fin:
                    turn(0, 0)
                with pe.Fori(1, KD // 2) as i:
                    down(i, 0)
                    if fin:
                        turn(2 * i - 2, 1)
                    down(i, 1)
                    if fin:
                        turn(2 * i, 0)
                if fin:
                    turn(KD - 2, 1)
                    sum_partitions(norms[4])

            wo_phase(C_WOA, U_WOA, O_A + 4 * GROUPS)
            ffn_half(0, 0, norms[1])
            ffn_half(0, 1, None)

            pe.wait_ge(proj_free, U_B)
            for c in range(4):
                pe.wait_ge(w_ready, C_LAT + c + 1)
                for t in range(NT):
                    for kk in range(2):
                        k = 2 * c + kk
                        if t == 0:
                            pe.wait_ge(x_ready, norms[2].base + k + 1)
                        wh, wl = w_block(c % 2, B_IN, kk)
                        xh, xl = x_hi[:, k, t * P:(t + 1) * P], x_lo[:, k, t * P:(t + 1) * P]
                        for half, (a, b) in enumerate(((0, QL), (QL, B_IN))):
                            last = product(banks[2 * t + half][:, 0:b - a], xh, xl, wh[:, a:b], wl[:, a:b],
                                           k == 0, k == KD - 1)
                last.then_inc(w_used, 1)
            sum_partitions(norms[2])
            pe.wait_ge(latn_ready, 2 * NT)
            for b in range(QL // P + KVL // P):
                if b >= 2:
                    pe.wait_ge(pt_free, T_BPRE + b - 1)
                for t in range(NT):
                    last = pe.transpose(banks[3 + b % 2][:, t * P:(t + 1) * P], lat[:, t, b * P:(b + 1) * P], ident[:])
                last.then_inc(pt_done, 1)
            pe.wait_ge(rope_v, 4)
            pe.wait_ge(pt_free, T_BPRE + 4)
            for t in range(NT):
                last = pe.transpose(banks[4][0:ROPE, t * P:(t + 1) * P], lat[:, t, QL + KVL:B_IN], ident[:])
            last.then_inc(pt_done, 1)

            def b_q(g):
                pe.wait_ge(w_ready, C_B + 2 * g + 1)
                for t in range(NT):
                    pe.wait_ge(proj_free, U_B + U_BG * g + t - 1)
                    for k in range(QL // P):
                        wh, wl = w_block(0, HG * QK, k)
                        ch, cl = cq_hi[:, k, t * P:(t + 1) * P], cq_lo[:, k, t * P:(t + 1) * P]
                        last = product(banks[6 + t % 2][:, 0:HG * QK], ch, cl, wh, wl, k == 0, k == QL // P - 1)
                    last.then_inc(proj_done, 1)

            def b_k(g, i):
                if i == 0:
                    pe.wait_ge(w_ready, C_B + 2 * g + 2)
                pe.wait_ge(proj_free, U_B + U_BG * g + 4 + i - 1)
                for k in range(KVL // P):
                    wh, wl = (w[1][:, k * HG * HD + i * P:k * HG * HD + (i + 1) * P] for w in (w_hi, w_lo))
                    o = banks[6 + i][:]
                    first = pe.matmul(o, wl, ckv_hi[:, k, :], start=k == 0, stop=False)
                    if i == 0 and k == 0:
                        first.then_inc(w_used, 1)
                    pe.matmul(o, wh, ckv_lo[:, k, :], start=False, stop=False)
                    last = pe.matmul(o, wh, ckv_hi[:, k, :], start=False, stop=k == KVL // P - 1)
                last.then_inc(proj_done, 1)

            def b_v(g, i):
                pe.wait_ge(proj_free, U_B + U_BG * g + 6 + i - 1)
                for t in (2 * i, 2 * i + 1):
                    o = banks[6 + i][:, t % 2 * HG * HD:(t % 2 + 1) * HG * HD]
                    for k in range(KVL // P):
                        wh, wl = (w[1][:, W_UKV // 2 + k * HG * HD:W_UKV // 2 + (k + 1) * HG * HD]
                                  for w in (w_hi, w_lo))
                        ch, cl = ckv_hi[:, k, t * P:(t + 1) * P], ckv_lo[:, k, t * P:(t + 1) * P]
                        last = product(o, ch, cl, wh, wl, k == 0, k == KVL // P - 1)
                last.then_inc(proj_done, 1)

            def b_turn_q(g, base, hd):
                if hd == 0:
                    pe.wait_ge(rope_v, 8 * g + 12)
                pe.wait_ge(pt_free, base + hd - 1)
                for t in range(NT):
                    last = pe.transpose(banks[3 + hd % 2][0:QK, t * P:(t + 1) * P],
                                        q_n[:, t, hd * QK:(hd + 1) * QK], ident[:])
                last.then_inc(pt_done, 1)

            pe.wait_ge(pt_free, T_BPRE + 5)
            b_q(0)
            b_k(0, 0)
            b_k(0, 1)
            for hd in range(HG):
                b_turn_q(0, T_BPRE + 6, hd)
            pe.wait_ge(krope_ready, HG)

            def b_group(g, last):
                def scores(u):
                    n, qb = u // 4, u % 4
                    before = 16 * g + (u - 2 if u >= 3 else (0, -2, -1)[u])
                    pe.wait_ge(exp_ready, S_B - S_A + before)
                    q = (slice(0, QK), n, slice(qb * P, (qb + 1) * P))
                    k = (slice(0, QK), n, slice(None))
                    product(banks[u % 3][:], bq_hi[q], bq_lo[q], bk_hi[k], bk_lo[k], True, True).then_inc(s_done, 1)

                def transposes(n, i):
                    pe.wait_ge(pt_free, T_B + B_TG * g + 4 * n + i - 1)
                    for qb in range(NT):
                        if i == 0:
                            pe.wait_ge(p_ready, 16 * (GROUPS + g) + 4 * n + qb + 1)
                        last_ = pe.transpose(banks[3 + i % 2][:, qb * P:(qb + 1) * P],
                                             s_b[:, n % 2, qb, i * P:(i + 1) * P], ident[:])
                        if n == 0 and i == 3 and qb == 0:
                            last_.then_inc(w_used, 1)
                    last_.then_inc(pt_done, 1)

                def values(n, i):
                    if i == 0:
                        pe.wait_ge(pt_free, T_B + B_TG * g + 4 * n + 4)
                        if n == 0:
                            pe.wait_ge(proj_free, U_B + U_BG * g + U_BG)
                    if i == 0 and n % 2 == 0:
                        pe.wait_ge(o_free, O_B + 2 * g + n // 2)
                    v = (slice(None), i, n // 2, slice(HD, HD + P) if n % 2 else slice(0, P))
                    p = (slice(None), n % 2, i, slice(None))
                    last_ = product(banks[5][:], bv_hi[v], bv_lo[v], bpt_hi[p], bpt_lo[p],
                                    n % 2 == 0 and i == 0, n % 2 == 1 and i == NT - 1)
                    if n % 2 and i == NT - 1:
                        last_.then_inc(o_done, 1)

                pe.wait_ge(proj_free, U_B + U_BG * g + 6)
                pe.wait_ge(pt_free, T_B + B_TG * g)
                scores(0)
                scores(1)
                scores(2)
                scores(3)
                for n in range(HG):
                    if n < 3:
                        scores(4 * n + 4)
                        scores(4 * n + 5)
                        scores(4 * n + 6)
                        scores(4 * n + 7)
                        for i in range(NT):
                            transposes(n, i)
                            if n:
                                values(n - 1, i)
                            elif i in (1, 2):
                                b_v(g, i - 1)
                        if n == 2 and not last:
                            b_q(g + 1)
                    else:
                        for i in range(NT):
                            transposes(n, i)
                            values(2, i)
                            if i % 2 == 0 and not last:
                                b_k(g + 1, i // 2)
                        for i in range(NT):
                            if not last:
                                b_turn_q(g + 1, T_B + B_TG * g + 16, i)
                            values(3, i)

            with pe.Fori(0, GROUPS - 1) as g:
                b_group(g, False)
            b_group(GROUPS - 1, True)

            wo_phase(C_WOB, U_WOB, O_B + 2 * GROUPS)
            ffn_half(1, 0, norms[3])
            ffn_half(1, 1, None, fin=True)

        @block.vector
        def _(dve):
            def w_split_lo(c2, s, cols, kv=False):
                wait(dve, w_hi_ready, 2 * c2 + s + 1)
                dve.tensor_tensor(split_part(w_lo, s, cols, kv), raw_part(s, cols, kv), f(split_part(w_hi, s, cols, kv)),
                                  ALU.subtract) \
                    .then_inc(w_ready, 1)

            def split_x_lo(n, m):
                wait(dve, x_hi_ready, n.base + m + 1)
                dve.scalar_tensor_tensor(x_lo[:, m, :], h[:, m, :], gains[:, n.gain, m, :], f(x_hi[:, m, :]),
                                         ALU.mult, ALU.subtract).then_inc(x_ready, 1)

            steps = [0]

            def rs_stepped(ins):
                steps[0] += 1
                ins.then_inc(rs_step, 1)
                dve.wait_ge(rs_step, steps[0])

            def invert_n(n):
                dve.wait_ge(st_done, n.number + 1)
                dve.tensor_scalar(ms_n[:, 0, :], n.sums, 1.0 / D, EPS, ALU.mult, ALU.add).then_inc(ms_ready, 1)
                dve.wait_ge(rms_n, n.number + 1)
                rs_stepped(dve.reciprocal(rs_n[:], ms_n[:, 1, :]))
                rs_stepped(dve.tensor_tensor(ms_n[:, 2, :], ms_n[:, 0, :], rs_n[:], ALU.mult))
                rs_stepped(dve.scalar_tensor_tensor(ms_n[:, 2, :], ms_n[:, 2, :], -0.5, rs_n[:], ALU.mult, ALU.mult))
                dve.scalar_tensor_tensor(rs_n[:], ms_n[:, 2, :], 1.5, rs_n[:], ALU.add, ALU.mult) \
                    .then_inc(rs_n_ready, 1)

            def take_rs_t(n):
                dve.wait_ge(rs_spread, {0: 1, 1: 2, 3: 3}[n.number])
                dve.tensor_copy(rs_t[:], banks[5][:]).then_inc(o_free, 1)
                dve.wait_ge(o_free, n.o_index + 1)

            dve.memset(eps[:], EPS).then_inc(vec_consts, 1)
            dve.memset(ones[:], 1.0).then_inc(vec_consts, 1)
            for t in (kp_hi, kp_lo, av_hi, av_lo):
                dve.memset(f(t[:]), 0.0).then_inc(vec_consts, 1)
            def read_x(m):
                dve.wait_ge(pt_done, m + 1)
                dve.tensor_copy(h[:, m, :], banks[3 + m % 2][:]).then_inc(pt_free, 1)

            read_x(0)
            dve.wait_ge(gain_in, 16)
            for m in range(KD):
                if m + 1 < KD:
                    read_x(m + 1)
                split_x_lo(norms[0], m)
                if m < 2:
                    w_split_lo(0, m, W_COLS)
            w_split_lo(C_V // 2, 0, 4 * GROUPS * HD)
            invert_n(norms[0])
            w_split_lo(C_V // 2, 1, 4 * GROUPS * HD)
            dve.wait_ge(small_in, 8 * 16)
            dve.tensor_scalar(par_all[:, :, HG:], sink_in[:].rearrange("p (g h) -> p g h", g=GROUPS), -1.0, None,
                              ALU.mult).then_inc(vec_consts, 1)
            for qb in range(NT):
                nk = A_KB[qb][1]
                dve.wait_ge(near_p, qb + 1)
                view = near[:, qb, 0:nk * P]
                dve.tensor_copy(view, dist_i[:, qb, 0:nk * P]).then_inc(near_v, 1)
                dve.wait_ge(near_v, 2 * qb + 1)
                dve.scalar_tensor_tensor(view, view, -1.0, view, ALU.mult, ALU.min).then_inc(near_v, 1)
            take_rs_t(norms[0])

            for m in range(2):
                dve.wait_ge(w_used, m + 1)
                for a in range(2):
                    rows = slice(a * HD, (a + 1) * HD)
                    for b in range(2):
                        ins = dve.tensor_tensor(k_dup[b * HD:(b + 1) * HD, 2 * m + a, :], banks[6 + m][rows, :],
                                                rs_t[rows, :], ALU.mult)
                        if a == 1 and b == 1:
                            ins.then_inc(proj_free, 1)
                        else:
                            ins.then_inc(k_dup_ready, 1)
                w_split_lo(C_Q // 2, m, W_COLS)

            def a_k_lo(g):
                for b in range(2):
                    rows = slice(b * HD, (b + 1) * HD)
                    wait(dve, kp_hi_ready, 2 * g + b + 1)
                    dve.tensor_tensor(kp_lo[rows, b, :], k_dup[rows, g, :], f(kp_hi[rows, b, :]), ALU.subtract) \
                        .then_inc(kp_ready, 1)

            v_by_group = v_all[:].rearrange("p t (g d) -> p t g d", g=GROUPS)

            def a_v_lo(g):
                wait(dve, v_hi_ready, g + 1)
                dve.tensor_tensor(av_lo[:, :, HD:2 * HD], v_by_group[:, :, g, :], f(av_hi[:, :, HD:2 * HD]),
                                  ALU.subtract).then_inc(v_ready, 1)

            def a_q_out(g, i, first=False):
                wait(dve, w_used, C_Q + 2 * g + i + 1)
                if not (first and i == 0):
                    wait(dve, q_ready, 2 * g + i)
                dve.scalar_tensor_tensor(q_tmp[:], banks[6 + i][:], HD ** -0.5, rs_t[:], ALU.mult, ALU.mult) \
                    .then_inc(proj_free, 1)

            def a_q_lo(g, i):
                wait(dve, q_hi_ready, 2 * g + i + 1)
                dve.tensor_tensor(aq_lo[:, i, :], q_tmp[:], f(aq_hi[:, i, :]), ALU.subtract).then_inc(q_ready, 1)

            a_k_lo(0)
            for i in range(2):
                a_q_out(0, i, first=True)
                a_q_lo(0, i)
            a_v_lo(0)

            ot_lo_q = ot_lo[:].rearrange("p (g a) (n q) -> p g a n q", a=2, n=NT)
            ot_hi_q = ot_hi[:].rearrange("p (g a) (n q) -> p g a n q", a=2, n=NT)

            def invert_sum(count, u):
                wait(dve, exp_ready, count)
                dve.reciprocal(stat[:, 2, u % 8:u % 8 + 1], stat[:, 1, u % 8:u % 8 + 1]).then_inc(rsum_ready, 1)

            def a_group(g, last):
                def read_scores(u):
                    n, hd = u // HG, u % HG
                    w = A_KB[n][1] * P
                    if u % 2:
                        wait(dve, bias_odd_ready, 8 * g + u // 2 + 1)
                    else:
                        wait(dve, bias_ready, 8 * g + u // 2 + 1)
                    wait(dve, s_done, 16 * g + u + 1)
                    if n >= 2:
                        wait(dve, pt_done, T_A + A_TG * g + A_T0[n - 1])
                    dve.tensor_tensor_reduce(s_a[:, n % 2, hd, 1:1 + w], bias[:, u % 2, 0:w], banks[u % 3][:, 0:w],
                                             -1.0, par[:, HG + hd:HG + hd + 1], ALU.add, ALU.min,
                                             stat[:, 0, u % 8:u % 8 + 1]).then_inc(s_free, 1)

                def pt_lo(n, i):
                    unit = T_A + A_T0[n] + i
                    wait(dve, pt_hi_ready, unit - T_A + A_TG * g + 1)
                    dve.tensor_tensor(apt_lo[:, n % 2, i, :], banks[3 + unit % 2][:], f(apt_hi[:, n % 2, i, :]),
                                      ALU.subtract).then_inc(pt_free, 1)

                def o_lo(n):
                    wait(dve, o_hi_ready, 4 * g + n + 1)
                    dve.tensor_tensor(ot_lo_q[:, g, :, n, :], banks[5][:, 0:2 * P].rearrange("p (a q) -> p a q", a=2),
                                      f(ot_hi_q[:, g, :, n, :]), ALU.subtract).then_inc(o_free, 1)

                def inv(u):
                    invert_sum(16 * g + u + 1, u)

                read_scores(0)
                read_scores(1)
                inv(0)
                read_scores(2)
                inv(1)
                read_scores(3)
                inv(2)
                for n in range(NT):
                    u = 4 * n + 4
                    if n < 3:
                        read_scores(u)
                        inv(u - 1)
                        if n:
                            pt_lo(n - 1, 1)
                        if n > 1:
                            o_lo(n - 2)
                        read_scores(u + 1)
                        inv(u)
                        read_scores(u + 2)
                        inv(u + 1)
                        if n and A_KB[n - 1][1] > 2:
                            pt_lo(n - 1, 2)
                        read_scores(u + 3)
                        if n < 2:
                            w_split_lo(C_Q // 2 + 1 + g, n, W_COLS)
                        pt_lo(n, 0)
                        inv(u + 2)
                    else:
                        inv(u - 1)
                        pt_lo(2, 1)
                        o_lo(1)
                        pt_lo(2, 2)
                        if not last:
                            a_q_out(g + 1, 0)
                            a_q_lo(g + 1, 0)
                            a_k_lo(g + 1)
                        pt_lo(3, 0)
                        o_lo(2)
                        pt_lo(3, 1)
                if not last:
                    a_q_out(g + 1, 1)
                    a_q_lo(g + 1, 1)
                o_lo(3)
                if not last:
                    a_v_lo(g + 1)

            with dve.Fori(0, GROUPS - 1) as g:
                a_group(g, False)
            a_group(GROUPS - 1, True)

            def add_to_h(c, bank_s, m, used, dst=None):
                wait(dve, w_used, used)
                dst = h[:, m, :] if dst is None else dst
                dve.tensor_tensor(dst, h[:, m, :], banks[6 + bank_s][:], ALU.add).then_inc(proj_free, 1)

            def wo_phase(n, c0):
                with dve.Fori(0, KD // 2) as i:
                    for s in range(2):
                        w_split_lo(c0 // 2 + 1 + i, s, W_COLS)
                        add_to_h(c0, s, 2 * i + s, c0 + 2 * i + s + 1)
                        split_x_lo(n, 2 * i + s)

            def ffn_half(layer, half, n, next_cols, mid=None):
                c2 = ((C_FFN0, C_FFN1)[layer] + half * C_HALF) // 2
                j0 = (2 * layer + half) * HALF

                def hidden(j, cols, first=False):
                    w_split_lo(c2 + j + 1, 0, cols)
                    if first:
                        invert_n(norms[2 * layer + 1])
                        w_split_lo(c2 + j + 1, 1, cols)
                        take_rs_t(norms[2 * layer + 1])
                    wait(dve, w_used, 2 * c2 + 2 * j + 1)
                    if not (isinstance(j, int) and j0 + j == 0):
                        wait(dve, silu_ready, j0 + j)
                    dve.tensor_tensor(gate_t[:], banks[0 if first else 6][:], rs_t[:], ALU.mult).then_inc(proj_free, 1)
                    if not first:
                        w_split_lo(c2 + j + 1, 1, cols)
                    wait(dve, w_used, 2 * c2 + 2 * j + 2)
                    wait(dve, silu_rs_ready, j0 + j + 1)
                    if not (isinstance(j, int) and j0 + j == 0):
                        wait(dve, f_ready, j0 + j)
                    dve.tensor_tensor(hid[:], banks[1 if first else 7][:], gate_s[:], ALU.mult).then_inc(proj_free, 1)
                    wait(dve, f_hi_ready, j0 + j + 1)
                    dve.tensor_tensor(f_lo[:, j, :], hid[:], f(f_hi[:, j, :]), ALU.subtract).then_inc(f_ready, 1)

                hidden(0, W_COLS, first=half == 0)
                with dve.Fori(1, HALF - 1) as j:
                    hidden(j, W_COLS)
                hidden(HALF - 1, W_DOWN)
                if mid is not None:
                    mid()

                def turned(m, s):
                    wait(dve, pt_done, T_FIN + m + 1)
                    dve.tensor_tensor(out_n_v[:, :, m, :], banks[3 + s][:].rearrange("p (t n) -> p t n", t=NT),
                                      g_fin[:, m, :].unsqueeze(1).to_broadcast([P, NT, P]), ALU.mult) \
                        .then_inc(pt_free, 1)

                final = n is not None and n.gain is None

                def pair(i, cols):
                    for s in range(2):
                        m = 2 * i + s
                        if cols:
                            w_split_lo(c2 + HALF + 1 + i, s, cols)
                        if final and not (isinstance(i, int) and i == 0):
                            wait(dve, pt_done, T_FIN + m - 1)
                            wait(dve, sq_ready, n.base + m - 1)
                        add_to_h(c2, s, m, 2 * c2 + 2 * HALF + m + 1, h_fin[:, s, :] if final else None)
                        if final:
                            if not (isinstance(i, int) and i == 0 and s == 0):
                                turned(m - 1, 1 - s)
                        elif n is not None:
                            split_x_lo(n, m)

                pair(0, W_DOWN)
                with dve.Fori(1, KD // 2 - 1) as i:
                    pair(i, W_DOWN)
                pair(KD // 2 - 1, next_cols)
                if final:
                    turned(KD - 1, 1)

            tab = [0]

            def step(ins):
                tab[0] += 1
                ins.then_inc(tab_v, 1)
                dve.wait_ge(tab_v, tab[0])

            def angles():
                dve.wait_ge(pool_consts, 2 + HEADS + ROPE // 2)
                step(dve.tensor_copy(pos_f[:], pos_r[:]))
                for t in range(NT):
                    step(dve.tensor_scalar(ang[:, t, :], inv_f[:], pos_f[:, t:t + 1], None, ALU.mult))
                step(dve.tensor_scalar(turns[:], ang[:], float(1.0 / (2.0 * np.pi)), None, ALU.mult))
                step(dve.tensor_scalar(turns[:], turns[:], ROUND, None, ALU.add))
                step(dve.tensor_scalar(turns[:], turns[:], ROUND, None, ALU.subtract))
                step(dve.tensor_scalar(turns_hi[:], turns[:], 1.0 / 2048.0, None, ALU.mult))
                step(dve.tensor_scalar(turns_hi[:], turns_hi[:], ROUND, None, ALU.add))
                step(dve.tensor_scalar(turns_hi[:], turns_hi[:], ROUND, 2048.0, ALU.subtract, ALU.mult))
                step(dve.tensor_tensor(turns[:], turns[:], turns_hi[:], ALU.subtract))
                for part in two_pi_parts():
                    step(dve.scalar_tensor_tensor(ang[:], turns_hi[:], -part, ang[:], ALU.mult, ALU.add))
                    step(dve.scalar_tensor_tensor(ang[:], turns[:], -part, ang[:], ALU.mult, ALU.add))
                step(dve.tensor_scalar(ang[:], ang[:], 3.1415925, -3.1415925, ALU.min, ALU.max))
                assert tab[0] == TAB_STEPS

            def cosines():
                dve.wait_ge(tab_a, 1)
                step(dve.tensor_tensor(turns[:], half_sin[:], half_sin[:], ALU.mult))
                step(dve.tensor_scalar(cos_n[:, :, 0:16], turns[:], -2.0, 1.0, ALU.mult, ALU.add))
                step(dve.tensor_scalar(cos_n[:, :, 16:32], turns[:], -2.0, 1.0, ALU.mult, ALU.add))
                dve.wait_ge(tab_a, 2)
                step(dve.tensor_scalar(sin_n[:, :, 0:16], sin_n[:, :, 16:32], -1.0, None, ALU.mult))

            out_n_v = out_n[:].rearrange("p t (m n) -> p t m n", n=P)

            wo_phase(norms[1], C_WOA)
            ffn_half(0, 0, None, W_COLS)
            angles()
            ffn_half(0, 1, norms[2], W_LAT, mid=cosines)

            w_split_lo(C_LAT // 2 + 1, 0, W_LAT)
            w_split_lo(C_LAT // 2 + 1, 1, W_LAT)
            invert_n(norms[2])
            dve.wait_ge(rs_n_ready, 3)
            for t in range(NT):
                dve.tensor_scalar(lat[:, t, QL:B_IN], banks[2 * t + 1][:, 0:B_IN - QL], rs_n[:, 2 * t:2 * t + 1], None,
                                  ALU.mult).then_inc(lat_ready, 1)
            w_split_lo(C_B // 2, 0, W_UQ)
            w_split_lo(C_B // 2, 1, W_UKV, kv=True)

            def rotate(view, cos_v, sin_v, a, b, base):
                dve.tensor_tensor(a, view, cos_v, ALU.mult).then_inc(rope_v, 1)
                dve.tensor_tensor(b[..., 0:16], view[..., 16:32], sin_v[..., 0:16], ALU.mult).then_inc(rope_v, 1)
                dve.tensor_tensor(b[..., 16:32], view[..., 0:16], sin_v[..., 16:32], ALU.mult).then_inc(rope_v, 1)
                wait(dve, rope_v, base + 3)
                dve.tensor_tensor(view, a, b, ALU.add).then_inc(rope_v, 1)

            dve.wait_ge(lat_ready, 2 * NT)
            dve.wait_ge(tab_v, TAB_STEPS + 4)
            rotate(lat[:, :, QL + KVL:B_IN], cos_n[:], sin_n[:],
                   rope_a[:, 0:NT * ROPE].rearrange("p (t d) -> p t d", t=NT),
                   rope_b[:, 0:NT * ROPE].rearrange("p (t d) -> p t d", t=NT), 0)
            dve.wait_ge(lrms_ready, 2)
            dve.reciprocal(lat_stat[:, 2, :], lat_stat[:, 1, :]).then_inc(lrs_ready, 1)
            dve.wait_ge(lrs_ready, 1)
            for t in range(NT):
                dve.tensor_scalar(lat[:, t, 0:QL], lat[:, t, 0:QL], lat_stat[:, 2, t:t + 1], None, ALU.mult) \
                    .then_inc(latn_ready, 1)

            dve.wait_ge(rms_n, 2)
            for t in (bv_hi, bv_lo):
                dve.memset(f(t[:]), 0.0).then_inc(vec_consts, 1)

            def b_pt_lo(unit, base, dst, hi, rows=P, gain=None):
                wait(dve, pt_hi_ready, unit - T_A + base + 1)
                src = banks[3 + unit % 2][0:rows, :]
                if gain is None:
                    dve.tensor_tensor(dst, src, f(hi), ALU.subtract).then_inc(pt_free, 1)
                else:
                    dve.scalar_tensor_tensor(dst, src, gain, f(hi), ALU.mult, ALU.subtract).then_inc(pt_free, 1)

            for b in range(QL // P):
                b_pt_lo(T_BPRE + b, 0, cq_lo[:, b, :], cq_hi[:, b, :], gain=g_q[:, b:b + 1])
            for b in range(KVL // P):
                b_pt_lo(T_BPRE + 3 + b, 0, ckv_lo[:, b, :], ckv_hi[:, b, :], gain=g_kv[:, b:b + 1])
            dve.wait_ge(pt_done, T_BPRE + 6)
            dve.wait_ge(rope_v, 4)
            dve.tensor_copy(rope_a[NOPE:QK, :], banks[4][0:ROPE, :]).then_inc(pt_free, 1)
            for hd in range(HG):
                if hd < HG - 1:
                    dve.wait_ge(krope_hi, hd + 1)
                else:
                    dve.wait_ge(pt_hi_ready, T_BPRE + 6 - T_A)
                ins = dve.tensor_tensor(bk_lo[NOPE:QK, hd, :], rope_a[NOPE:QK, :], f(bk_hi[NOPE:QK, hd, :]), ALU.subtract)
                ins.then_inc(krope_ready, 1)

            def b_rotate_q(g, half):
                wait(dve, proj_free, U_B + U_BG * g + 2 * half + 2)
                ts = slice(2 * half, 2 * half + 2)
                view = q_n[:].rearrange("p t (h d) -> p t h d", h=HG)[:, ts, :, NOPE:QK]
                shape = [P, 2, HG, ROPE]
                rotate(view, cos_n[:, ts, :].unsqueeze(2).to_broadcast(shape),
                       sin_n[:, ts, :].unsqueeze(2).to_broadcast(shape),
                       rope_a[:].rearrange("p (t h d) -> p t h d", t=NT, h=HG)[:, ts],
                       rope_b[:].rearrange("p (t h d) -> p t h d", t=NT, h=HG)[:, ts], 8 * g + 4 * half + 4)

            def b_k_lo(g, i):
                for b in range(2):
                    wait(dve, kp_hi_ready, 2 * GROUPS + 4 * g + 2 * i + b + 1)
                    ins = dve.tensor_tensor(bk_lo[0:NOPE, 2 * i + b, :], banks[6 + i][b * HD:(b + 1) * HD, :],
                                            f(bk_hi[0:NOPE, 2 * i + b, :]), ALU.subtract)
                    if b:
                        ins.then_inc(proj_free, 1)

            def b_q_lo(g, base):
                for hd in range(HG):
                    wait(dve, pt_hi_ready, base - T_A + hd + 1)
                    dve.tensor_tensor(bq_lo[0:QK, hd, :], banks[3 + hd % 2][0:QK, :], f(bq_hi[0:QK, hd, :]),
                                      ALU.subtract).then_inc(pt_free, 1)

            bv_hi_v = bv_hi[:].rearrange("p t a (s d) -> p (t a) s d", d=HD)
            bv_lo_v = bv_lo[:].rearrange("p t a (s d) -> p (t a) s d", d=HD)

            def b_v_lo(g, i):
                wait(dve, v_hi_ready, GROUPS + 2 * g + i + 1)
                dve.tensor_tensor(bv_lo_v[:, 4 * i:4 * i + 4, ::2, :],
                                  banks[6 + i][:].rearrange("p (t s d) -> p t s d", t=4, s=2),
                                  f(bv_hi_v[:, 4 * i:4 * i + 4, ::2, :]), ALU.subtract).then_inc(proj_free, 1)

            dve.wait_ge(krope_ready, HG)
            b_rotate_q(0, 0)
            b_rotate_q(0, 1)
            b_k_lo(0, 0)
            b_k_lo(0, 1)
            b_q_lo(0, T_BPRE + 6)

            def b_group(g, last, cols0, cols1):
                def maximum(u):
                    wait(dve, s_done, 16 * (GROUPS + g) + u + 1)
                    dve.tensor_reduce(stat[:, 0, u % 8:u % 8 + 1], banks[u % 3][:], AX_X, ALU.max, negate=True) \
                        .then_inc(max_ready, 1)

                def pt_lo(n, i):
                    wait(dve, pt_hi_ready, T_B - T_A + B_TG * g + 4 * n + i + 1)
                    dve.tensor_tensor(bpt_lo[:, n % 2, i, :], banks[3 + i % 2][:], f(bpt_hi[:, n % 2, i, :]),
                                      ALU.subtract).then_inc(pt_free, 1)

                def o_lo(pair):
                    wait(dve, o_hi_ready, 4 * GROUPS + 2 * g + pair + 1)
                    dve.tensor_tensor(ot_lo[:, 2 * g + pair, :], banks[5][:], f(ot_hi[:, 2 * g + pair, :]),
                                      ALU.subtract).then_inc(o_free, 1)

                def inv(u):
                    invert_sum(16 * (GROUPS + g) + u + 1, u)

                maximum(0)
                maximum(1)
                inv(0)
                maximum(2)
                inv(1)
                maximum(3)
                inv(2)
                for n in range(HG):
                    u = 4 * n + 4
                    if n < 3:
                        maximum(u)
                        inv(u - 1)
                        maximum(u + 1)
                        inv(u)
                        maximum(u + 2)
                        inv(u + 1)
                        maximum(u + 3)
                        pt_lo(n, 0)
                        inv(u + 2)
                        pt_lo(n, 1)
                        if n == 0:
                            b_v_lo(g, 0)
                        pt_lo(n, 2)
                        if n == 0:
                            b_v_lo(g, 1)
                        pt_lo(n, 3)
                        if n < 2:
                            w_split_lo(C_B // 2 + 1 + g, n, (cols0, cols1)[n], kv=n == 1 and cols0 == W_UQ)
                        else:
                            o_lo(0)
                            if not last:
                                b_rotate_q(g + 1, 0)
                                b_rotate_q(g + 1, 1)
                    else:
                        inv(u - 1)
                        for i in range(4):
                            pt_lo(n, i)
                            if i % 2 == 0 and not last:
                                b_k_lo(g + 1, i // 2)
                        if not last:
                            b_q_lo(g + 1, T_B + B_TG * g + 16)
                        o_lo(1)

            with dve.Fori(0, GROUPS - 1) as g:
                b_group(g, False, W_UQ, W_UKV)
            b_group(GROUPS - 1, True, W_COLS, W_COLS)

            wo_phase(norms[3], C_WOB)
            ffn_half(1, 0, None, W_COLS)
            ffn_half(1, 1, norms[4], 0)
            invert_n(norms[4])
            dve.wait_ge(rs_n_ready, 5)
            dve.wait_ge(pt_free, T_FIN + KD)
            for t in (0, 2):
                dve.tensor_scalar(out_n[:, t, :], out_n[:, t, :], rs_n[:, 2 * t:2 * t + 1], None, ALU.mult) \
                    .then_inc(out_ready[0], 1)


_INS = ["x", "positions", "norm_mix", "norm_ffn", "a_w_qkv", "a_sink", "a_w_o", "b_w_in", "b_g_q", "b_g_kv",
        "b_w_uq", "b_w_ukv", "b_w_o", "ffn_w_gu", "ffn_w_down", "final_norm"]


def kernel(**inputs):
    import concourse.bacc as bacc
    from concourse.bass_utils import run_bass_kernel_spmd as run

    nc = bacc.Bacc("TRN2", target_bir_lowering=False, num_devices=1)
    arrays, args = {}, []
    for name in _INS:
        a = np.ascontiguousarray(inputs[name])
        arrays[f"in_{name}"] = a
        args.append(nc.dram_tensor(f"in_{name}", a.shape, mybir.dt.from_np(a.dtype), kind="ExternalInput").ap())
    args.append(nc.dram_tensor("out_0", (1, T, D), F32, kind="ExternalOutput").ap())
    build(nc, *args)
    r = run(nc, [arrays], core_ids=[0])
    return r.results[0]["out_0"]
```

```python
from contextlib import ExitStack

import numpy as np
import concourse.bass as bass
from concourse import mybir

F32 = mybir.dt.float32
F32R = mybir.dt.float32r
I32 = mybir.dt.int32
ALU = mybir.AluOpType
ACT = mybir.ActivationFunctionType
AX_X = mybir.AxisListType.X

P = 128
D = 1024
KD = D // P
T = 512
NT = T // P
HEADS = 16
GROUPS = 4
HG = HEADS // GROUPS
HD = 64
WINDOW = 128
QL, KVL, ROPE, NOPE = 384, 256, 32, 64
B_IN = QL + KVL + ROPE
QK = NOPE + ROPE
DFF = 2816
FB = DFF // P
HALF = FB // 2
EPS = 1e-6
MASKED = -1e36
SLOT = HALF * P
SA = 1 + 3 * P

C_K, C_V, C_Q, C_WOA = 0, 2, 4, 12
C_FFN0 = C_WOA + KD
C_HALF = 2 * HALF + KD
C_LAT = C_FFN0 + 2 * C_HALF
C_B = C_LAT + 4
C_WOB = C_B + 2 * GROUPS
C_FFN1 = C_WOB + KD
C_END = C_FFN1 + 2 * C_HALF
W_COLS = KD * P
W_DOWN = HALF * P
W_LAT = 2 * B_IN
W_UQ = QL // P * HG * QK
W_UKV = KVL // P * HG * 2 * HD

U_K, U_Q, U_WOA = 0, 2, 10
U_FFN0 = U_WOA + KD
U_B = U_FFN0 + 2 * C_HALF
U_BG = 8
U_WOB = U_B + U_BG * GROUPS
U_FFN1 = U_WOB + KD

T_A = KD
A_KB = [(0, 2), (0, 3), (1, 3), (2, 2)]
A_T0 = [0, 2, 5, 8]
A_TG = 10
T_BPRE = T_A + A_TG * GROUPS
T_B = T_BPRE + 6 + HG
B_TG = 4 * HG + HG
T_FIN = T_B + B_TG * GROUPS - HG

O_NORM0, O_A = 0, 1
O_NORM1 = O_A + 4 * GROUPS
O_B = O_NORM1 + 1
O_NORM3 = O_B + 2 * GROUPS
S_A = 16
S_B = S_A + 16 * GROUPS

INV_FREQ = np.float32(10000.0) ** (-np.arange(16, dtype=np.float32) * np.float32(2.0) / np.float32(32))
ROUND = 12582912.0


TAB_STEPS = 21
LRS_KV, LRS_Q = 6, 7


def two_pi_parts():
    rest, parts = 2.0 * np.pi, []
    for _ in range(4):
        m, e = np.frexp(rest)
        part = float(np.ldexp(np.floor(m * 2048.0), int(e) - 11))
        parts.append(part)
        rest -= part
    return parts


def build(nc, x, positions, norm_mix, norm_ffn, a_w_qkv, a_sink, a_w_o, b_w_in, b_g_q, b_g_kv,
          b_w_uq, b_w_ukv, b_w_o, ffn_w_gu, ffn_w_down, final_norm, out):
    ctx = ExitStack()
    with ctx:
        place = {"at": (nc.sbuf_base + 63) // 64 * 64}
        top = nc.sbuf_usable_end

        def tile_at(name, shape, dtype, offset):
            size = 4 * int(np.prod(shape[1:]))
            assert offset + size <= top, (name, offset + size, top)
            return nc.alloc_sbuf_tensor_at(name, shape, dtype, offset=offset), offset + (size + 31) // 32 * 32

        def tile(name, shape, dtype=F32):
            t, place["at"] = tile_at(name, shape, dtype, place["at"])
            return t

        def region(start, specs):
            tiles, at = [], start
            for name, shape, dtype in specs:
                t, at = tile_at(name, shape, dtype, at)
                tiles.append(t)
            return tiles

        h = tile("h", [P, KD, T])
        x_hi = tile("x_hi", [P, KD, T], F32R)
        x_lo = tile("x_lo", [P, KD, T], F32R)
        ot_start = place["at"]
        ot_hi = tile("ot_hi", [P, KD, T], F32R)
        ot_lo = tile("ot_lo", [P, KD, T], F32R)
        scratch_size = 88 * 1024
        scratch = place["at"]
        place["at"] += scratch_size
        w_raw = [tile(f"w_raw{s}", [P, SLOT]) for s in range(2)]
        w_hi = [tile(f"w_hi{s}", [P, SLOT], F32R) for s in range(2)]
        w_lo = [tile(f"w_lo{s}", [P, SLOT], F32R) for s in range(2)]
        ident = tile("ident", [P, P])
        ones = tile("ones", [P, 2])
        rs_t = tile("rs_t", [P, T])
        rs_n = tile("rs_n", [P, 8])
        ms_n = tile("ms_n", [P, 3, 8])
        gains = tile("gains", [P, 4, KD, 1])
        g_q = tile("g_q", [P, QL // P])
        g_kv = tile("g_kv", [P, KVL // P])
        par_all = tile("par_all", [P, GROUPS, 2 * HG])
        par = tile("par", [P, 2 * HG])
        sink_in = tile("sink_in", [P, HEADS])
        stat = tile("stat", [P, 3, 8])
        lat_stat = tile("lat_stat", [P, 4, 8])
        q_scale = tile("q_scale", [P, NT])
        cos_n = tile("cos_n", [P, NT, ROPE])
        sin_n = tile("sin_n", [P, NT, ROPE])
        x_start = ot_start - 2 * 4 * KD * T

        x_n, sq0, ss0 = region(ot_start, [
            ("x_n", [P, NT, D], F32), ("sq0", [P, 2, T], F32), ("ss0", [P, T], F32)])
        (q_tmp, aq_hi, aq_lo, k_dup, kp_hi, kp_lo, v_all, av_hi, av_lo, near, bias, s_a, apt_hi, apt_lo) = \
            region(scratch, [
                ("q_tmp", [P, T], F32), ("aq_hi", [P, 2, T], F32R), ("aq_lo", [P, 2, T], F32R),
                ("k_dup", [P, GROUPS, T], F32), ("kp_hi", [P, 2, T], F32R), ("kp_lo", [P, 2, T], F32R),
                ("v_all", [P, NT, GROUPS * HD], F32),
                ("av_hi", [P, NT, 3 * HD], F32R), ("av_lo", [P, NT, 3 * HD], F32R),
                ("near", [P, NT, 3 * P], F32), ("bias", [P, 2, 3 * P], F32),
                ("s_a", [P, 2, HG, SA], F32),
                ("apt_hi", [P, 2, 3, T], F32R), ("apt_lo", [P, 2, 3, T], F32R)])
        v0_hi, v0_lo = region(scratch + 46 * 1024, [
            ("v0_hi", [P, 4 * GROUPS * HD], F32R), ("v0_lo", [P, 4 * GROUPS * HD], F32R)])
        pos_k, pos_q, dist_i = region(scratch + 58 * 1024, [
            ("pos_k", [P, T], I32), ("pos_q", [P, NT], I32), ("dist_i", [P, NT, 3 * P], I32)])
        pos_r, pos_f, inv_f, ang, turns, turns_hi, half_sin = region(scratch + 44 * 1024, [
            ("pos_r", [P, NT], I32), ("pos_f", [P, NT], F32), ("inv_f", [P, 16], F32), ("ang", [P, NT, 16], F32),
            ("turns", [P, NT, 16], F32), ("turns_hi", [P, NT, 16], F32), ("half_sin", [P, NT, 16], F32)])
        f_hi, f_lo, gate_t, gate_s, hid = region(ot_start, [
            ("f_hi", [P, HALF, T], F32R), ("f_lo", [P, HALF, T], F32R),
            ("gate_t", [P, T], F32), ("gate_s", [P, T], F32), ("hid", [P, T], F32)])
        sq1, ss1, h_fin, g_fin = region(scratch + 48 * 1024, [
            ("sq1", [P, 2, T], F32), ("ss1", [P, T], F32),
            ("h_fin", [P, 2, T], F32), ("g_fin", [P, KD, P], F32)])
        (out_n,) = region(x_start, [("out_n", [P, NT, D], F32)])
        bq_hi, bq_lo, bk_hi, bk_lo = region(x_start, [
            ("bq_hi", [P, HG, T], F32R), ("bq_lo", [P, HG, T], F32R),
            ("bk_hi", [P, HG, T], F32R), ("bk_lo", [P, HG, T], F32R)])
        cq_hi, cq_lo, ckv_hi, ckv_lo, q_n, bv_hi, bv_lo, s_b, bpt_hi, bpt_lo, rope_a = region(scratch, [
            ("cq_hi", [P, QL // P, T], F32R), ("cq_lo", [P, QL // P, T], F32R),
            ("ckv_hi", [P, KVL // P, T], F32R), ("ckv_lo", [P, KVL // P, T], F32R),
            ("q_n", [P, NT, HG * QK], F32),
            ("bv_hi", [P, NT, 2, 3 * HD], F32R), ("bv_lo", [P, NT, 2, 3 * HD], F32R),
            ("s_b", [P, 2, HG, T], F32),
            ("bpt_hi", [P, 2, NT, T], F32R), ("bpt_lo", [P, 2, NT, T], F32R),
            ("rope_a", [P, T], F32)])
        krope_t = ss1
        rope_b = rs_t
        lat, lat_sq = region(scratch + 54 * 1024, [("lat", [P, NT, B_IN], F32), ("lat_sq", [P, QL], F32)])

        banks = [ctx.enter_context(nc.psum_tensor(f"bank{i}", [P, T], F32)) for i in range(8)]
        lat_banks = [banks[3], banks[4], banks[0], banks[4], banks[3]]

        def sem(name):
            return ctx.enter_context(nc.semaphore(name))

        x_in = [sem(f"x_in{i}") for i in range(NT)]
        gain_in = sem("gain_in")
        small_in = sem("small_in")
        pos_in = sem("pos_in")
        gfin_in = sem("gfin_in")
        w_in = [sem(f"w_in{i}") for i in range(2)]
        w_hi_ready = sem("w_hi_ready")
        w_ready = sem("w_ready")
        w_used = sem("w_used")
        pool_consts = sem("pool_consts")
        vec_consts = sem("vec_consts")
        near_p = sem("near_p")
        near_v = sem("near_v")
        tab_v = sem("tab_v")
        tab_a = sem("tab_a")
        proj_done = sem("proj_done")
        proj_free = sem("proj_free")
        pt_done = sem("pt_done")
        pt_hi_ready = sem("pt_hi_ready")
        pt_free = sem("pt_free")
        s_done = sem("s_done")
        s_free = sem("s_free")
        o_done = sem("o_done")
        o_hi_ready = sem("o_hi_ready")
        o_free = sem("o_free")
        x_hi_ready = sem("x_hi_ready")
        x_ready = sem("x_ready")
        sq_ready = sem("sq_ready")
        ss_ready = sem("ss_ready")
        st_done = sem("st_done")
        ms_ready = sem("ms_ready")
        rms_n = sem("rms_n")
        rs_step = sem("rs_step")
        rs_n_ready = sem("rs_n_ready")
        rs_spread = sem("rs_spread")
        k_dup_ready = sem("k_dup_ready")
        q_hi_ready = sem("q_hi_ready")
        q_ready = sem("q_ready")
        kp_hi_ready = sem("kp_hi_ready")
        kp_ready = sem("kp_ready")
        v_hi_ready = sem("v_hi_ready")
        v_ready = sem("v_ready")
        par_ready = sem("par_ready")
        sinkcol_ready = sem("sinkcol_ready")
        bias_ready = sem("bias_ready")
        bias_odd_ready = sem("bias_odd_ready")
        max_ready = sem("max_ready")
        exp_ready = sem("exp_ready")
        rsum_ready = sem("rsum_ready")
        p_ready = sem("p_ready")
        lat_done = sem("lat_done")
        lat_q_ready = sem("lat_q_ready")
        lat_kv_ready = sem("lat_kv_ready")
        lsq_ready = sem("lsq_ready")
        kv_sq_ready = sem("kv_sq_ready")
        lrms_ready = sem("lrms_ready")
        lrs_step = sem("lrs_step")
        latn_ready = sem("latn_ready")
        rope_v = sem("rope_v")
        krope_hi = sem("krope_hi")
        krope_ready = sem("krope_ready")
        krope_pool = sem("krope_pool")
        silu_ready = sem("silu_ready")
        silu_rs_ready = sem("silu_rs_ready")
        f_hi_ready = sem("f_hi_ready")
        f_ready = sem("f_ready")
        out_ready = [sem("out_ready_v"), sem("out_ready_a")]
        out_sent = sem("out_sent")

        def wait(eng, s, value):
            eng.wait_ge(s, value)
            if not isinstance(value, int):
                eng.nop(nofuse=True)

        def wait_on(eng, s, value):
            eng.wait_ge(s, value)

        def f(ap):
            return ap.bitcast(F32)

        def raw_part(s, cols, kv):
            w = w_raw[s][:, 0:cols]
            return w if not kv else w.rearrange("p (b c d) -> p b c d", c=2, d=HD)

        def split_part(w, s, cols, kv):
            w = w[s][:, 0:cols]
            return w if not kv else w.rearrange("p (c b d) -> p b c d", c=2, d=HD)

        class Norm:

            def __init__(self, number, gain, block_sem, block_base, tiles, sums, o_index):
                self.number, self.gain, self.base = number, gain, KD * number
                self.block_sem, self.block_base = block_sem, block_base
                self.sq, self.ss = tiles
                self.sums, self.o_index = sums, o_index

        later = (sq1, ss1)
        U_DOWN0 = U_FFN0 + C_HALF + 2 * HALF
        U_DOWN1 = U_FFN1 + C_HALF + 2 * HALF
        norms = [
            Norm(0, 0, pt_free, 0, (sq0, ss0), banks[4][:, 0:8], O_NORM0),
            Norm(1, 2, proj_free, U_WOA, later, banks[4][:, 0:8], O_NORM1),
            Norm(2, 1, proj_free, U_DOWN0, later, banks[0][:, 0:8], None),
            Norm(3, 3, proj_free, U_WOB, later, banks[4][:, 0:8], O_NORM3),
            Norm(4, None, proj_free, U_DOWN1, later, banks[5][:, 0:8], None)]

        qkv_v = a_w_qkv[0].rearrange("(k p) (j n) -> p k j n", p=P, n=P)
        v_v = a_w_qkv[0].rearrange("(k p) n -> p k n", p=P)
        wo_v = [w[0].rearrange("(k p) (m n) -> p k m n", p=P, n=P) for w in (a_w_o, b_w_o)]
        gu_v = [ffn_w_gu[i].rearrange("(k p) (j n) -> p k j n", p=P, n=P) for i in range(2)]
        down_v = [ffn_w_down[i].rearrange("(k p) (m n) -> p k m n", p=P, n=P) for i in range(2)]
        in_v = b_w_in[0].rearrange("(k p) n -> p k n", p=P)
        uq_v = b_w_uq[0].rearrange("(k p) (g n) -> p k g n", p=P, n=HG * QK)
        ukv_v = b_w_ukv[0].rearrange("(k p) (g n) -> p k g n", p=P, n=HG * 2 * HD)

        block = ctx.enter_context(nc.Block())

        @block.sync
        def _(sp):
            def load(c2, s, src, cols):
                if not (isinstance(c2, int) and c2 == 0):
                    wait(sp, w_ready, 2 * c2 + s - 1)
                dst = w_raw[s][:, 0:src.shape[1] * cols].rearrange("p (k n) -> p k n", n=cols)
                sp.dma_start(dst, src).then_inc(w_in[s], 16)

            xv = x[0].rearrange("(t p) d -> p t d", p=P)
            for t in range(NT):
                sp.dma_start(x_n[:, t, :], xv[:, t, :]).then_inc(x_in[t], 16)
            def load_gain(i, g, landed):
                with nc.allow_non_contiguous_dma(reason="gains by partition"):
                    sp.dma_start(gains[:, i, :, 0], g.rearrange("(k p) -> p k", p=P)).then_inc(landed, 16)

            load_gain(0, norm_mix[0], gain_in)
            load(0, 0, qkv_v[:, :, 8, :], P)
            load(0, 1, qkv_v[:, :, 9, :], P)
            for i, g in enumerate((norm_mix[1], norm_ffn[0], norm_ffn[1])):
                load_gain(i + 1, g, small_in)
            with nc.allow_non_contiguous_dma(reason="gains by partition"):
                sp.dma_start(g_q[:], b_g_q[0].rearrange("(k p) -> p k", p=P)).then_inc(small_in, 16)
                sp.dma_start(g_kv[:], b_g_kv[0].rearrange("(k p) -> p k", p=P)).then_inc(small_in, 16)
                sp.dma_start(pos_q[:], positions[0].rearrange("(t p) -> p t", p=P)).then_inc(small_in, 16)
            sp.dma_start(sink_in[:], a_sink[0].partition_broadcast(P)).then_inc(small_in, 16)
            sp.dma_start(pos_k[:], positions[0].partition_broadcast(P)).then_inc(small_in, 16)

            for s in range(2):
                load(C_V // 2, s, v_v[:, 4 * s:4 * s + 4, (HEADS + GROUPS) * HD:], GROUPS * HD)
            with sp.Fori(0, GROUPS) as g:
                for s in range(2):
                    load(C_Q // 2 + g, s, qkv_v[:, :, 2 * g + s, :], P)

            def load_wo(layer, c0):
                with sp.Fori(0, KD // 2) as i:
                    for s in range(2):
                        load(c0 // 2 + i, s, wo_v[layer][:, :, 2 * i + s, :], P)

            def load_ffn(layer, c0):
                for half in range(2):
                    c2 = c0 // 2 + half * C_HALF // 2
                    with sp.Fori(0, HALF) as j:
                        load(c2 + j, 0, gu_v[layer][:, :, half * HALF + j, :], P)
                        load(c2 + j, 1, gu_v[layer][:, :, FB + half * HALF + j, :], P)
                    with sp.Fori(0, KD // 2) as i:
                        for s in range(2):
                            load(c2 + HALF + i, s,
                                 down_v[layer][:, half * HALF:(half + 1) * HALF, 2 * i + s, :], P)

            load_wo(0, C_WOA)
            sp.wait_ge(w_used, C_WOA + 1)
            with nc.allow_non_contiguous_dma(reason="positions by partition"):
                sp.dma_start(pos_r[:], positions[0].rearrange("(t p) -> p t", p=P)).then_inc(pos_in, 16)
            load_ffn(0, C_FFN0)
            for i in range(4):
                load(C_LAT // 2 + i // 2, i % 2, in_v[:, 2 * i:2 * i + 2, :], B_IN)
            with sp.Fori(0, GROUPS) as g:
                load(C_B // 2 + g, 0, uq_v[:, :, g, :], HG * QK)
                load(C_B // 2 + g, 1, ukv_v[:, :, g, :], HG * 2 * HD)
            load_wo(1, C_WOB)
            sp.wait_ge(w_used, C_WOB + 1)
            sp.dma_start(g_fin[:], final_norm.rearrange("(k n) -> k n", n=P).partition_broadcast(P)) \
                .then_inc(gfin_in, 16)
            load_ffn(1, C_FFN1)
            ov = out[0].rearrange("(t p) d -> p t d", p=P)
            for t in range(NT):
                sp.wait_ge(out_ready[t % 2], t // 2 + 1)
                sp.dma_start(ov[:, t, :], out_n[:, t, :]).then_inc(out_sent, 16)
            sp.wait_ge(out_sent, 16 * NT)

        @block.gpsimd
        def _(pool):
            def w_split_hi(c2, s, cols, kv=False):
                wait(pool, w_in[s], 16 * c2 + 16)
                if not (isinstance(c2, int) and c2 == 0):
                    wait(pool, w_used, 2 * c2 + s - 1)
                pool.tensor_scalar(split_part(w_hi, s, cols, kv), raw_part(s, cols, kv), 1.0, 1.0, ALU.mult, ALU.mult) \
                    .then_inc(w_hi_ready, 1)

            def sum_squares(n, m, b, first=False):
                wait(pool, sq_ready, n.base + m + 1)
                if first:
                    if n.number:
                        pool.wait_ge(st_done, n.number)
                    pool.tensor_scalar(n.ss[:], n.sq[:, b, :], 1.0, 1.0, ALU.mult, ALU.mult).then_inc(ss_ready, 1)
                else:
                    wait(pool, ss_ready, n.base + m)
                    pool.tensor_tensor(n.ss[:], n.ss[:], n.sq[:, b, :], ALU.add).then_inc(ss_ready, 1)

            pool.memset(ident[:], 0.0).then_inc(pool_consts, 1)
            pool.wait_ge(pool_consts, 1)
            pool.affine_select(out=ident[:], in_=ident[:], compare_op=ALU.not_equal, fill=1.0, base=0,
                               pattern=[[-1, P]], channel_multiplier=1).then_inc(pool_consts, 1)
            for i in range(HEADS):
                slope = float(np.float32(2.0 ** (-8.0 * (i + 1) / HEADS)))
                pool.memset(par_all[:, i // HG, i % HG:i % HG + 1], slope).then_inc(pool_consts, 1)
            w_split_hi(0, 0, W_COLS)
            w_split_hi(0, 1, W_COLS)
            sum_squares(norms[0], 0, 0, first=True)
            sum_squares(norms[0], 1, 1)
            pool.wait_ge(w_in[0], 32)
            pool.tensor_scalar(v0_hi[:], w_raw[0][:, 0:4 * GROUPS * HD], 1.0, 1.0, ALU.mult, ALU.mult) \
                .then_inc(w_hi_ready, 1)
            with pool.Fori(1, KD // 2) as i:
                for s in range(2):
                    sum_squares(norms[0], 2 * i + s, s)
            pool.wait_ge(small_in, 8 * 16)
            for qb in range(NT):
                k0, nk = A_KB[qb]
                pool.tensor_tensor(dist_i[:, qb, 0:nk * P], pos_k[:, k0 * P:(k0 + nk) * P],
                                   pos_q[:, qb:qb + 1].to_broadcast([P, nk * P]), ALU.subtract).then_inc(near_p, 1)
            w_split_hi(C_V // 2, 1, 4 * GROUPS * HD)
            w_split_hi(C_Q // 2, 0, W_COLS)
            for qb in range(NT):
                k0, nk = A_KB[qb]
                gap = (k0 - qb) * P
                view = near[:, qb, 0:nk * P]
                pool.wait_ge(near_v, 2 * qb + 2)
                pool.affine_select(out=view, in_=view, compare_op=ALU.is_ge, fill=MASKED, base=WINDOW - gap,
                                   pattern=[[-1, nk * P]], channel_multiplier=1).then_inc(near_p, 1)
                pool.wait_ge(near_p, NT + 2 * qb + 1)
                pool.affine_select(out=view, in_=view, compare_op=ALU.is_ge, fill=MASKED, base=WINDOW + gap,
                                   pattern=[[1, nk * P]], channel_multiplier=-1).then_inc(near_p, 1)
            w_split_hi(C_Q // 2, 1, W_COLS)

            pool.wait_ge(near_p, 3 * NT)
            pool.wait_ge(pool_consts, 2 + HEADS)
            pool.wait_ge(vec_consts, 6)

            def a_group(g, last=False):
                wait(pool, s_free, S_A + 16 * g)
                pool.tensor_copy(par[:], par_all[:, g, :]).then_inc(par_ready, 1)
                wait(pool, par_ready, g + 1)
                wait(pool, pt_done, T_A + A_TG * g)
                for b in range(2):
                    pool.tensor_copy(s_a[:, b, :, 0:1], par[:, HG:2 * HG].unsqueeze(2)).then_inc(sinkcol_ready, 1)

                def make_bias(u):
                    nk = A_KB[u // HG][1]
                    if u >= 2:
                        wait(pool, s_free, S_A + 16 * g + u - 1)
                    pool.tensor_scalar(bias[:, u % 2, 0:nk * P], near[:, u // HG, 0:nk * P],
                                       par[:, u % HG:u % HG + 1], 1.0, ALU.mult, ALU.mult).then_inc(bias_ready, 1)

                make_bias(0)
                for u in range(16):
                    n, hd = u // HG, u % HG
                    nk = A_KB[n][1]
                    if u + 2 < 16 and u % 2 == 0:
                        make_bias(u + 2)
                    wait(pool, rsum_ready, 16 * g + u + 1)
                    view = s_a[:, n % 2, hd, 1:1 + nk * P]
                    pool.tensor_scalar(view, view, stat[:, 2, u % 8:u % 8 + 1], 1.0, ALU.mult, ALU.mult) \
                        .then_inc(p_ready, 1)
                    if u == 3:
                        w_split_hi(C_Q // 2 + 1 + g, 1, W_COLS)
                    if u == 12 and not last:
                        w_split_hi(C_Q // 2 + 2 + g, 0, W_COLS)

            w_split_hi(C_Q // 2 + 1, 0, W_COLS)
            with pool.Fori(0, GROUPS - 1) as g:
                a_group(g)
            a_group(GROUPS - 1, last=True)

            def wo_phase(n, c0):
                for s in range(2):
                    w_split_hi(c0 // 2 + 1, s, W_COLS)
                    sum_squares(n, s, s, first=s == 0)
                with pool.Fori(1, KD // 2) as i:
                    for s in range(2):
                        w_split_hi(c0 // 2 + 1 + i, s, W_COLS)
                        sum_squares(n, 2 * i + s, s)

            def ffn_half(layer, half, n, next_cols):
                c2 = ((C_FFN0, C_FFN1)[layer] + half * C_HALF) // 2
                j0 = (2 * layer + half) * HALF

                def hidden(j, cols, first=False, second=False):
                    if not second:
                        w_split_hi(c2 + j + 1, 0, cols)
                    if first:
                        w_split_hi(c2 + j + 1, 1, cols)
                        w_split_hi(c2 + j + 2, 0, cols)
                    if second:
                        w_split_hi(c2 + j + 1, 1, cols)
                    wait(pool, silu_ready, j0 + j + 1)
                    pool.tensor_tensor(gate_s[:], gate_s[:], rs_t[:], ALU.mult).then_inc(silu_rs_ready, 1)
                    if not (first or second):
                        w_split_hi(c2 + j + 1, 1, cols)

                hidden(0, W_COLS, first=half == 0)
                hidden(1, W_COLS, second=half == 0)
                with pool.Fori(2, HALF - 1) as j:
                    hidden(j, W_COLS)
                hidden(HALF - 1, W_DOWN)

                def pair(i, cols, first=False):
                    for s in range(2):
                        if cols:
                            w_split_hi(c2 + HALF + 1 + i, s, cols)
                        if n is not None:
                            sum_squares(n, 2 * i + s, s, first=first and s == 0)

                pair(0, W_DOWN, first=True)
                with pool.Fori(1, KD // 2 - 1) as i:
                    pair(i, W_DOWN)
                pair(KD // 2 - 1, next_cols)

            wo_phase(norms[1], C_WOA)
            ffn_half(0, 0, None, W_COLS)
            pool.wait_ge(pos_in, 16)
            for i in range(ROPE // 2):
                pool.memset(inv_f[:, i:i + 1], float(INV_FREQ[i])).then_inc(pool_consts, 1)
            ffn_half(0, 1, norms[2], W_LAT)

            w_split_hi(C_LAT // 2 + 1, 0, W_LAT)
            w_split_hi(C_LAT // 2 + 1, 1, W_LAT)
            w_split_hi(C_B // 2, 0, W_UQ)
            w_split_hi(C_B // 2, 1, W_UKV, kv=True)
            pool.wait_ge(lrs_step, LRS_KV)
            for t in range(NT):
                view = lat[:, t, QL:QL + KVL]
                pool.tensor_scalar(view, view, lat_stat[:, 2, NT + t:NT + t + 1], 1.0, ALU.mult, ALU.mult) \
                    .then_inc(latn_ready, 1)
            pool.wait_ge(pt_free, T_BPRE + 6)
            pool.wait_ge(latn_ready, NT)
            for hd in (2, 3):
                pool.tensor_scalar(bk_hi[NOPE:QK, hd, :], krope_t[NOPE:QK, :], 1.0, 1.0, ALU.mult, ALU.mult) \
                    .then_inc(krope_pool, 1)
            for hd in (2, 3):
                pool.wait_ge(krope_pool, hd - 1)
                pool.tensor_tensor(bk_lo[NOPE:QK, hd, :], krope_t[NOPE:QK, :], f(bk_hi[NOPE:QK, hd, :]),
                                   ALU.subtract).then_inc(krope_pool, 1)
            pool.wait_ge(krope_pool, 4)

            def b_group(g, cols0, cols1):
                for u in range(16):
                    wait(pool, rsum_ready, 16 * (GROUPS + g) + u + 1)
                    view = s_b[:, u // 4 % 2, u % 4, :]
                    pool.tensor_scalar(view, view, stat[:, 2, u % 8:u % 8 + 1], 1.0, ALU.mult, ALU.mult) \
                        .then_inc(p_ready, 1)
                    if u == 3:
                        w_split_hi(C_B // 2 + 1 + g, 0, cols0)
                    if u == 7:
                        w_split_hi(C_B // 2 + 1 + g, 1, cols1, kv=cols0 == W_UQ)

            with pool.Fori(0, GROUPS - 1) as g:
                b_group(g, W_UQ, W_UKV)
            b_group(GROUPS - 1, W_COLS, W_COLS)

            wo_phase(norms[3], C_WOB)
            ffn_half(1, 0, None, W_COLS)
            ffn_half(1, 1, norms[4], 0)

        @block.scalar
        def _(act):
            def split_x(n, m, b, src=None):
                src = h[:, m, :] if src is None else src
                wait(act, n.block_sem, n.block_base + m + 1)
                if n.gain is not None:
                    act.activation(x_hi[:, m, :], src, ACT.Copy, scale=gains[:, n.gain, m, :]) \
                        .then_inc(x_hi_ready, 1)
                if n.number or not isinstance(m, int):
                    wait(act, ss_ready, n.base + m - 1)
                act.activation(n.sq[:, b, :], src, ACT.Square).then_inc(sq_ready, 1)

            def rms(n):
                act.wait_ge(ms_ready, n.number + 1)
                act.activation(ms_n[:, 1, :], ms_n[:, 0, :], ACT.Sqrt).then_inc(rms_n, 1)

            act.wait_ge(gain_in, 16)
            for s in range(2):
                split_x(norms[0], s, s)
            with act.Fori(1, KD // 2) as i:
                for s in range(2):
                    split_x(norms[0], 2 * i + s, s)
            rms(norms[0])
            act.wait_ge(w_used, C_V + 2)
            act.wait_ge(rs_n_ready, 1)
            for t in range(NT):
                act.activation(v_all[:, t, :], banks[t][:, 0:GROUPS * HD], ACT.Copy, scale=rs_n[:, 2 * t:2 * t + 1]) \
                    .then_inc(s_free, 16 // NT)

            def a_k_hi(g, first=False):
                if not first:
                    wait(act, s_done, 16 * g)
                for b in range(2):
                    act.activation(kp_hi[b * HD:(b + 1) * HD, b, :], k_dup[b * HD:(b + 1) * HD, g, :], ACT.Copy) \
                        .then_inc(kp_hi_ready, 1)

            v_by_group = v_all[:].rearrange("p t (g d) -> p t g d", g=GROUPS)

            def a_v_hi(g, first=False):
                if not first:
                    wait(act, o_done, 4 * g)
                act.activation(av_hi[:, :, HD:2 * HD], v_by_group[:, :, g, :], ACT.Copy).then_inc(v_hi_ready, 1)

            def a_q_hi(g, i, first=False):
                if not first:
                    wait(act, s_done, 16 * g)
                wait(act, proj_free, U_Q + 2 * g + i + 1)
                act.activation(aq_hi[:, i, :], q_tmp[:], ACT.Copy).then_inc(q_hi_ready, 1)

            act.wait_ge(k_dup_ready, 6)
            act.wait_ge(proj_free, U_Q)
            a_k_hi(0, first=True)
            a_q_hi(0, 0, first=True)
            a_q_hi(0, 1, first=True)
            act.wait_ge(s_free, S_A)
            a_v_hi(0, first=True)
            def a_group(g, last):
                def expo(u):
                    n, hd = u // HG, u % HG
                    if u == 0:
                        wait(act, sinkcol_ready, 2 * g + 2)
                    (wait if u else wait_on)(act, s_free, S_A + 16 * g + u + 1)
                    view = s_a[:, n % 2, hd, 0:1 + A_KB[n][1] * P]
                    act.activation(view, view, ACT.Exp, scale=-1.0, bias=stat[:, 0, u % 8:u % 8 + 1],
                                   accum_out=stat[:, 1, u % 8:u % 8 + 1]).then_inc(exp_ready, 1)

                def odd_bias(u):
                    nk = A_KB[u // HG][1]
                    if u == 1:
                        wait(act, par_ready, g + 1)
                    else:
                        wait(act, s_free, S_A + 16 * g + u - 1)
                    act.activation(bias[:, 1, 0:nk * P], near[:, u // HG, 0:nk * P], ACT.Copy,
                                   scale=par[:, u % HG:u % HG + 1]).then_inc(bias_odd_ready, 1)

                def pt_hi(n, i):
                    unit = T_A + A_T0[n] + i
                    wait(act, pt_done, unit + A_TG * g + 1)
                    act.activation(apt_hi[:, n % 2, i, :], banks[3 + unit % 2][:], ACT.Copy).then_inc(pt_hi_ready, 1)

                def o_hi(n):
                    wait(act, o_done, 4 * g + n + 1)
                    act.activation(ot_hi_q[:, g, :, n, :], banks[5][:, 0:2 * P].rearrange("p (a q) -> p a q", a=2),
                                   ACT.Copy).then_inc(o_hi_ready, 1)

                odd_bias(1)
                expo(0)
                expo(1)
                odd_bias(3)
                expo(2)
                expo(3)
                odd_bias(5)
                for n in range(NT):
                    if n < 3:
                        expo(4 * n + 4)
                        expo(4 * n + 5)
                        odd_bias(4 * n + 7)
                        expo(4 * n + 6)
                        pt_hi(n, 0)
                        expo(4 * n + 7)
                        if n < 2:
                            odd_bias(4 * n + 9)
                        pt_hi(n, 1)
                        if n:
                            o_hi(n - 1)
                        if A_KB[n][1] > 2:
                            pt_hi(n, 2)
                    else:
                        if not last:
                            a_q_hi(g + 1, 0)
                            a_k_hi(g + 1)
                        pt_hi(n, 0)
                        o_hi(n - 1)
                        pt_hi(n, 1)
                if not last:
                    a_q_hi(g + 1, 1)
                o_hi(3)
                if not last:
                    a_v_hi(g + 1)

            ot_hi_q = ot_hi[:].rearrange("p (g a) (n q) -> p g a n q", a=2, n=NT)
            with act.Fori(0, GROUPS - 1) as g:
                a_group(g, False)
            a_group(GROUPS - 1, True)

            def wo_phase(n):
                with act.Fori(0, KD // 2) as i:
                    for s in range(2):
                        split_x(n, 2 * i + s, s)
                rms(n)

            def ffn_half(layer, half, n):
                u0 = (U_FFN0, U_FFN1)[layer] + half * C_HALF
                j0 = (2 * layer + half) * HALF
                with act.Fori(0, HALF) as j:
                    wait(act, proj_free, u0 + 2 * j + 1)
                    act.activation(gate_s[:], gate_t[:], ACT.Silu).then_inc(silu_ready, 1)
                    wait(act, proj_free, u0 + 2 * j + 2)
                    act.activation(f_hi[:, j, :], hid[:], ACT.Copy).then_inc(f_hi_ready, 1)
                if n is not None:
                    with act.Fori(0, KD // 2) as i:
                        for s in range(2):
                            split_x(n, 2 * i + s, s, h_fin[:, s, :] if n.gain is None else None)

            wo_phase(norms[1])
            ffn_half(0, 0, None)
            act.wait_ge(tab_v, TAB_STEPS)
            act.activation(half_sin[:], ang[:], ACT.Sin, scale=0.5).then_inc(tab_a, 1)
            act.activation(sin_n[:, :, 16:32], ang[:], ACT.Sin).then_inc(tab_a, 1)
            ffn_half(0, 1, norms[2])

            for t in range(NT):
                if t == 2:
                    rms(norms[2])
                if t < NT - 1:
                    act.wait_ge(lat_done, t + 1)
                else:
                    act.wait_ge(w_used, C_LAT + 4)
                act.activation(lat[:, t, 0:QL], banks[2 * t][:, 0:QL], ACT.Copy).then_inc(lat_q_ready, 1)

            def b_pt_hi(unit, dst, scale):
                wait(act, pt_done, unit + 1)
                act.activation(dst, lat_banks[unit - T_BPRE][:], ACT.Copy, scale=scale).then_inc(pt_hi_ready, 1)

            b_pt_hi(T_BPRE, cq_hi[:, 0, :], g_q[:, 0:1])
            b_pt_hi(T_BPRE + 1, cq_hi[:, 1, :], g_q[:, 1:2])
            b_pt_hi(T_BPRE + 2, cq_hi[:, 2, :], g_q[:, 2:3])
            act.wait_ge(lat_q_ready, NT)
            for t in range(NT):
                if t:
                    act.wait_ge(lsq_ready, t)
                act.activation(lat_sq[:], lat[:, t, 0:QL], ACT.Square, scale=QL ** -0.5,
                               accum_out=lat_stat[:, 0, t:t + 1]).then_inc(lsq_ready, 1)
            act.wait_ge(lrs_step, 2)
            act.activation(lat_stat[:, 1, :], lat_stat[:, 0, :], ACT.Sqrt).then_inc(lrms_ready, 1)

            def b_q_out(g, t):
                if t == 0 and not (isinstance(g, int) and g == 0):
                    wait(act, pt_done, T_B + B_TG * (g - 1))
                wait(act, proj_done, U_BG * g + t + 1)
                act.activation(q_n[:, t, :], banks[6 + t % 2][:, 0:HG * QK], ACT.Copy,
                               scale=q_scale[:, t:t + 1]).then_inc(proj_free, 1)

            def b_k_hi(g, i):
                wait(act, proj_done, U_BG * g + 4 + i + 1)
                for b in range(2):
                    act.activation(bk_hi[0:NOPE, 2 * i + b, :], banks[6 + i][b * HD:(b + 1) * HD, :], ACT.Copy) \
                        .then_inc(kp_hi_ready, 1)

            def b_q_hi(hd, base):
                wait(act, pt_done, base + hd + 1)
                act.activation(bq_hi[0:QK, hd, :], banks[3 + hd % 2][0:QK, :], ACT.Copy).then_inc(pt_hi_ready, 1)

            bv_hi_v = bv_hi[:].rearrange("p t a (s d) -> p (t a) s d", d=HD)

            def b_v_hi(g, i):
                wait(act, o_done, 4 * GROUPS + 2 * g)
                wait(act, proj_done, U_BG * g + 6 + i + 1)
                act.activation(bv_hi_v[:, 4 * i:4 * i + 4, ::2, :],
                               banks[6 + i][:].rearrange("p (t s d) -> p t s d", t=4, s=2), ACT.Copy) \
                    .then_inc(v_hi_ready, 1)

            act.wait_ge(lrs_step, LRS_Q)
            for t in range(3):
                b_q_out(0, t)
            for b in range(KVL // P):
                b_pt_hi(T_BPRE + 3 + b, ckv_hi[:, b, :], g_kv[:, b:b + 1])
            b_q_out(0, 3)
            act.wait_ge(pt_free, T_BPRE + 6)
            act.activation(bk_hi[NOPE:QK, 0, :], krope_t[NOPE:QK, :], ACT.Copy).then_inc(pt_hi_ready, 1)
            b_q_hi(0, T_BPRE + 6)
            b_q_hi(1, T_BPRE + 6)
            b_k_hi(0, 0)
            act.activation(bk_hi[NOPE:QK, 1, :], krope_t[NOPE:QK, :], ACT.Copy).then_inc(krope_hi, 1)
            b_q_hi(2, T_BPRE + 6)
            b_k_hi(0, 1)
            b_q_hi(3, T_BPRE + 6)
            act.wait_ge(vec_consts, 8)
            act.wait_ge(krope_pool, 4)

            def b_group(g, last):
                def expo(u):
                    n = u // 4
                    if u >= 8:
                        wait(act, pt_done, T_B + B_TG * g + 4 * (n - 1))
                    elif isinstance(g, int) and g == 0:
                        pass
                    else:
                        wait(act, pt_done, T_B + B_TG * g)
                    (wait if u else wait_on)(act, max_ready, 16 * g + u + 1)
                    act.activation(s_b[:, n % 2, u % 4, :], banks[u % 3][:], ACT.Exp, bias=stat[:, 0, u % 8:u % 8 + 1],
                                   accum_out=stat[:, 1, u % 8:u % 8 + 1]).then_inc(exp_ready, 1)

                def pt_hi(n, i):
                    wait(act, pt_done, T_B + B_TG * g + 4 * n + i + 1)
                    act.activation(bpt_hi[:, n % 2, i, :], banks[3 + i % 2][:], ACT.Copy).then_inc(pt_hi_ready, 1)

                def o_hi(pair):
                    wait(act, o_done, 4 * GROUPS + 2 * g + pair + 1)
                    act.activation(ot_hi[:, 2 * g + pair, :], banks[5][:], ACT.Copy).then_inc(o_hi_ready, 1)

                expo(0)
                expo(1)
                expo(2)
                expo(3)
                for n in range(HG):
                    if n < 3:
                        expo(4 * n + 4)
                        expo(4 * n + 5)
                        expo(4 * n + 6)
                        if n == 0:
                            expo(7)
                            b_v_hi(g, 0)
                        pt_hi(n, 0)
                        if n:
                            expo(4 * n + 7)
                        for i in range(1, 4):
                            if n == 0 and i == 2:
                                b_v_hi(g, 1)
                            if n == 2 and i < 3 and not last:
                                b_q_out(g + 1, i - 1)
                            pt_hi(n, i)
                        if n == 2:
                            o_hi(0)
                    else:
                        if not last:
                            b_q_out(g + 1, 2)
                            b_q_out(g + 1, 3)
                        for i in range(4):
                            pt_hi(n, i)
                            if i % 2 == 0 and not last:
                                b_k_hi(g + 1, i // 2)
                        if not last:
                            for hd in range(HG):
                                b_q_hi(hd, T_B + B_TG * g + 16)
                        o_hi(1)

            with act.Fori(0, GROUPS - 1) as g:
                b_group(g, False)
            b_group(GROUPS - 1, True)

            wo_phase(norms[3])
            ffn_half(1, 0, None)
            ffn_half(1, 1, norms[4])
            rms(norms[4])
            act.wait_ge(rs_n_ready, 5)
            act.wait_ge(pt_free, T_FIN + KD)
            for t in (1, 3):
                act.activation(out_n[:, t, :], out_n[:, t, :], ACT.Copy, scale=rs_n[:, 2 * t:2 * t + 1]) \
                    .then_inc(out_ready[1], 1)

        @block.tensor
        def _(pe):
            def product(o, lh, ll, rh, rl, start, stop):
                pe.matmul(o, ll, rh, start=start, stop=False)
                pe.matmul(o, lh, rl, start=False, stop=False)
                return pe.matmul(o, lh, rh, start=False, stop=stop)

            def w_block(s, cols, k):
                return w_hi[s][:, k * cols:(k + 1) * cols], w_lo[s][:, k * cols:(k + 1) * cols]

            def project(c2, s, unit, unit_base, src_hi, src_lo, blocks=KD, ready=None):
                pe.wait_ge(w_ready, 2 * c2 + s + 1)
                if not (isinstance(unit_base, int) and unit + unit_base < 2):
                    pe.wait_ge(proj_free, unit_base + unit - 1)
                for k in range(blocks):
                    if ready is not None:
                        pe.wait_ge(*ready(k))
                    wh, wl = w_block(s, P, k)
                    last = product(banks[6 + unit % 2][:], wh, wl, src_hi[:, k, :], src_lo[:, k, :],
                                   k == 0, k == blocks - 1)
                last.then_inc(w_used, 1)

            def wo_part(c0, u0, s, ks):
                if ks[0] == 0:
                    pe.wait_ge(w_ready, c0 + s + 1)
                    pe.wait_ge(proj_free, u0 + s - 1)
                    pe.wait_ge(o_free, O_A + 4 * (GROUPS - 1) if c0 == C_WOA else O_B + 2 * (GROUPS - 1))
                for k in ks:
                    wh, wl = w_block(s, P, k)
                    last = product(banks[6 + s][:], wh, wl, ot_hi[:, k, :], ot_lo[:, k, :], k == 0, k == KD - 1)
                if ks[-1] == KD - 1:
                    last.then_inc(w_used, 1)

            def sum_partitions(n):
                pe.wait_ge(ss_ready, n.base + KD)
                for t in range(NT):
                    last = pe.matmul(n.sums[:, 2 * t:2 * t + 2], n.ss[:, t * P:(t + 1) * P], ones[:],
                                     start=True, stop=True)
                last.then_inc(st_done, 1)

            def spread(n):
                pe.wait_ge(rs_n_ready, n.number + 1)
                if n.o_index:
                    pe.wait_ge(o_free, n.o_index)
                for t in range(NT):
                    last = pe.transpose(banks[5][:, t * P:(t + 1) * P],
                                        rs_n[:, 2 * t:2 * t + 1].to_broadcast([P, P]), ident[:])
                last.then_inc(rs_spread, 1)

            pe.wait_ge(pool_consts, 2)

            def k_block(k):
                for s in range(2):
                    if k == 0:
                        pe.wait_ge(w_ready, s + 1)
                    pe.wait_ge(x_ready, k + 1)
                    wh, wl = w_block(s, P, k)
                    last = product(banks[6 + s][:], wh, wl, x_hi[:, k, :], x_lo[:, k, :], k == 0, k == KD - 1)
                    if k == KD - 1:
                        last.then_inc(w_used, 1)

            for m in range(KD):
                if m >= 6:
                    pe.wait_ge(pt_free, m - 5)
                for t in range(NT):
                    if m == 0:
                        pe.wait_ge(x_in[t], 16)
                    last = pe.transpose(banks[m % 6][:, t * P:(t + 1) * P], x_n[:, t, m * P:(m + 1) * P], ident[:])
                last.then_inc(pt_done, 1)
                if m >= 5:
                    k_block(m - 5)
            for k in range(3, KD):
                k_block(k)
            pe.wait_ge(vec_consts, 5)

            pe.wait_ge(pt_free, KD)
            for s in range(2):
                pe.wait_ge(w_ready, C_V + s + 1)
                for t in range(NT):
                    if s == 0 and t == 2:
                        sum_partitions(norms[0])
                    if s == 1 and t == 1:
                        spread(norms[0])
                    for k in range(4):
                        if s == 0:
                            cols = slice(k * GROUPS * HD, (k + 1) * GROUPS * HD)
                            wh, wl = v0_hi[:, cols], v0_lo[:, cols]
                        else:
                            wh, wl = w_block(s, GROUPS * HD, k)
                        xk = (4 * s + k, slice(t * P, (t + 1) * P))
                        last = product(banks[t][:, 0:GROUPS * HD], x_hi[:, xk[0], xk[1]], x_lo[:, xk[0], xk[1]],
                                       wh, wl, s == 0 and k == 0, s == 1 and k == 3)
                last.then_inc(w_used, 1)

            def a_q(g, i):
                project(C_Q // 2 + g, i, i, U_Q + 2 * g, x_hi, x_lo)

            def a_q_part(g, ks):
                if ks[0] == 0:
                    pe.wait_ge(w_ready, C_Q + 2 * g + 2)
                    pe.wait_ge(proj_free, U_Q + 2 * g)
                for k in ks:
                    wh, wl = w_block(1, P, k)
                    last = product(banks[7][:], wh, wl, x_hi[:, k, :], x_lo[:, k, :], k == 0, k == KD - 1)
                if ks[-1] == KD - 1:
                    last.then_inc(w_used, 1)

            a_q(0, 0)
            a_q(0, 1)

            def a_group(g, last):
                def scores(u):
                    n, hd = u // HG, u % HG
                    k0, nk = A_KB[n]
                    before = 16 * g + (u - 2 if u >= 3 else (0, -2, -1)[u])
                    pe.wait_ge(s_free, S_A + before)
                    q = (slice(None), hd // 2, slice(n * P, (n + 1) * P))
                    k = (slice(None), hd % 2, slice(k0 * P, (k0 + nk) * P))
                    product(banks[u % 3][:, 0:nk * P], aq_hi[q], aq_lo[q], kp_hi[k], kp_lo[k], True, True) \
                        .then_inc(s_done, 1)

                def transposes(n, i):
                    unit = T_A + A_T0[n] + i
                    pe.wait_ge(pt_free, A_TG * g + unit - 1)
                    for j, hd in enumerate((0, 2, 1, 3)):
                        if i == 0:
                            pe.wait_ge(p_ready, 16 * g + 4 * n + (hd + 1 if j != 2 else 3))
                        last_ = pe.transpose(banks[3 + unit % 2][:, j * P:(j + 1) * P],
                                             s_a[:, n % 2, hd, 1 + i * P:1 + (i + 1) * P], ident[:])
                    last_.then_inc(pt_done, 1)

                def values(n):
                    k0, nk = A_KB[n]
                    pe.wait_ge(pt_free, T_A + A_TG * g + A_T0[n] + nk)
                    pe.wait_ge(o_free, O_A + 4 * g + n)
                    if n == 0:
                        pe.wait_ge(v_ready, g + 1)
                    for i in range(nk):
                        for odd in range(2):
                            v = (slice(None), k0 + i, slice(0, P) if odd else slice(HD, HD + P))
                            p = (slice(None), n % 2, i, slice(2 * P * odd, 2 * P * (odd + 1)))
                            last_ = product(banks[5][:, 0:2 * P], av_hi[v], av_lo[v], apt_hi[p], apt_lo[p],
                                            i == 0 and odd == 0, i == nk - 1 and odd == 1)
                    last_.then_inc(o_done, 1)

                pe.wait_ge(kp_ready, 2 * g + 2)
                pe.wait_ge(q_ready, 2 * g + 1)
                scores(0)
                scores(1)

                def next_q(ks):
                    if last:
                        if ks[-1] < 6:
                            wo_part(C_WOA, U_WOA, 0, ks)
                        else:
                            wo_part(C_WOA, U_WOA, 1, (0, 1))
                        return
                    if ks[0] == 0:
                        pe.wait_ge(w_ready, C_Q + 2 * g + 3)
                        pe.wait_ge(proj_free, U_Q + 2 * g + 1)
                    for k in ks:
                        wh, wl = w_block(0, P, k)
                        last_ = product(banks[6][:], wh, wl, x_hi[:, k, :], x_lo[:, k, :], k == 0, k == KD - 1)
                    if ks[-1] == KD - 1:
                        last_.then_inc(w_used, 1)

                next_q((0, 1))
                pe.wait_ge(q_ready, 2 * g + 2)
                scores(2)
                scores(3)
                for n in range(NT):
                    if n < 3:
                        if n == 0:
                            next_q((2,))
                        scores(4 * n + 4)
                        scores(4 * n + 5)
                        if n == 0:
                            next_q((3,))
                        scores(4 * n + 6)
                        scores(4 * n + 7)
                        next_q(((4,), (5,), (6, 7))[n])
                        transposes(n, 0)
                        transposes(n, 1)
                        if n:
                            values(n - 1)
                        if A_KB[n][1] > 2:
                            transposes(n, 2)
                    else:
                        if not last:
                            a_q_part(g + 1, range(0, KD // 2))
                        transposes(n, 0)
                        values(n - 1)
                        transposes(n, 1)
                        if last:
                            wo_part(C_WOA, U_WOA, 1, (2, 3))
                        else:
                            a_q_part(g + 1, range(KD // 2, KD))
                values(3)
                if last:
                    wo_part(C_WOA, U_WOA, 1, (4, 5))

            with pe.Fori(0, GROUPS - 1) as g:
                a_group(g, False)
            a_group(GROUPS - 1, True)

            def wo_phase(c0, u0, o_count):
                pe.wait_ge(o_free, o_count)
                for s in range(2):
                    wo_part(c0, u0, s, (6, 7))
                with pe.Fori(1, KD // 2) as i:
                    for s in range(2):
                        project(c0 // 2 + i, s, s, u0 + 2 * i, ot_hi, ot_lo)

            def ffn_half(layer, half, n, fin=None):
                c2 = ((C_FFN0, C_FFN1)[layer] + half * C_HALF) // 2
                u0 = (U_FFN0, U_FFN1)[layer] + half * C_HALF
                j0 = (2 * layer + half) * HALF
                if n is not None:
                    def part(c, bank, blocks):
                        if blocks[0] == 0:
                            pe.wait_ge(w_ready, 2 * c2 + c + 1)
                            pe.wait_ge(proj_free, u0 if bank >= 6 else u0 - 1)
                        for k in blocks:
                            pe.wait_ge(x_ready, n.base + k + 1)
                            wh, wl = w_block(c % 2, P, k)
                            last = product(banks[bank][:], wh, wl, x_hi[:, k, :], x_lo[:, k, :],
                                           k == 0, k == KD - 1)
                        return last

                    part(0, 0, range(KD - 1))
                    part(1, 1, range(KD - 3))
                    part(0, 0, [KD - 1]).then_inc(w_used, 1)
                    sum_partitions(n)
                    part(1, 1, [KD - 3, KD - 2, KD - 1]).then_inc(w_used, 1)
                    part(2, 6, range(KD // 2))
                    spread(n)
                    part(2, 6, range(KD // 2, KD)).then_inc(w_used, 1)
                    part(3, 7, range(KD)).then_inc(w_used, 1)
                else:
                    for j in range(2):
                        for s in range(2):
                            project(c2 + j, s, s, u0 + 2 * j, x_hi, x_lo)
                with pe.Fori(2, HALF) as j:
                    for s in range(2):
                        project(c2 + j, s, s, u0 + 2 * j, x_hi, x_lo)

                def down(i, s, first=False):
                    project(c2 + HALF + i, s, s, u0 + 2 * HALF + 2 * i, f_hi, f_lo, blocks=HALF,
                            ready=(lambda k: (f_ready, j0 + k + 1)) if first else None)

                def turn(m0, s):
                    pe.wait_ge(proj_free, U_DOWN1 + m0 + s + 1)
                    pe.wait_ge(pt_free, T_FIN + m0 + s - 1)
                    for t in range(NT):
                        last = pe.transpose(banks[3 + s][:, t * P:(t + 1) * P], h_fin[:, s, t * P:(t + 1) * P], ident[:])
                    last.then_inc(pt_done, 1)

                down(0, 0, first=True)
                down(0, 1)
                if fin:
                    turn(0, 0)
                with pe.Fori(1, KD // 2) as i:
                    down(i, 0)
                    if fin:
                        turn(2 * i - 2, 1)
                    down(i, 1)
                    if fin:
                        turn(2 * i, 0)
                if fin:
                    turn(KD - 2, 1)
                    sum_partitions(norms[4])

            wo_phase(C_WOA, U_WOA, O_A + 4 * GROUPS)
            ffn_half(0, 0, norms[1])
            ffn_half(0, 1, None)

            for c in range(4):
                pe.wait_ge(w_ready, C_LAT + c + 1)
                for t in range(NT):
                    if c == 0 and t == NT - 1:
                        pe.wait_ge(proj_free, U_B)
                    if c == 3 and t == 2:
                        pe.wait_ge(lat_q_ready, 1)
                        sum_partitions(norms[2])
                    for kk in range(2):
                        k = 2 * c + kk
                        if t == 0:
                            pe.wait_ge(x_ready, norms[2].base + k + 1)
                        wh, wl = w_block(c % 2, B_IN, kk)
                        xh, xl = x_hi[:, k, t * P:(t + 1) * P], x_lo[:, k, t * P:(t + 1) * P]
                        for half, (a, b) in enumerate(((0, QL), (QL, B_IN))):
                            last = product(banks[2 * t + half][:, 0:b - a], xh, xl, wh[:, a:b], wl[:, a:b],
                                           k == 0, k == KD - 1)
                    if c == 3 and t < NT - 1:
                        last.then_inc(lat_done, 1)
                last.then_inc(w_used, 1)

            def lat_turn(b, ts):
                for t in ts:
                    last = pe.transpose(lat_banks[b][:, t * P:(t + 1) * P], lat[:, t, b * P:(b + 1) * P], ident[:])
                if ts[-1] == NT - 1:
                    last.then_inc(pt_done, 1)

            pe.wait_ge(lat_q_ready, 3)
            pe.wait_ge(lat_kv_ready, 3)
            for b in range(QL // P):
                lat_turn(b, range(3))
            pe.wait_ge(lat_q_ready, NT)
            pe.wait_ge(lat_kv_ready, NT)
            for b in range(QL // P):
                lat_turn(b, (3,))

            def b_q(g, t, first=False):
                if t == 0:
                    pe.wait_ge(w_ready, C_B + 2 * g + 1)
                pe.wait_ge(proj_free, U_B + U_BG * g + t - 1)
                for k in range(QL // P):
                    if first:
                        pe.wait_ge(pt_free, T_BPRE + k + 1)
                    wh, wl = w_block(0, HG * QK, k)
                    ch, cl = cq_hi[:, k, t * P:(t + 1) * P], cq_lo[:, k, t * P:(t + 1) * P]
                    last = product(banks[6 + t % 2][:, 0:HG * QK], ch, cl, wh, wl, k == 0, k == QL // P - 1)
                last.then_inc(proj_done, 1)

            def b_k(g, i):
                if i == 0:
                    pe.wait_ge(w_ready, C_B + 2 * g + 2)
                pe.wait_ge(proj_free, U_B + U_BG * g + 4 + i - 1)
                for k in range(KVL // P):
                    wh, wl = (w[1][:, k * HG * HD + i * P:k * HG * HD + (i + 1) * P] for w in (w_hi, w_lo))
                    o = banks[6 + i][:]
                    first = pe.matmul(o, wl, ckv_hi[:, k, :], start=k == 0, stop=False)
                    if i == 0 and k == 0:
                        first.then_inc(w_used, 1)
                    pe.matmul(o, wh, ckv_lo[:, k, :], start=False, stop=False)
                    last = pe.matmul(o, wh, ckv_hi[:, k, :], start=False, stop=k == KVL // P - 1)
                last.then_inc(proj_done, 1)

            def b_v(g, i):
                pe.wait_ge(proj_free, U_B + U_BG * g + 6 + i - 1)
                for t in (2 * i, 2 * i + 1):
                    o = banks[6 + i][:, t % 2 * HG * HD:(t % 2 + 1) * HG * HD]
                    for k in range(KVL // P):
                        wh, wl = (w[1][:, W_UKV // 2 + k * HG * HD:W_UKV // 2 + (k + 1) * HG * HD]
                                  for w in (w_hi, w_lo))
                        ch, cl = ckv_hi[:, k, t * P:(t + 1) * P], ckv_lo[:, k, t * P:(t + 1) * P]
                        last = product(o, ch, cl, wh, wl, k == 0, k == KVL // P - 1)
                last.then_inc(proj_done, 1)

            def b_turn_q(g, base, hd):
                if hd == 0:
                    pe.wait_ge(rope_v, 8 * g + 12)
                pe.wait_ge(pt_free, base + hd - 1)
                for t in range(NT):
                    last = pe.transpose(banks[3 + hd % 2][0:QK, t * P:(t + 1) * P],
                                        q_n[:, t, hd * QK:(hd + 1) * QK], ident[:])
                last.then_inc(pt_done, 1)

            for t in range(3):
                b_q(0, t, first=t == 0)
            pe.wait_ge(latn_ready, NT)
            for b in (3, 4):
                pe.wait_ge(pt_free, T_BPRE + b - 1)
                lat_turn(b, range(NT))
            b_q(0, 3)
            pe.wait_ge(rope_v, 4)
            pe.wait_ge(pt_free, T_BPRE + 4)
            for t in range(NT):
                last = pe.transpose(banks[4][0:ROPE, t * P:(t + 1) * P], lat[:, t, QL + KVL:B_IN], ident[:])
            last.then_inc(pt_done, 1)
            pe.wait_ge(pt_free, T_BPRE + 5)
            for i in range(2):
                b_k(0, i)
                for hd in (2 * i, 2 * i + 1):
                    b_turn_q(0, T_BPRE + 6, hd)
            pe.wait_ge(krope_ready, 2)
            pe.wait_ge(krope_pool, 4)

            def b_group(g, last):
                def scores(u):
                    n, qb = u // 4, u % 4
                    if qb == 0:
                        pe.wait_ge(pt_free, T_B + B_TG * g - HG + n + 1)
                        if n % 2 == 0:
                            pe.wait_ge(proj_free, U_B + U_BG * g + 5 + n // 2)
                    before = 16 * g + (u - 2 if u >= 3 else (0, -2, -1)[u])
                    pe.wait_ge(exp_ready, S_B - S_A + before)
                    q = (slice(0, QK), n, slice(qb * P, (qb + 1) * P))
                    k = (slice(0, QK), n, slice(None))
                    product(banks[u % 3][:], bq_hi[q], bq_lo[q], bk_hi[k], bk_lo[k], True, True).then_inc(s_done, 1)

                def transposes(n, i):
                    pe.wait_ge(pt_free, T_B + B_TG * g + 4 * n + i - 1)
                    for qb in range(NT):
                        if i == 0:
                            pe.wait_ge(p_ready, 16 * (GROUPS + g) + 4 * n + qb + 1)
                        last_ = pe.transpose(banks[3 + i % 2][:, qb * P:(qb + 1) * P],
                                             s_b[:, n % 2, qb, i * P:(i + 1) * P], ident[:])
                        if n == 0 and i == 3 and qb == 0:
                            last_.then_inc(w_used, 1)
                    last_.then_inc(pt_done, 1)

                def values(n, i):
                    if i == 0:
                        pe.wait_ge(pt_free, T_B + B_TG * g + 4 * n + 4)
                        if n == 0:
                            pe.wait_ge(proj_free, U_B + U_BG * g + U_BG)
                    if i == 0 and n % 2 == 0:
                        pe.wait_ge(o_free, O_B + 2 * g + n // 2)
                    v = (slice(None), i, n // 2, slice(HD, HD + P) if n % 2 else slice(0, P))
                    p = (slice(None), n % 2, i, slice(None))
                    last_ = product(banks[5][:], bv_hi[v], bv_lo[v], bpt_hi[p], bpt_lo[p],
                                    n % 2 == 0 and i == 0, n % 2 == 1 and i == NT - 1)
                    if n % 2 and i == NT - 1:
                        last_.then_inc(o_done, 1)

                scores(0)
                scores(1)
                scores(2)
                scores(3)
                for n in range(HG):
                    if n < 3:
                        scores(4 * n + 4)
                        scores(4 * n + 5)
                        scores(4 * n + 6)
                        scores(4 * n + 7)
                        if n and not last:
                            b_q(g + 1, n - 1)
                        if n == 2 and last:
                            wo_part(C_WOB, U_WOB, 0, (0, 1, 2))
                        for i in range(NT):
                            if n == 0 and i % 2 == 0:
                                b_v(g, i // 2)
                            transposes(n, i)
                            if n:
                                values(n - 1, i)
                        if n == 2 and last:
                            wo_part(C_WOB, U_WOB, 0, (3, 4, 5))
                        elif n == 2:
                            b_q(g + 1, 2)
                    else:
                        if last:
                            wo_part(C_WOB, U_WOB, 1, (0, 1))
                        else:
                            b_q(g + 1, 3)
                        for i in range(NT):
                            transposes(n, i)
                            values(2, i)
                            if i == 2 and last:
                                wo_part(C_WOB, U_WOB, 1, (2, 3))
                            elif i % 2 == 0 and not last:
                                b_k(g + 1, i // 2)
                        for i in range(NT):
                            if not last:
                                b_turn_q(g + 1, T_B + B_TG * g + 16, i)
                            values(3, i)
                        if last:
                            wo_part(C_WOB, U_WOB, 1, (4, 5))

            with pe.Fori(0, GROUPS - 1) as g:
                b_group(g, False)
            b_group(GROUPS - 1, True)

            wo_phase(C_WOB, U_WOB, O_B + 2 * GROUPS)
            ffn_half(1, 0, norms[3])
            ffn_half(1, 1, None, fin=True)

        @block.vector
        def _(dve):
            def w_split_lo(c2, s, cols, kv=False):
                wait(dve, w_hi_ready, 2 * c2 + s + 1)
                dve.tensor_tensor(split_part(w_lo, s, cols, kv), raw_part(s, cols, kv), f(split_part(w_hi, s, cols, kv)),
                                  ALU.subtract) \
                    .then_inc(w_ready, 1)

            def w_half_lo(c2, s, cols, part, kv=False):
                if part == 0:
                    wait(dve, w_hi_ready, 2 * c2 + s + 1)
                    at = slice(0, cols // 2)
                else:
                    at = slice(cols // 2, cols)
                if kv:
                    raw = w_raw[s][:, 0:cols].rearrange("p (b c d) -> p b c d", c=2, d=HD)[:, :, part, :]
                    hi, lo = (w[s][:, at].rearrange("p (b d) -> p b d", d=HD) for w in (w_hi, w_lo))
                else:
                    raw, hi, lo = w_raw[s][:, at], w_hi[s][:, at], w_lo[s][:, at]
                ins = dve.tensor_tensor(lo, raw, f(hi), ALU.subtract)
                if part:
                    ins.then_inc(w_ready, 1)

            def split_x_lo(n, m):
                wait(dve, x_hi_ready, n.base + m + 1)
                dve.scalar_tensor_tensor(x_lo[:, m, :], h[:, m, :], gains[:, n.gain, m, :], f(x_hi[:, m, :]),
                                         ALU.mult, ALU.subtract).then_inc(x_ready, 1)

            steps = [0]

            def rs_stepped(ins):
                steps[0] += 1
                ins.then_inc(rs_step, 1)
                dve.wait_ge(rs_step, steps[0])

            def invert_n(n):
                dve.wait_ge(st_done, n.number + 1)
                dve.tensor_scalar(ms_n[:, 0, :], n.sums, 1.0 / D, EPS, ALU.mult, ALU.add).then_inc(ms_ready, 1)
                dve.wait_ge(rms_n, n.number + 1)
                rs_stepped(dve.reciprocal(rs_n[:], ms_n[:, 1, :]))
                rs_stepped(dve.tensor_tensor(ms_n[:, 2, :], ms_n[:, 0, :], rs_n[:], ALU.mult))
                rs_stepped(dve.scalar_tensor_tensor(ms_n[:, 2, :], ms_n[:, 2, :], -0.5, rs_n[:], ALU.mult, ALU.mult))
                dve.scalar_tensor_tensor(rs_n[:], ms_n[:, 2, :], 1.5, rs_n[:], ALU.add, ALU.mult) \
                    .then_inc(rs_n_ready, 1)

            def take_rs_t(n):
                dve.wait_ge(rs_spread, {0: 1, 1: 2, 3: 3}[n.number])
                dve.tensor_copy(rs_t[:], banks[5][:]).then_inc(o_free, 1)
                dve.wait_ge(o_free, n.o_index + 1)

            dve.memset(ones[:], 1.0).then_inc(vec_consts, 1)
            for t in (kp_hi, kp_lo, av_hi, av_lo):
                dve.memset(f(t[:]), 0.0).then_inc(vec_consts, 1)
            def read_x(m):
                dve.wait_ge(pt_done, m + 1)
                dve.tensor_copy(h[:, m, :], banks[m % 6][:]).then_inc(pt_free, 1)

            read_x(0)
            dve.wait_ge(gain_in, 16)
            for m in range(KD):
                if m + 1 < KD:
                    read_x(m + 1)
                split_x_lo(norms[0], m)
                if m < 2:
                    w_split_lo(0, m, W_COLS)
                if m == 4:
                    dve.wait_ge(w_hi_ready, C_V + 1)
                    dve.tensor_tensor(v0_lo[:], w_raw[0][:, 0:4 * GROUPS * HD], f(v0_hi[:]), ALU.subtract) \
                        .then_inc(w_ready, 1)
            w_split_lo(C_V // 2, 1, 4 * GROUPS * HD)
            invert_n(norms[0])
            w_split_lo(C_Q // 2, 0, W_COLS)
            dve.wait_ge(small_in, 8 * 16)
            dve.tensor_scalar(par_all[:, :, HG:], sink_in[:].rearrange("p (g h) -> p g h", g=GROUPS), -1.0, None,
                              ALU.mult).then_inc(vec_consts, 1)
            take_rs_t(norms[0])

            for m in range(2):
                dve.wait_ge(w_used, m + 1)
                for a in range(2):
                    rows = slice(a * HD, (a + 1) * HD)
                    for b in range(2):
                        ins = dve.tensor_tensor(k_dup[b * HD:(b + 1) * HD, 2 * m + a, :], banks[6 + m][rows, :],
                                                rs_t[rows, :], ALU.mult)
                        if a == 1 and b == 1:
                            ins.then_inc(proj_free, 1)
                        else:
                            ins.then_inc(k_dup_ready, 1)
                if m == 0:
                    for qb in range(NT):
                        nk = A_KB[qb][1]
                        dve.wait_ge(near_p, qb + 1)
                        view = near[:, qb, 0:nk * P]
                        dve.tensor_copy(view, dist_i[:, qb, 0:nk * P]).then_inc(near_v, 1)
                        dve.wait_ge(near_v, 2 * qb + 1)
                        dve.scalar_tensor_tensor(view, view, -1.0, view, ALU.mult, ALU.min).then_inc(near_v, 1)
            w_split_lo(C_Q // 2, 1, W_COLS)

            def a_k_lo(g):
                for b in range(2):
                    rows = slice(b * HD, (b + 1) * HD)
                    wait(dve, kp_hi_ready, 2 * g + b + 1)
                    dve.tensor_tensor(kp_lo[rows, b, :], k_dup[rows, g, :], f(kp_hi[rows, b, :]), ALU.subtract) \
                        .then_inc(kp_ready, 1)

            v_by_group = v_all[:].rearrange("p t (g d) -> p t g d", g=GROUPS)

            def a_v_lo(g):
                wait(dve, v_hi_ready, g + 1)
                dve.tensor_tensor(av_lo[:, :, HD:2 * HD], v_by_group[:, :, g, :], f(av_hi[:, :, HD:2 * HD]),
                                  ALU.subtract).then_inc(v_ready, 1)

            def a_q_out(g, i, first=False):
                wait(dve, w_used, C_Q + 2 * g + i + 1)
                if not (first and i == 0):
                    wait(dve, q_ready, 2 * g + i)
                dve.scalar_tensor_tensor(q_tmp[:], banks[6 + i][:], HD ** -0.5, rs_t[:], ALU.mult, ALU.mult) \
                    .then_inc(proj_free, 1)

            def a_q_lo(g, i):
                wait(dve, q_hi_ready, 2 * g + i + 1)
                dve.tensor_tensor(aq_lo[:, i, :], q_tmp[:], f(aq_hi[:, i, :]), ALU.subtract).then_inc(q_ready, 1)

            a_k_lo(0)
            for i in range(2):
                a_q_out(0, i, first=True)
                a_q_lo(0, i)
                if i == 0:
                    w_split_lo(C_Q // 2 + 1, 0, W_COLS)
            a_v_lo(0)

            ot_lo_q = ot_lo[:].rearrange("p (g a) (n q) -> p g a n q", a=2, n=NT)
            ot_hi_q = ot_hi[:].rearrange("p (g a) (n q) -> p g a n q", a=2, n=NT)

            def invert_sum(count, u):
                wait(dve, exp_ready, count)
                dve.reciprocal(stat[:, 2, u % 8:u % 8 + 1], stat[:, 1, u % 8:u % 8 + 1]).then_inc(rsum_ready, 1)

            def a_group(g, last):
                def read_scores(u):
                    n, hd = u // HG, u % HG
                    w = A_KB[n][1] * P
                    if u % 2:
                        wait(dve, bias_odd_ready, 8 * g + u // 2 + 1)
                    else:
                        wait(dve, bias_ready, 8 * g + u // 2 + 1)
                    wait(dve, s_done, 16 * g + u + 1)
                    if n >= 2:
                        wait(dve, pt_done, T_A + A_TG * g + A_T0[n - 1])
                    dve.tensor_tensor_reduce(s_a[:, n % 2, hd, 1:1 + w], bias[:, u % 2, 0:w], banks[u % 3][:, 0:w],
                                             -1.0, par[:, HG + hd:HG + hd + 1], ALU.add, ALU.min,
                                             stat[:, 0, u % 8:u % 8 + 1]).then_inc(s_free, 1)

                def pt_lo(n, i):
                    unit = T_A + A_T0[n] + i
                    wait(dve, pt_hi_ready, unit - T_A + A_TG * g + 1)
                    dve.tensor_tensor(apt_lo[:, n % 2, i, :], banks[3 + unit % 2][:], f(apt_hi[:, n % 2, i, :]),
                                      ALU.subtract).then_inc(pt_free, 1)

                def o_lo(n):
                    wait(dve, o_hi_ready, 4 * g + n + 1)
                    dve.tensor_tensor(ot_lo_q[:, g, :, n, :], banks[5][:, 0:2 * P].rearrange("p (a q) -> p a q", a=2),
                                      f(ot_hi_q[:, g, :, n, :]), ALU.subtract).then_inc(o_free, 1)

                def inv(u):
                    invert_sum(16 * g + u + 1, u)

                read_scores(0)
                read_scores(1)
                inv(0)
                read_scores(2)
                inv(1)
                read_scores(3)
                inv(2)
                for n in range(NT):
                    u = 4 * n + 4
                    if n < 3:
                        read_scores(u)
                        inv(u - 1)
                        if n == 1:
                            pt_lo(0, 0)
                        read_scores(u + 1)
                        if n:
                            pt_lo(n - 1, 1)
                        if n > 1:
                            o_lo(n - 2)
                        inv(u)
                        read_scores(u + 2)
                        inv(u + 1)
                        if n and A_KB[n - 1][1] > 2:
                            pt_lo(n - 1, 2)
                        read_scores(u + 3)
                        if n == 0:
                            w_split_lo(C_Q // 2 + 1 + g, 1, W_COLS)
                        if n:
                            pt_lo(n, 0)
                        inv(u + 2)
                    else:
                        inv(u - 1)
                        pt_lo(2, 1)
                        if not last:
                            w_split_lo(C_Q // 2 + 2 + g, 0, W_COLS)
                        o_lo(1)
                        pt_lo(2, 2)
                        if not last:
                            a_q_out(g + 1, 0)
                            a_q_lo(g + 1, 0)
                            a_k_lo(g + 1)
                        pt_lo(3, 0)
                        o_lo(2)
                        pt_lo(3, 1)
                if not last:
                    a_q_out(g + 1, 1)
                    a_q_lo(g + 1, 1)
                o_lo(3)
                if not last:
                    a_v_lo(g + 1)

            with dve.Fori(0, GROUPS - 1) as g:
                a_group(g, False)
            a_group(GROUPS - 1, True)

            def add_to_h(c, bank_s, m, used, dst=None):
                wait(dve, w_used, used)
                dst = h[:, m, :] if dst is None else dst
                dve.tensor_tensor(dst, h[:, m, :], banks[6 + bank_s][:], ALU.add).then_inc(proj_free, 1)

            def wo_phase(n, c0):
                with dve.Fori(0, KD // 2) as i:
                    for s in range(2):
                        add_to_h(c0, s, 2 * i + s, c0 + 2 * i + s + 1)
                        w_split_lo(c0 // 2 + 1 + i, s, W_COLS)
                        split_x_lo(n, 2 * i + s)

            def ffn_half(layer, half, n, next_cols, mid=None):
                c2 = ((C_FFN0, C_FFN1)[layer] + half * C_HALF) // 2
                j0 = (2 * layer + half) * HALF

                def hidden(j, cols, first=False, second=False):
                    if not second:
                        w_split_lo(c2 + j + 1, 0, cols)
                    if first:
                        invert_n(norms[2 * layer + 1])
                        w_split_lo(c2 + j + 1, 1, cols)
                        take_rs_t(norms[2 * layer + 1])
                    wait(dve, w_used, 2 * c2 + 2 * j + 1)
                    if not (isinstance(j, int) and j0 + j == 0):
                        wait(dve, silu_ready, j0 + j)
                    dve.tensor_tensor(gate_t[:], banks[0 if first else 6][:], rs_t[:], ALU.mult).then_inc(proj_free, 1)
                    if first:
                        w_split_lo(c2 + j + 2, 0, cols)
                    else:
                        w_split_lo(c2 + j + 1, 1, cols)
                    wait(dve, w_used, 2 * c2 + 2 * j + 2)
                    wait(dve, silu_rs_ready, j0 + j + 1)
                    if not (isinstance(j, int) and j0 + j == 0):
                        wait(dve, f_ready, j0 + j)
                    dve.tensor_tensor(hid[:], banks[1 if first else 7][:], gate_s[:], ALU.mult).then_inc(proj_free, 1)
                    wait(dve, f_hi_ready, j0 + j + 1)
                    dve.tensor_tensor(f_lo[:, j, :], hid[:], f(f_hi[:, j, :]), ALU.subtract).then_inc(f_ready, 1)

                hidden(0, W_COLS, first=half == 0)
                hidden(1, W_COLS, second=half == 0)
                with dve.Fori(2, HALF - 1) as j:
                    hidden(j, W_COLS)
                hidden(HALF - 1, W_DOWN)
                if mid is not None:
                    mid()

                def turned(m, s):
                    wait(dve, pt_done, T_FIN + m + 1)
                    dve.tensor_tensor(out_n_v[:, :, m, :], banks[3 + s][:].rearrange("p (t n) -> p t n", t=NT),
                                      g_fin[:, m, :].unsqueeze(1).to_broadcast([P, NT, P]), ALU.mult) \
                        .then_inc(pt_free, 1)

                final = n is not None and n.gain is None

                def pair(i, cols):
                    for s in range(2):
                        m = 2 * i + s
                        if final and not (isinstance(i, int) and i == 0):
                            wait(dve, pt_done, T_FIN + m - 1)
                            wait(dve, sq_ready, n.base + m - 1)
                        add_to_h(c2, s, m, 2 * c2 + 2 * HALF + m + 1, h_fin[:, s, :] if final else None)
                        if cols:
                            w_split_lo(c2 + HALF + 1 + i, s, cols)
                        if final:
                            if not (isinstance(i, int) and i == 0 and s == 0):
                                turned(m - 1, 1 - s)
                        elif n is not None:
                            split_x_lo(n, m)

                pair(0, W_DOWN)
                with dve.Fori(1, KD // 2 - 1) as i:
                    pair(i, W_DOWN)
                pair(KD // 2 - 1, next_cols)
                if final:
                    turned(KD - 1, 1)

            tab = [0]

            def step(ins):
                tab[0] += 1
                ins.then_inc(tab_v, 1)
                dve.wait_ge(tab_v, tab[0])

            def angles():
                dve.wait_ge(pool_consts, 2 + HEADS + ROPE // 2)
                step(dve.tensor_copy(pos_f[:], pos_r[:]))
                for t in range(NT):
                    step(dve.tensor_scalar(ang[:, t, :], inv_f[:], pos_f[:, t:t + 1], None, ALU.mult))
                step(dve.tensor_scalar(turns[:], ang[:], float(1.0 / (2.0 * np.pi)), None, ALU.mult))
                step(dve.tensor_scalar(turns[:], turns[:], ROUND, None, ALU.add))
                step(dve.tensor_scalar(turns[:], turns[:], ROUND, None, ALU.subtract))
                step(dve.tensor_scalar(turns_hi[:], turns[:], 1.0 / 2048.0, None, ALU.mult))
                step(dve.tensor_scalar(turns_hi[:], turns_hi[:], ROUND, None, ALU.add))
                step(dve.tensor_scalar(turns_hi[:], turns_hi[:], ROUND, 2048.0, ALU.subtract, ALU.mult))
                step(dve.tensor_tensor(turns[:], turns[:], turns_hi[:], ALU.subtract))
                for part in two_pi_parts():
                    step(dve.scalar_tensor_tensor(ang[:], turns_hi[:], -part, ang[:], ALU.mult, ALU.add))
                    step(dve.scalar_tensor_tensor(ang[:], turns[:], -part, ang[:], ALU.mult, ALU.add))
                step(dve.tensor_scalar(ang[:], ang[:], 3.1415925, -3.1415925, ALU.min, ALU.max))
                assert tab[0] == TAB_STEPS

            def cosines():
                dve.wait_ge(tab_a, 1)
                step(dve.tensor_tensor(turns[:], half_sin[:], half_sin[:], ALU.mult))
                step(dve.tensor_scalar(cos_n[:, :, 0:16], turns[:], -2.0, 1.0, ALU.mult, ALU.add))
                step(dve.tensor_scalar(cos_n[:, :, 16:32], turns[:], -2.0, 1.0, ALU.mult, ALU.add))
                dve.wait_ge(tab_a, 2)
                step(dve.tensor_scalar(sin_n[:, :, 0:16], sin_n[:, :, 16:32], -1.0, None, ALU.mult))

            out_n_v = out_n[:].rearrange("p t (m n) -> p t m n", n=P)

            wo_phase(norms[1], C_WOA)
            ffn_half(0, 0, None, W_COLS)
            angles()
            for t in (bv_hi, bv_lo):
                dve.memset(f(t[:, :, :, HD:2 * HD]), 0.0).then_inc(vec_consts, 1)
            ffn_half(0, 1, norms[2], W_LAT, mid=cosines)

            w_split_lo(C_LAT // 2 + 1, 0, W_LAT)
            w_split_lo(C_LAT // 2 + 1, 1, W_LAT)
            w_split_lo(C_B // 2, 0, W_UQ)
            def kv_squares(t):
                dve.wait_ge(lat_kv_ready, t + 1)
                view = lat[:, t, QL:QL + KVL]
                dve.tensor_tensor_reduce((rope_a, rope_b)[t // 2][:, t % 2 * KVL:(t % 2 + 1) * KVL], view, view,
                                         1.0 / KVL, 0.0, ALU.mult, ALU.add, lat_stat[:, 0, NT + t:NT + t + 1]) \
                    .then_inc(kv_sq_ready, 1)

            for t in range(NT):
                if t == 2:
                    invert_n(norms[2])
                if t < NT - 1:
                    dve.wait_ge(lat_done, t + 1)
                else:
                    dve.wait_ge(w_used, C_LAT + 4)
                dve.tensor_copy(lat[:, t, QL:B_IN], banks[2 * t + 1][:, 0:B_IN - QL]).then_inc(lat_kv_ready, 1)
                if t < NT - 1:
                    kv_squares(t)
            kv_squares(NT - 1)

            def rotate(view, cos_v, sin_v, a, b, base):
                dve.tensor_tensor(a, view, cos_v, ALU.mult).then_inc(rope_v, 1)
                dve.tensor_tensor(b[..., 0:16], view[..., 16:32], sin_v[..., 0:16], ALU.mult).then_inc(rope_v, 1)
                dve.tensor_tensor(b[..., 16:32], view[..., 0:16], sin_v[..., 16:32], ALU.mult).then_inc(rope_v, 1)
                wait(dve, rope_v, base + 3)
                dve.tensor_tensor(view, a, b, ALU.add).then_inc(rope_v, 1)

            def lrs(ins):
                lat_steps[0] += 1
                ins.then_inc(lrs_step, 1)
                dve.wait_ge(lrs_step, lat_steps[0])

            lat_steps = [0]

            def b_pt_lo(unit, dst, hi, gain):
                wait(dve, pt_hi_ready, unit - T_A + 1)
                dve.scalar_tensor_tensor(dst, lat_banks[unit - T_BPRE][:], gain, f(hi), ALU.mult, ALU.subtract) \
                    .then_inc(pt_free, 1)

            lrs(dve.tensor_scalar(lat_stat[:, 3, 0:4], ms_n[:, 0, ::2], EPS, None, ALU.mult))
            for b in range(QL // P):
                b_pt_lo(T_BPRE + b, cq_lo[:, b, :], cq_hi[:, b, :], g_q[:, b:b + 1])
            dve.wait_ge(lsq_ready, NT)
            dve.wait_ge(kv_sq_ready, NT)
            lrs(dve.tensor_tensor(lat_stat[:, 0, :].rearrange("p (a t) -> p a t", a=2),
                                  lat_stat[:, 0, :].rearrange("p (a t) -> p a t", a=2),
                                  lat_stat[:, 3, 0:4].unsqueeze(1).to_broadcast([P, 2, NT]), ALU.add))
            dve.wait_ge(lrms_ready, 1)
            lrs(dve.reciprocal(lat_stat[:, 2, :], lat_stat[:, 1, :]))
            lrs(dve.tensor_tensor(lat_stat[:, 3, :], lat_stat[:, 0, :], lat_stat[:, 2, :], ALU.mult))
            lrs(dve.scalar_tensor_tensor(lat_stat[:, 3, :], lat_stat[:, 3, :], -0.5, lat_stat[:, 2, :], ALU.mult, ALU.mult))
            lrs(dve.scalar_tensor_tensor(lat_stat[:, 2, :], lat_stat[:, 3, :], 1.5, lat_stat[:, 2, :], ALU.add, ALU.mult))
            assert lat_steps[0] == LRS_KV
            lrs(dve.tensor_scalar(q_scale[:], lat_stat[:, 2, 0:NT], QK ** -0.5, None, ALU.mult))
            assert lat_steps[0] == LRS_Q
            w_split_lo(C_B // 2, 1, W_UKV, kv=True)
            dve.wait_ge(rs_n_ready, 3)
            krope = lat[:, :, QL + KVL:B_IN]
            lrs(dve.tensor_tensor(krope, krope, rs_n[:, ::2].unsqueeze(2).to_broadcast([P, NT, ROPE]), ALU.mult))
            dve.wait_ge(tab_v, TAB_STEPS + 4)
            rotate(krope, cos_n[:], sin_n[:],
                   rope_a[:, 0:NT * ROPE].rearrange("p (t d) -> p t d", t=NT),
                   rope_b[:, 0:NT * ROPE].rearrange("p (t d) -> p t d", t=NT), 0)
            def b_rotate_q(g, half):
                wait(dve, proj_free, U_B + U_BG * g + 2 * half + 2)
                ts = slice(2 * half, 2 * half + 2)
                view = q_n[:].rearrange("p t (h d) -> p t h d", h=HG)[:, ts, :, NOPE:QK]
                shape = [P, 2, HG, ROPE]
                rotate(view, cos_n[:, ts, :].unsqueeze(2).to_broadcast(shape),
                       sin_n[:, ts, :].unsqueeze(2).to_broadcast(shape),
                       rope_a[:].rearrange("p (t h d) -> p t h d", t=NT, h=HG)[:, ts],
                       rope_b[:].rearrange("p (t h d) -> p t h d", t=NT, h=HG)[:, ts], 8 * g + 4 * half + 4)

            def b_k_lo(g, i):
                for b in range(2):
                    wait(dve, kp_hi_ready, 2 * GROUPS + 4 * g + 2 * i + b + 1)
                    ins = dve.tensor_tensor(bk_lo[0:NOPE, 2 * i + b, :], banks[6 + i][b * HD:(b + 1) * HD, :],
                                            f(bk_hi[0:NOPE, 2 * i + b, :]), ALU.subtract)
                    if b:
                        ins.then_inc(proj_free, 1)

            def b_q_lo(hd, base):
                wait(dve, pt_hi_ready, base - T_A + hd + 1)
                dve.tensor_tensor(bq_lo[0:QK, hd, :], banks[3 + hd % 2][0:QK, :], f(bq_hi[0:QK, hd, :]),
                                  ALU.subtract).then_inc(pt_free, 1)

            bv_hi_v = bv_hi[:].rearrange("p t a (s d) -> p (t a) s d", d=HD)
            bv_lo_v = bv_lo[:].rearrange("p t a (s d) -> p (t a) s d", d=HD)

            def b_v_lo(g, i):
                wait(dve, v_hi_ready, GROUPS + 2 * g + i + 1)
                dve.tensor_tensor(bv_lo_v[:, 4 * i:4 * i + 4, ::2, :],
                                  banks[6 + i][:].rearrange("p (t s d) -> p t s d", t=4, s=2),
                                  f(bv_hi_v[:, 4 * i:4 * i + 4, ::2, :]), ALU.subtract).then_inc(proj_free, 1)

            dve.wait_ge(rope_v, 4)
            b_rotate_q(0, 0)
            for b in range(KVL // P):
                b_pt_lo(T_BPRE + 3 + b, ckv_lo[:, b, :], ckv_hi[:, b, :], g_kv[:, b:b + 1])
            b_rotate_q(0, 1)
            dve.wait_ge(pt_done, T_BPRE + 6)
            dve.wait_ge(rope_v, 4)
            dve.tensor_copy(krope_t[NOPE:QK, :], banks[4][0:ROPE, :]).then_inc(pt_free, 1)

            def krope_lo(hd):
                dve.tensor_tensor(bk_lo[NOPE:QK, hd, :], krope_t[NOPE:QK, :], f(bk_hi[NOPE:QK, hd, :]), ALU.subtract) \
                    .then_inc(krope_ready, 1)

            dve.wait_ge(pt_hi_ready, T_BPRE + 6 - T_A)
            krope_lo(0)
            b_q_lo(0, T_BPRE + 6)
            b_q_lo(1, T_BPRE + 6)
            b_k_lo(0, 0)
            dve.wait_ge(krope_hi, 1)
            krope_lo(1)
            b_q_lo(2, T_BPRE + 6)
            b_k_lo(0, 1)
            b_q_lo(3, T_BPRE + 6)

            def b_group(g, last, cols0, cols1):
                def maximum(u):
                    wait(dve, s_done, 16 * (GROUPS + g) + u + 1)
                    dve.tensor_reduce(stat[:, 0, u % 8:u % 8 + 1], banks[u % 3][:], AX_X, ALU.max, negate=True) \
                        .then_inc(max_ready, 1)

                def pt_lo(n, i):
                    wait(dve, pt_hi_ready, T_B - T_A + B_TG * g + 4 * n + i + 1)
                    dve.tensor_tensor(bpt_lo[:, n % 2, i, :], banks[3 + i % 2][:], f(bpt_hi[:, n % 2, i, :]),
                                      ALU.subtract).then_inc(pt_free, 1)

                def o_lo(pair):
                    wait(dve, o_hi_ready, 4 * GROUPS + 2 * g + pair + 1)
                    dve.tensor_tensor(ot_lo[:, 2 * g + pair, :], banks[5][:], f(ot_hi[:, 2 * g + pair, :]),
                                      ALU.subtract).then_inc(o_free, 1)

                def inv(u):
                    invert_sum(16 * (GROUPS + g) + u + 1, u)

                maximum(0)
                maximum(1)
                inv(0)
                maximum(2)
                inv(1)
                maximum(3)
                inv(2)
                for n in range(HG):
                    u = 4 * n + 4
                    if n < 3:
                        maximum(u)
                        inv(u - 1)
                        if n:
                            pt_lo(n - 1, 3)
                        maximum(u + 1)
                        inv(u)
                        if n:
                            w_half_lo(C_B // 2 + 1 + g, n - 1, (cols0, cols1)[n - 1], 1, kv=n == 2 and not last)
                        maximum(u + 2)
                        inv(u + 1)
                        maximum(u + 3)
                        if n == 0:
                            b_v_lo(g, 0)
                        pt_lo(n, 0)
                        inv(u + 2)
                        pt_lo(n, 1)
                        if n == 2:
                            inv(u + 3)
                        if n == 0:
                            b_v_lo(g, 1)
                        if n < 2:
                            w_half_lo(C_B // 2 + 1 + g, n, (cols0, cols1)[n], 0, kv=n == 1 and not last)
                        pt_lo(n, 2)
                        if n == 2:
                            pt_lo(2, 3)
                            o_lo(0)
                            if not last:
                                b_rotate_q(g + 1, 0)
                    else:
                        for i in range(4):
                            pt_lo(n, i)
                            if i == 0 and not last:
                                b_k_lo(g + 1, 0)
                            if i == 1 and not last:
                                b_rotate_q(g + 1, 1)
                        if not last:
                            for hd in range(HG):
                                b_q_lo(hd, T_B + B_TG * g + 16)
                                if hd == 0:
                                    b_k_lo(g + 1, 1)
                        o_lo(1)

            with dve.Fori(0, GROUPS - 1) as g:
                b_group(g, False, W_UQ, W_UKV)
            b_group(GROUPS - 1, True, W_COLS, W_COLS)

            wo_phase(norms[3], C_WOB)
            ffn_half(1, 0, None, W_COLS)
            ffn_half(1, 1, norms[4], 0)
            invert_n(norms[4])
            dve.wait_ge(rs_n_ready, 5)
            dve.wait_ge(pt_free, T_FIN + KD)
            for t in (0, 2):
                dve.tensor_scalar(out_n[:, t, :], out_n[:, t, :], rs_n[:, 2 * t:2 * t + 1], None, ALU.mult) \
                    .then_inc(out_ready[0], 1)


_INS = ["x", "positions", "norm_mix", "norm_ffn", "a_w_qkv", "a_sink", "a_w_o", "b_w_in", "b_g_q", "b_g_kv",
        "b_w_uq", "b_w_ukv", "b_w_o", "ffn_w_gu", "ffn_w_down", "final_norm"]


def kernel(**inputs):
    import concourse.bacc as bacc
    from concourse.bass_utils import run_bass_kernel_spmd as run

    nc = bacc.Bacc("TRN2", target_bir_lowering=False, num_devices=1)
    arrays, args = {}, []
    for name in _INS:
        a = np.ascontiguousarray(inputs[name])
        arrays[f"in_{name}"] = a
        args.append(nc.dram_tensor(f"in_{name}", a.shape, mybir.dt.from_np(a.dtype), kind="ExternalInput").ap())
    args.append(nc.dram_tensor("out_0", (1, T, D), F32, kind="ExternalOutput").ap())
    build(nc, *args)
    r = run(nc, [arrays], core_ids=[0])
    return r.results[0]["out_0"]
```
